# Optimizing a Trainium2 kernel written in Bass

```python
import math
import jax, jax.numpy as jnp
from jax import lax
import numpy as np

D_MODEL = 1024
BATCH = 1
SEQ = 512
DEPTH = 2

MLA_HEADS = 8
MLA_Q_LORA = 256
MLA_KV_LORA = 128
MLA_NOPE = 64
MLA_ROPE = 32
MLA_V = 64
MLA_QK = MLA_NOPE + MLA_ROPE
ROPE_THETA = 10000.0
Q_BLOCK = 128
DIL_HEADS = 8
DIL_HEAD_DIM = 64
DIL_PATTERNS = ((128, 1), (512, 4), (2048, 16))
REL_BUCKETS = 32
REL_MAX_DIST = 1024
FFN_HIDDEN = -(-8 * D_MODEL // (3 * 256)) * 256
EPS = 1e-6
NEG_INF = -1e30
IN_SIZES = (MLA_Q_LORA, MLA_KV_LORA, MLA_ROPE, 3 * DIL_HEADS * DIL_HEAD_DIM, D_MODEL, D_MODEL)
IN_COLS = sum(IN_SIZES)
IN_SPLIT = tuple(int(s) for s in np.cumsum(IN_SIZES)[:-1])

kernel_name = 'hybrid_mla_dilated_encoder'

def rmsnorm(x, g):
    x32 = x.astype(jnp.float32)
    r = lax.rsqrt(jnp.mean(x32 * x32, axis=-1, keepdims=True) + EPS)
    return (x32 * r).astype(x.dtype) * g

def modulate(h, shift, scale):
    return h * (1.0 + scale[:, None, :]) + shift[:, None, :]

def rope_tables(positions, dtype):
    half = MLA_ROPE // 2
    inv = ROPE_THETA ** (-jnp.arange(half, dtype=jnp.float32) / half)
    ang = positions.astype(jnp.float32)[..., None] * inv
    return jnp.cos(ang)[:, :, None, :].astype(dtype), jnp.sin(ang)[:, :, None, :].astype(dtype)

def apply_rope(x, cos, sin):
    half = x.shape[-1] // 2
    x1, x2 = x[..., :half], x[..., half:]
    return jnp.concatenate([x1 * cos - x2 * sin, x2 * cos + x1 * sin], axis=-1)

def t5_bucket(rel):
    nb = REL_BUCKETS // 2
    max_exact = nb // 2
    ret = jnp.where(rel > 0, nb, 0)
    n = jnp.abs(rel)
    nf = jnp.maximum(n, 1).astype(jnp.float32)
    large = max_exact + (jnp.log(nf / max_exact) / math.log(REL_MAX_DIST / max_exact) * (nb - max_exact)).astype(jnp.int32)
    large = jnp.minimum(large, nb - 1)
    return ret + jnp.where(n < max_exact, n, large)

def mla_attention(q_c, kv_c, k_rope, cos, sin, q_a_norm, w_q_b, kv_a_norm, w_kv_b, q_norm, k_norm):
    B, S, _ = q_c.shape
    q = (rmsnorm(q_c, q_a_norm) @ w_q_b).reshape(B, S, MLA_HEADS, MLA_QK)
    kv = (rmsnorm(kv_c, kv_a_norm) @ w_kv_b).reshape(B, S, MLA_HEADS, MLA_NOPE + MLA_V)
    k_nope, v = kv[..., :MLA_NOPE], kv[..., MLA_NOPE:]
    k = jnp.concatenate([k_nope, jnp.broadcast_to(k_rope[:, :, None, :], (B, S, MLA_HEADS, MLA_ROPE))], axis=-1)
    q = rmsnorm(q, q_norm)
    k = rmsnorm(k, k_norm)
    q = jnp.concatenate([q[..., :MLA_NOPE], apply_rope(q[..., MLA_NOPE:], cos, sin)], axis=-1)
    k = jnp.concatenate([k[..., :MLA_NOPE], apply_rope(k[..., MLA_NOPE:], cos, sin)], axis=-1)
    scale = MLA_QK ** -0.5
    n_blk = S // Q_BLOCK
    qb = q.reshape(B, n_blk, Q_BLOCK, MLA_HEADS, MLA_QK).transpose(1, 0, 2, 3, 4)

    def attend(qi):
        s = jnp.einsum('bqhd,bkhd->bhqk', qi, k).astype(jnp.float32) * scale
        p = jax.nn.softmax(s, axis=-1).astype(v.dtype)
        return jnp.einsum('bhqk,bkhd->bqhd', p, v)

    o = lax.map(attend, qb)
    return o.transpose(1, 0, 2, 3, 4).reshape(B, S, MLA_HEADS * MLA_V)

def strided_band_attention(q, k, v, dil, half, rel_bias):
    B, S, H, dh = q.shape
    L = S // dil
    W = half
    n = -(-L // W)
    Lp = n * W

    def to_sub(t):
        return t.reshape(B, L, dil, H, dh).transpose(0, 2, 3, 1, 4)

    qb = jnp.pad(to_sub(q), ((0, 0), (0, 0), (0, 0), (0, Lp - L), (0, 0))).reshape(B, dil, H, n, W, dh)
    kv_pad = ((0, 0), (0, 0), (0, 0), (W, Lp - L + W), (0, 0))

    def bands(t):
        tb = jnp.pad(to_sub(t), kv_pad).reshape(B, dil, H, n + 2, W, dh)
        return jnp.concatenate([tb[:, :, :, :-2], tb[:, :, :, 1:-1], tb[:, :, :, 2:]], axis=-2)

    kb, vb = bands(k), bands(v)
    s = jnp.einsum('brhnqd,brhnkd->brhnqk', qb, kb).astype(jnp.float32) * (dh ** -0.5)
    qi = jnp.arange(W)[:, None]
    ki = jnp.arange(3 * W)[None, :]
    rel = ki - W - qi
    key_idx = jnp.arange(n)[:, None, None] * W + ki[None] - W
    valid = (jnp.abs(rel) <= W)[None] & (key_idx >= 0) & (key_idx < L)
    bias = rel_bias[t5_bucket(rel * dil)].astype(jnp.float32).transpose(2, 0, 1)
    s = jnp.where(valid, s + bias[:, None], NEG_INF)
    m = jnp.max(s, axis=-1, keepdims=True)
    p = jnp.exp(s - m)
    den = jnp.sum(p, axis=-1)
    o = jnp.einsum('brhnqk,brhnkd->brhnqd', p, vb.astype(jnp.float32)) / den[..., None]
    lse = m[..., 0] + jnp.log(den)
    o = o.reshape(B, dil, H, Lp, dh)[:, :, :, :L].transpose(0, 3, 1, 2, 4).reshape(B, S, H, dh)
    lse = lse.reshape(B, dil, H, Lp)[..., :L].transpose(0, 3, 1, 2).reshape(B, S, H)
    return o, lse

def dilated_attention(qkv, rel_bias, q_norm, k_norm):
    B, S, _ = qkv.shape
    qkv = qkv.reshape(B, S, 3, DIL_HEADS, DIL_HEAD_DIM)
    q = rmsnorm(qkv[:, :, 0], q_norm)
    k = rmsnorm(qkv[:, :, 1], k_norm)
    v = qkv[:, :, 2]
    outs, lses = [], []
    for window, dil in DIL_PATTERNS:
        o, lse = strided_band_attention(q, k, v, dil, window // (2 * dil), rel_bias)
        outs.append(o)
        lses.append(lse)
    w = jax.nn.softmax(jnp.stack(lses, axis=0), axis=0)
    y = jnp.einsum('pbsh,pbshd->bshd', w, jnp.stack(outs, axis=0))
    return y.reshape(B, S, DIL_HEADS * DIL_HEAD_DIM).astype(qkv.dtype)

def swiglu(h, w_gate, w_up, w_down):
    return (jax.nn.silu(h @ w_gate) * (h @ w_up)) @ w_down

def setup_inputs(seed: int = 0) -> dict:
    key = jax.random.key(seed)
    ks = jax.random.split(key, 24)
    f32 = jnp.float32

    def w(k, shape, fan_in):
        return jax.random.normal(k, shape, f32) * (fan_in ** -0.5)

    def gain(k, shape):
        return 1.0 + 0.02 * jax.random.normal(k, shape, f32)

    return {
        'x': jax.random.normal(ks[0], (BATCH, SEQ, D_MODEL), f32),
        'c': jax.random.normal(ks[1], (BATCH, D_MODEL), f32),
        'positions': jax.random.randint(ks[2], (BATCH, 1), 0, 1024, dtype=jnp.int32) + jnp.arange(SEQ, dtype=jnp.int32)[None, :],
        'rel_bias': 0.5 * jax.random.normal(ks[3], (REL_BUCKETS, DIL_HEADS), f32),
        'norm1_g': gain(ks[4], (DEPTH, D_MODEL)),
        'norm2_g': gain(ks[5], (DEPTH, D_MODEL)),
        'ada_w': 0.5 * w(ks[6], (DEPTH, D_MODEL, 6 * D_MODEL), D_MODEL),
        'ada_b': 0.02 * jax.random.normal(ks[7], (DEPTH, 6 * D_MODEL), f32),
        'w_in': w(ks[8], (DEPTH, D_MODEL, IN_COLS), D_MODEL),
        'q_a_norm': gain(ks[9], (DEPTH, MLA_Q_LORA)),
        'w_q_b': w(ks[10], (DEPTH, MLA_Q_LORA, MLA_HEADS * MLA_QK), MLA_Q_LORA),
        'kv_a_norm': gain(ks[11], (DEPTH, MLA_KV_LORA)),
        'w_kv_b': w(ks[12], (DEPTH, MLA_KV_LORA, MLA_HEADS * (MLA_NOPE + MLA_V)), MLA_KV_LORA),
        'q_norm_a': gain(ks[13], (DEPTH, MLA_QK)),
        'k_norm_a': gain(ks[14], (DEPTH, MLA_QK)),
        'q_norm_b': gain(ks[15], (DEPTH, DIL_HEAD_DIM)),
        'k_norm_b': gain(ks[16], (DEPTH, DIL_HEAD_DIM)),
        'w_branch_a': w(ks[17], (DEPTH, MLA_HEADS * MLA_V, D_MODEL), MLA_HEADS * MLA_V),
        'w_branch_b': w(ks[18], (DEPTH, DIL_HEADS * DIL_HEAD_DIM, D_MODEL), DIL_HEADS * DIL_HEAD_DIM),
        'w_out': w(ks[19], (DEPTH, D_MODEL, D_MODEL), D_MODEL),
        'w_ffn_gate': w(ks[20], (DEPTH, D_MODEL, FFN_HIDDEN), D_MODEL),
        'w_ffn_up': w(ks[21], (DEPTH, D_MODEL, FFN_HIDDEN), D_MODEL),
        'w_ffn_down': w(ks[22], (DEPTH, FFN_HIDDEN, D_MODEL), FFN_HIDDEN),
    }

def reference(x, c, positions, rel_bias, norm1_g, norm2_g, ada_w, ada_b, w_in, q_a_norm, w_q_b,
              kv_a_norm, w_kv_b, q_norm_a, k_norm_a, q_norm_b, k_norm_b, w_branch_a, w_branch_b,
              w_out, w_ffn_gate, w_ffn_up, w_ffn_down):
    cos, sin = rope_tables(positions, x.dtype)
    c_act = jax.nn.silu(c)
    for l in range(DEPTH):
        mod = c_act @ ada_w[l] + ada_b[l]
        sh1, sc1, g1, sh2, sc2, g2 = jnp.split(mod, 6, axis=-1)
        h = modulate(rmsnorm(x, norm1_g[l]), sh1, sc1)
        proj = h @ w_in[l]
        q_c, kv_c, k_r, qkv_b, gate_a, gate_b = jnp.split(proj, IN_SPLIT, axis=-1)
        y_a = mla_attention(q_c, kv_c, k_r, cos, sin, q_a_norm[l], w_q_b[l], kv_a_norm[l], w_kv_b[l],
                            q_norm_a[l], k_norm_a[l])
        y_b = dilated_attention(qkv_b, rel_bias, q_norm_b[l], k_norm_b[l])
        merged = jax.nn.sigmoid(gate_a) * (y_a @ w_branch_a[l]) + jax.nn.sigmoid(gate_b) * (y_b @ w_branch_b[l])
        x = x + g1[:, None, :] * (merged @ w_out[l])
        h = modulate(rmsnorm(x, norm2_g[l]), sh2, sc2)
        x = x + g2[:, None, :] * swiglu(h, w_ffn_gate[l], w_ffn_up[l], w_ffn_down[l])
    return x


_drawn_inputs = setup_inputs


def setup_inputs(seed=0):
    import zlib

    import numpy as np

    out = dict(_drawn_inputs(seed))
    spreads = {}
    factors = {'rel_bias': 4.911,
     'norm1_g': 8.0,
     'norm2_g': 6.302,
     'q_a_norm': 8.0,
     'w_q_b': 2.714,
     'kv_a_norm': 8.0,
     'q_norm_a': 8.0,
     'k_norm_a': 8.0,
     'q_norm_b': 8.0,
     'k_norm_b': 8.0}
    for name, (base, spread) in spreads.items():
        noise = np.random.default_rng([zlib.crc32(name.encode()), seed]).standard_normal(out[name].shape)
        drawn = base * np.exp(spread * noise) if base else spread * noise
        out[name] = __import__('jax').numpy.asarray(drawn.astype(out[name].dtype))
    for name, factor in factors.items():
        out[name] = (out[name] * factor).astype(out[name].dtype)
    return out
```

```python
import math
from contextlib import ExitStack

import numpy as np

import concourse.bass as bass
from concourse import mybir

F32 = mybir.dt.float32
F32R = mybir.dt.float32r
I32 = mybir.dt.int32
ALU = mybir.AluOpType
ACT = mybir.ActivationFunctionType
AX = mybir.AxisListType

P = 128
D = 1024
S = 512
DEPTH = 2
KD = D // P
NT = S // P
HEADS = 8
Q_LORA, KV_LORA, ROPE, NOPE, VDIM = 256, 128, 32, 64, 64
QK = NOPE + ROPE
HALF = ROPE // 2
DH = 64
FFN = 2816
KF = FFN // P
EPS = 1e-6
NEG_INF = -1e30
PATTERNS = ((128, 1), (512, 4), (2048, 16))
REL_BUCKETS, REL_MAX_DIST = 32, 1024
ROPE_THETA = 10000.0
IN_COLS = Q_LORA + KV_LORA + ROPE + 3 * HEADS * DH + 2 * D
COL_KV = Q_LORA
COL_DIL = COL_KV + KV_LORA + ROPE
COL_DV = COL_DIL + 2 * HEADS * DH
COL_GA = COL_DIL + 3 * HEADS * DH
COL_GB = COL_GA + D
PANEL = 2048
PC = PANEL // KD
TW = 2 * S - P

R_ADAB, R_N1, R_N2, R_QA, R_KVA, R_QNA, R_KNA, R_QNB, R_KNB, R_C = 0, 48, 56, 64, 66, 67, 68, 69, 70, 71
ROWS = R_C + KD
M_SH1, M_SC1, M_G1, M_SH2, M_SC2, M_G2 = (KD * i for i in range(6))

PN_QC, PN_KV, PN_DV, PN_WQB, PN_WKVB, PN_DQK = 0, 1, 2, 4, 5, 6
PN_GA = PN_DQK + 4
PN_GB = PN_GA + 4
PN_OUT = PN_GB + 8
PN_FFN = PN_OUT + 4
PN_DOWN = PN_FFN + KF
PANELS = PN_DOWN + 12
ADA_UNITS = 12
LOADS = PANELS + 2 * ADA_UNITS
RAW_LATE = 2 * ADA_UNITS
STEPS = 2 * HEADS


def ada_unit(g):
    if g < HEADS:
        return g
    return HEADS + (g - HEADS) // 2 if g % 2 == 0 else None


def raw_of_step(g):
    panels = PN_DQK + 1 + (g + 1) // 2
    units = g if g < HEADS else HEADS + (g - HEADS + 1) // 2
    return panels + 2 * units


def load_order():
    order = [("panel", p) for p in range(PN_DQK + 1)]
    for g in range(STEPS):
        if g % 2 == 0:
            order.append(("panel", PN_DQK + 1 + g // 2))
        if ada_unit(g) is not None:
            order += [("ada", 2 * ada_unit(g)), ("ada", 2 * ada_unit(g) + 1)]
    return order + [("panel", -2), ("panel", -1)]


LOAD_ORDER = load_order()


class Event:

    def __init__(self, sem, per_layer, credit=0):
        self.sem, self.per_layer, self.credit = sem, per_layer, credit

    def at(self, layer, n):
        return layer * self.per_layer + (n + self.credit)


def encoder_trunk(nc, x, c, positions, rel_bias, norm1_g, norm2_g, ada_w, ada_b, w_in, q_a_norm, w_q_b,
                  kv_a_norm, w_kv_b, q_norm_a, k_norm_a, q_norm_b, k_norm_b, w_branch_a, w_branch_b,
                  w_out, w_ffn_gate, w_ffn_up, w_ffn_down, consts, buckets, out):
    bias_scratch = nc.dram_tensor("bias_scratch", (HEADS, P, 2 * S), F32).ap()

    with ExitStack() as ctx:
        def sb(name, shape, dt=F32, within=ctx):
            return within.enter_context(nc.sbuf_tensor(name, shape, dt))

        def sem(name):
            return ctx.enter_context(nc.semaphore(name))

        def event(name, per_layer, credit=0):
            return Event(sem(name), per_layer, credit)

        xT = sb("xT", [P, KD, S])
        h_hi = sb("h_hi", [P, KD, S], F32R)
        h_lo = sb("h_lo", [P, KD, S], F32R)
        raw = [sb(f"raw{i}", [P, PANEL]) for i in range(2)]
        w_hi = [sb(f"w_hi{i}", [P, PANEL], F32R) for i in range(2)]
        w_lo = [sb(f"w_lo{i}", [P, PANEL], F32R) for i in range(2)]
        sumsq = sb("sumsq", [P, S])
        rstd = sb("rstd", [P, S])
        trig = sb("trig", [P, S])
        cst = sb("cst", [P, 3 * P + 4])
        ones = sb("ones", [P, P])
        prm = sb("prm", [P, DEPTH, ROWS])
        prl = sb("prl", [P, ROWS])
        mods = sb("mods", [P, 6 * KD])
        g_norm = sb("g_norm", [P, KD])
        silu_c = sb("silu_c", [P, KD])
        eps_col = sb("eps_col", [P, 1])
        spare = sb("spare", [P, 4])
        nmax = sb("nmax", [P, NT])
        den = sb("den", [P, NT])
        rden = sb("rden", [P, NT])
        ident = cst[:, 0:P]
        block_ones = cst[:, P:2 * P]
        pair_sum = cst[64:128, 2 * P:3 * P]
        rope_inv, rope_phase, rope_arg, rope_sign = (cst[:, 3 * P + i:3 * P + i + 1] for i in range(4))

        def layout(*buffers):
            made = []
            with ExitStack() as scope:
                for name, shape, dt in buffers:
                    made.append(sb(name, shape, dt, scope))
            return made

        KB = 256
        (qk, dqk, v_mla, v_dil, ya_hi, ya_lo, prob, probT, toep, ada_acc) = layout(
            ("qk", [P, HEADS, 2, S], F32),
            ("dqk", [P, KD, S], F32),
            ("v_mla", [P, NT, HEADS * VDIM], F32), ("v_dil", [P, NT, HEADS * DH], F32),
            ("ya_hi", [P, 4, S], F32R), ("ya_lo", [P, 4, S], F32R),
            ("prob", [P, 2, S], F32), ("probT", [P, NT, S], F32),
            ("toep", [P, 2, TW], F32), ("ada_acc", [P, S], F32))
        (yb_hi, yb_lo, gate_a, m_hi, m_lo, _, sig_a, sig_b, mix) = layout(
            ("yb_hi", [P, 4, S], F32R), ("yb_lo", [P, 4, S], F32R), ("gate_a", [P, KD, S], F32),
            ("m_hi", [P, KD, S], F32R), ("m_lo", [P, KD, S], F32R), ("over_ya", [P, 16 * KB], F32),
            ("sig_a", [P, 2, S], F32), ("sig_b", [P, 2, S], F32), ("mix", [P, 2, S], F32))
        (_, sq_qk, r_qk, _, qc_hi, qc_lo, kvc_hi, kvc_lo, k_rot, q_gain) = layout(
            ("over_qk", [P, 32 * KB], F32), ("sq_qk", [P, 2, 2, S], F32), ("r_qk", [P, 2, 2, S], F32),
            ("over_v", [P, 16 * KB], F32),
            ("qc_hi", [P, 2, S], F32R), ("qc_lo", [P, 2, S], F32R),
            ("kvc_hi", [P, S], F32R), ("kvc_lo", [P, S], F32R), ("k_rot", [P, S], F32), ("q_gain", [P, S], F32))
        (a_hi, a_lo, tn, sq) = layout(
            ("a_hi", [P, KF, S], F32R), ("a_lo", [P, KF, S], F32R), ("tn", [P, 2, S], F32), ("sq", [P, 2, S], F32))
        (ada0, xnat, rows, pos_i, angle, turns, bucket_sb, rel_sb, _, btab) = layout(
            ("ada0", [P, 4, KD, S], F32), ("xnat", [P, NT, D], F32), ("rows", [ROWS, DEPTH, P], F32),
            ("pos_i", [P, S], I32), ("angle", [P, S], F32), ("turns", [P, S], F32),
            ("bucket_sb", [REL_BUCKETS + 1, 2 * S], F32), ("rel_sb", [REL_BUCKETS + 1, HEADS], F32),
            ("gap", [P, 5 * KB - 8], F32), ("btab", [P, 2, S], F32))
        (xout,) = layout(("xout", [P, NT, D], F32))
        sb("region", [P, 101 * KB])

        bank = [ctx.enter_context(nc.psum_tensor(f"bank{i}", [P, S], F32)) for i in range(4)]
        tr = ctx.enter_context(nc.psum_tensor("tr", [P, 2, S], F32))
        pv = ctx.enter_context(nc.psum_tensor("pv", [P, S], F32))
        ss = ctx.enter_context(nc.psum_tensor("ss", [P, S], F32))
        b0, b1, s0, s1 = bank

        consts_in, buckets_in, rows_in, pos_in, x_in, ones_set, rel_ones = (
            sem(n) for n in ("consts_in", "buckets_in", "rows_in", "pos_in", "x_in", "ones_set", "rel_ones"))
        bias_out = [sem(f"bias_out{i}") for i in range(2)]
        ada0_in = [sem(f"ada0_in{u}") for u in range(4)]
        prm_done, prm_set, sig_c_set, c_set, ada0_step, ada0_reduced, mods0_set = (
            sem(n) for n in ("prm_done", "prm_set", "sig_c_set", "c_set", "ada0_step", "ada0_reduced", "mods0_set"))
        x_transposed, x_set, bias_done, btab_set, angle_step, sin_set, trig_set = (
            sem(n) for n in ("x_transposed", "x_set", "bias_done", "btab_set", "angle_step", "sin_set", "trig_set"))
        AB_EXTRA = 4
        raw_in = [event("raw_in0", 16 * (LOADS // 2)), event("raw_in1", 16 * (LOADS // 2 + AB_EXTRA))]
        hi_set = event("hi_set", PANELS)
        lo_set = event("lo_set", PANELS, credit=2)
        x_updated = event("x_updated", 2 * KD)
        sq_set = event("sq_set", 2 * KD, credit=KD)
        ADDS = KD - 1
        sum_done = event("sum_done", 2 * ADDS, credit=ADDS)
        norm_ss = event("norm_ss", 2)
        norm_ln = event("norm_ln", 2)
        rstd_set = event("rstd_set", 2)
        norm_t = event("norm_t", 2 * KD)
        h_hi_set = event("h_hi_set", 2 * KD)
        h_lo_set = event("h_lo_set", 2 * KD)
        prl_set = event("prl_set", 1)
        qnb_scaled = event("qnb_scaled", 1)
        g_norm_set = event("g_norm_set", 2)
        lat_done = event("lat_done", 2)
        vd_done = event("vd_done", 2 * NT)
        vm_done = event("vm_done", NT)
        v_set = event("v_set", 3 * NT)
        lat_sq = event("lat_sq", 5)
        lat_ss = event("lat_ss", 2)
        lat_ln = event("lat_ln", 2)
        lat_r = event("lat_r", 2)
        lat_t = event("lat_t", 3)
        lat_hi = event("lat_hi", 3)
        lat_lo = event("lat_lo", 3)
        rot_parts = event("rot_parts", 1)
        rot_sum = event("rot_sum", 1)
        rot_set = event("rot_set", 1)
        q_gain_set = event("q_gain_set", 1)
        q_done = event("q_done", HEADS)
        k_done = event("k_done", HEADS)
        head_sq = event("head_sq", 2 * HEADS)
        head_ss = event("head_ss", HEADS)
        head_ln = event("head_ln", HEADS)
        head_r = event("head_r", HEADS)
        q_scaled = event("q_scaled", HEADS)
        q_set = event("q_set", HEADS)
        k_set = event("k_set", HEADS)
        kr_set = event("kr_set", HEADS)
        scored = event("scored", NT * STEPS)
        biased = event("biased", NT * HEADS)
        max_set = event("max_set", NT * STEPS)
        exp_set = event("exp_set", NT * STEPS)
        rden_set = event("rden_set", NT * STEPS)
        prob_set = event("prob_set", NT * STEPS)
        transposed = event("transposed", NT * STEPS)
        probT_set = event("probT_set", NT * STEPS)
        pv_done = event("pv_done", STEPS)
        y_hi_set = event("y_hi_set", STEPS // 2)
        y_lo_set = event("y_lo_set", STEPS // 2)
        proj_done = event("proj_done", STEPS)
        dsq_set = event("dsq_set", HEADS)
        dss_done = event("dss_done", HEADS)
        dln_set = event("dln_set", HEADS)
        dr_set = event("dr_set", HEADS)
        dqk_set = event("dqk_set", HEADS)
        ga_set = event("ga_set", HEADS)
        toep_in = [event(f"toep_in{i}", 16 * HEADS // 2) for i in range(2)]
        ada_step = event("ada_step", KD * ADA_UNITS)
        ada_reduced = event("ada_reduced", ADA_UNITS)
        mods_set = event("mods_set", ADA_UNITS)
        gb_done = event("gb_done", KD)
        br_done = event("br_done", 2 * KD)
        siga_set = event("siga_set", KD)
        sigb_set = event("sigb_set", KD)
        mix_a = event("mix_a", KD)
        mix_b = event("mix_b", KD)
        mix_set = event("mix_set", KD)
        m_hi_set = event("m_hi_set", KD)
        m_lo_set = event("m_lo_set", KD)
        out_done = event("out_done", KD)
        gate_done = event("gate_done", KF)
        up_done = event("up_done", KF)
        fsig_set = event("fsig_set", KF)
        silu_set = event("silu_set", KF)
        act_set = event("act_set", KF)
        a_hi_set = event("a_hi_set", KF)
        a_lo_set = event("a_lo_set", KF)
        down_part = event("down_part", KD, credit=1)
        down_done = event("down_done", KD, credit=1)
        y_transposed, xout_left, xout_right, stored = (
            sem(n) for n in ("y_transposed", "xout_left", "xout_right", "stored"))

        block = ctx.enter_context(nc.Block())
        v = nc.vector
        a = nc.scalar
        pe_ = nc.tensor

        def wait(eng, ev, layer, n):
            eng.wait_ge(ev.sem, ev.at(layer, n))

        def panel(w, k=KD):
            return w[:, 0:PANEL].rearrange("p (k n) -> p k n", k=k)

        @block.sync
        def _(sp):
            sp.dma_start(cst[:, :], consts).then_inc(consts_in, 16)
            row_loads = [
                (R_ADAB, 6 * KD, ada_b.rearrange("l (r p) -> r l p", p=P)),
                (R_N1, KD, norm1_g.rearrange("l (r p) -> r l p", p=P)),
                (R_N2, KD, norm2_g.rearrange("l (r p) -> r l p", p=P)),
                (R_QA, 2, q_a_norm.rearrange("l (r p) -> r l p", p=P)),
                (R_KVA, 1, kv_a_norm.rearrange("l (r p) -> r l p", p=P))]
            for r, n, src in row_loads:
                sp.dma_start(rows[r:r + n, :, :], src).then_inc(rows_in, 16)
            for l in range(DEPTH):
                sp.dma_start(rows[R_C:R_C + KD, l, :], c.rearrange("o (r p) -> (o r) p", p=P)).then_inc(rows_in, 16)
            for r, src in ((R_QNA, q_norm_a), (R_KNA, k_norm_a)):
                for at, frm, n in ((0, 0, QK), (QK, NOPE + HALF, HALF), (QK + HALF, NOPE, HALF)):
                    sp.dma_start(rows[r:r + 1, :, at:at + n], src[:, frm:frm + n].rearrange("(o l) n -> o l n", o=1))\
                        .then_inc(rows_in, 16)
            for r, src in ((R_QNB, q_norm_b), (R_KNB, k_norm_b)):
                for at in (0, DH):
                    sp.dma_start(rows[r:r + 1, :, at:at + DH], src.rearrange("(o l) n -> o l n", o=1))\
                        .then_inc(rows_in, 16)
            for u in range(4):
                sp.dma_start(ada0[:, u, :, :], ada_w[0, :, u * S:(u + 1) * S].rearrange("(k p) n -> p k n", p=P))\
                    .then_inc(ada0_in[u], 16)

            def load(l, r, slot, parts):
                kind, n = LOAD_ORDER[r - 2] if isinstance(r, int) and r - 2 < len(LOAD_ORDER) - 2 else ("panel", r - 2 - RAW_LATE)
                if kind == "panel":
                    wait(sp, lo_set, l, n + 1)
                else:
                    wait(sp, ada_step, l, 4 * (n + 1))
                for dst, src in parts:
                    sp.dma_start(dst, src).then_inc(raw_in[slot].sem, 16)

            def columns(w, l, col, n=PC):
                return w[bass.ds(l, 1), :, bass.ds(col, n)].rearrange("o (k p) n -> p (o k) n", p=P)

            def load_columns(l, r, slot, w, col, n=PC, k=KD):
                load(l, r, slot, [(raw[slot][:, 0:k * n].rearrange("p (k n) -> p k n", k=k), columns(w, l, col, n))])

            def load_ada(l, r, g):
                u = ada_unit(g)
                if u is None:
                    return
                for half in range(2):
                    layer = l if u < HEADS else DEPTH - 1
                    col = M_G1 * P + u * S if u < HEADS else (u - HEADS) * S
                    src = ada_w[bass.ds(layer, 1), half * 4 * P:(half + 1) * 4 * P, col:col + S]
                    slot = (r + half) % 2
                    load(l, r + half, slot, [(raw[slot][:, :].rearrange("p (k n) -> p k n", k=4),
                                              src.rearrange("o (k p) n -> p (o k) n", p=P))])

            def load_step(l, g):
                r = raw_of_step(g)
                if g % 2 == 0:
                    p = PN_DQK + 1 + g // 2
                    col = (COL_DIL + (p - PN_DQK) * PC if p < PN_GA else
                           COL_GA + (p - PN_GA) * PC if p < PN_GB else COL_GB)
                    load_columns(l, r, r % 2, w_in, col)
                    r += 1
                load_ada(l, r, g)

            def load_branches(l, i):
                col = i * PC
                half = PANEL // 2
                load(l, PN_GB + 1 + RAW_LATE + 2 * i, 1, [
                    (raw[1][:, z * half:(z + 1) * half].rearrange("p (k n) -> p k n", k=4), columns(w, l, col))
                    for z, w in enumerate((w_branch_a, w_branch_b))])

            def load_down(l, gr):
                for q in range(3):
                    k0, k1 = 8 * q, min(8 * q + 8, KF)
                    r = PN_DOWN + RAW_LATE + 3 * gr + q
                    slot = (gr + q) % 2
                    src = w_ffn_down[bass.ds(l, 1), k0 * P:k1 * P, gr * PC:(gr + 1) * PC]
                    load(l, r, slot, [(raw[slot][:, 0:(k1 - k0) * PC].rearrange("p (k n) -> p k n", k=k1 - k0),
                                       src.rearrange("o (k p) n -> p (o k) n", p=P))])

            with sp.Fori(0, DEPTH) as l:
                load_columns(l, 0, 0, w_in, 0)
                load_columns(l, 1, 1, w_in, COL_KV, KV_LORA + ROPE)
                load_columns(l, 2, 0, w_in, COL_DV)
                load_columns(l, 3, 1, w_in, COL_DV + PC)
                load_columns(l, 4, 0, w_q_b, 0, HEADS * QK, k=2)
                load_columns(l, 5, 1, w_kv_b, 0, HEADS * P, k=1)
                load_columns(l, 6, 0, w_in, COL_DIL)
                for g in range(STEPS):
                    load_step(l, g)
                load_branches(l, 0)
                with sp.Fori(1, 4) as i:
                    wait(sp, ada_step, l, KD * ADA_UNITS)
                    load_columns(l, PN_GB + RAW_LATE + 2 * i, 0, w_in, COL_GB + i * PC)
                    load_branches(l, i)
                for i in range(4):
                    load_columns(l, PN_OUT + RAW_LATE + i, i % 2, w_out, i * PC)
                with sp.Fori(0, KF // 2) as t:
                    load_columns(l, PN_FFN + RAW_LATE + 2 * t, 0, w_ffn_gate, t * PC)
                    load_columns(l, PN_FFN + RAW_LATE + 2 * t + 1, 1, w_ffn_up, t * PC)
                for gr in range(4):
                    load_down(l, gr)

            for i in range(NT):
                sp.wait_ge(xout_left, i + 1)
                sp.wait_ge(xout_right, i + 1)
                sp.dma_start(out[0, i * P:(i + 1) * P, :], xout[:, i, :]).then_inc(stored, 16)
            sp.wait_ge(stored, 16 * NT)

        def wait_raw(eng, layer, m, slot, extra=0):
            wait(eng, raw_in[slot], layer, 16 * (m + 1 + extra))

        def spread(kind):
            if kind == "kv":
                k, wid, raw_wid = KD, PC, KV_LORA + ROPE
                moves = [(0, 0, P), (P, 0, NOPE), (P + NOPE, KV_LORA, ROPE),
                         (P + QK, KV_LORA + HALF, HALF), (P + QK + HALF, KV_LORA, HALF)]
            elif kind == "q_b":
                k, wid, raw_wid = 2 * HEADS, P, QK
                moves = [(0, 0, QK), (QK, NOPE + HALF, HALF), (QK + HALF, NOPE, HALF)]
            else:
                n = {"full": PANEL, "kv_b": HEADS * P, "six": 6 * PC}[kind]
                k, wid, raw_wid, moves = 1, n, n, [(0, 0, n)]
            return k, wid, raw_wid, moves

        def split_pieces(kind, raw_slot, dst):
            k, wid, raw_wid, moves = spread(kind)
            src = raw[raw_slot][:, 0:k * raw_wid].rearrange("p (k n) -> p k n", k=k)
            to = dst[:, 0:k * wid].rearrange("p (k n) -> p k n", k=k)
            return [(to[:, :, t:t + n], src[:, :, f:f + n]) for t, f, n in moves]

        def panel_done(p):
            if p < 0:
                return (down_part if p == -2 else down_done), 0
            if p < PN_DV:
                return lat_done, p + 1
            if p < PN_WQB:
                return vd_done, NT * (p - PN_DV + 1)
            if p < PN_DQK:
                return (q_done if p == PN_WQB else k_done), HEADS
            if p < PN_GB:
                return proj_done, 2 * (p - PN_DQK + 1)
            if p < PN_OUT:
                i = (p - PN_GB) // 2
                return (br_done, 4 * i + 4) if (p - PN_GB) % 2 else (gb_done, 2 * i + 2)
            if p < PN_FFN:
                return out_done, 2 * (p - PN_OUT + 1)
            if p < PN_DOWN:
                return (up_done if (p - PN_FFN) % 2 else gate_done), 2 * ((p - PN_FFN) // 2) + 2
            gr, q = divmod(p - PN_DOWN, 3)
            return (down_done, 2 * gr + 2) if q == 2 else (down_part, 2 * gr + q + 1)

        @block.scalar
        def _(act):
            def split_hi(l, slot, m, raw_slot, free, kind="full", extra=0):
                wait_raw(act, l, m, raw_slot, extra)
                wait(act, free[0], l, free[1])
                for to, frm in split_pieces(kind, raw_slot, w_hi[slot]):
                    last = a.activation(to, frm, ACT.Copy)
                last.then_inc(hi_set.sem, 1)

            def norm(l, n, shift):
                wait(act, norm_ss, l, n + 1)
                a.activation(rstd[:, :], ss[:, :], ACT.Ln, scale=1.0 / D, bias=eps_col[:, :]).then_inc(norm_ln.sem, 1)
                wait(act, norm_ln, l, n + 1)
                a.activation(rstd[:, :], rstd[:, :], ACT.Exp, scale=-0.5).then_inc(rstd_set.sem, 1)
                for k in range(KD):
                    wait(act, norm_t, l, KD * n + k + 1)
                    a.activation(h_hi[:, k, :], tn[:, k % 2, :], ACT.Identity, bias=mods[:, shift + k:shift + k + 1])\
                        .then_inc(h_hi_set.sem, 1)

            def square_x(l, n, slot, x_tile):
                wait(act, x_updated, l, n + 1)
                k = n % KD
                if k >= 2:
                    wait(act, sum_done, l, ADDS * (n // KD) + max(1, k - 2))
                a.activation(sq[:, slot, :], x_tile, ACT.Square).then_inc(sq_set.sem, 1)

            def load_toeplitz(head):
                src = bass.AP(tensor=bias_scratch.tensor, offset=head * P * 2 * S + P - 1,
                              ap=[[2 * S - 1, P], [1, TW]])
                act.dma_start(toep[:, head % 2, :], src).then_inc(toep_in[head % 2].sem, 16)

            a.preload_act_table_set("sigmoid_and_others")
            act.wait_ge(prm_set, DEPTH)
            a.activation(rstd[:, 0:KD], prm[:, 0, R_C:R_C + KD], ACT.Sigmoid).then_inc(sig_c_set, 1)
            act.wait_ge(angle_step, 9)
            a.activation(trig[:, :], angle[:, :], ACT.Sin).then_inc(sin_set, 1)
            a.preload_act_table_set("natural_log_exp_and_others")
            for k in range(KD):
                act.wait_ge(x_set, k + 1)
                if k >= 2:
                    act.wait_ge(sum_done.sem, max(1, k - 2))
                a.activation(sq[:, k % 2, :], xT[:, k, :], ACT.Square).then_inc(sq_set.sem, 1)

            for i in range(2):
                act.wait_ge(bias_out[i], 16 * HEADS)
            with act.Fori(0, DEPTH) as l:
                split_hi(l, 0, 0, 0, panel_done(-2))
                split_hi(l, 1, 0, 1, panel_done(-1), "kv")
                norm(l, 0, M_SH1)
                load_toeplitz(0)
                load_toeplitz(1)

                wait(act, lat_done, l, 2)
                a.activation(probT[:, 0, :], b0[:, :], ACT.Square).then_inc(lat_sq.sem, 1)
                a.activation(probT[:, 1, :], b1[:, :], ACT.Square).then_inc(lat_sq.sem, 1)
                a.activation(probT[:, 2, :], s0[:, :], ACT.Square).then_inc(lat_sq.sem, 1)
                for i in range(2):
                    a.activation(sq_qk[64:128, i, 1, :], s1[64:128, :], ACT.Square).then_inc(lat_sq.sem, 1)
                split_hi(l, 0, 1, 0, panel_done(0))
                split_hi(l, 1, 1, 1, panel_done(1))

                def dilated_v(half):
                    for i in range(NT):
                        wait(act, vd_done, l, NT * half + i + 1)
                        a.activation(v_dil[:, i, half * PC:(half + 1) * PC], tr[:, i % 2, 0:PC], ACT.Copy)\
                            .then_inc(v_set.sem, 1)

                dilated_v(0)
                for n, (acc, size) in enumerate(((ss, Q_LORA), (pv, KV_LORA))):
                    wait(act, lat_ss, l, n + 1)
                    a.activation(r_qk[:, 0, n, :], acc[:, :], ACT.Ln, scale=1.0 / size, bias=eps_col[:, :])\
                        .then_inc(lat_ln.sem, 1)
                    wait(act, lat_ln, l, n + 1)
                    a.activation(r_qk[:, 0, n, :], r_qk[:, 0, n, :], ACT.Exp, scale=-0.5).then_inc(lat_r.sem, 1)
                split_hi(l, 0, 2, 0, panel_done(2), "q_b")
                for n, to in enumerate((qc_hi[:, 0, :], qc_hi[:, 1, :], kvc_hi[:, :])):
                    wait(act, lat_t, l, n + 1)
                    a.activation(to, prob[:, n % 2, :], ACT.Copy).then_inc(lat_hi.sem, 1)
                dilated_v(1)
                split_hi(l, 1, 2, 1, panel_done(3), "kv_b")

                for i, acc in enumerate((ss, pv, ss, pv)):
                    wait(act, vm_done, l, i + 1)
                    a.activation(v_mla[:, i, :], acc[:, :], ACT.Copy).then_inc(v_set.sem, 1)

                def head_squares(h):
                    i = h % 2
                    wait(act, q_done, l, h + 1)
                    a.activation(sq_qk[0:QK, i, 0, :], bank[2 + i][0:QK, :], ACT.Square).then_inc(head_sq.sem, 1)
                    wait(act, k_done, l, h + 1)
                    a.activation(sq_qk[0:NOPE, i, 1, :], bank[i][0:NOPE, :], ACT.Square).then_inc(head_sq.sem, 1)

                def head_rms(h):
                    i = h % 2
                    wait(act, head_ss, l, h + 1)
                    if h >= 2:
                        wait(act, q_set, l, h - 1)
                        wait(act, k_set, l, h - 1)
                        wait(act, kr_set, l, h - 1)
                    a.activation(r_qk[:, i, :, :], tr[:, :, :], ACT.Ln, scale=1.0 / QK, bias=eps_col[:, :])\
                        .then_inc(head_ln.sem, 1)
                    wait(act, head_ln, l, h + 1)
                    a.activation(r_qk[:, i, :, :], r_qk[:, i, :, :], ACT.Exp, scale=-0.5).then_inc(head_r.sem, 1)

                wait(act, lat_lo, l, 3)
                head_squares(0)
                for h in range(1, HEADS):
                    head_squares(h)
                    head_rms(h - 1)
                head_rms(HEADS - 1)
                split_hi(l, 0, 3, 0, panel_done(4))

                def probT_copy(g, i):
                    n = NT * g + i
                    wait(act, transposed, l, n + 1)
                    if i == 0 and g:
                        wait(act, pv_done, l, g)
                    a.activation(probT[:, :, i * P:(i + 1) * P],
                                 tr[:, n % 2, :].rearrange("p (j q) -> p j q", j=NT), ACT.Copy)\
                        .then_inc(probT_set.sem, 1)

                def softmax_exp(g, i):
                    n = NT * g + i
                    wait(act, max_set, l, n + 1)
                    if n >= 2:
                        wait(act, transposed, l, n - 1)
                    scores = bank[2 + n % 2][:, :] if g < HEADS else prob[:, n % 2, :]
                    a.activation(prob[:, n % 2, :], scores, ACT.Exp,
                                 bias=nmax[:, i:i + 1], accum_out=den[:, i:i + 1]).then_inc(exp_set.sem, 1)

                def y_high(pair):
                    wait(act, pv_done, l, 2 * pair + 2)
                    to = ya_hi[:, pair, :] if pair < 4 else yb_hi[:, pair - 4, :]
                    a.activation(to, pv[:, :], ACT.Copy).then_inc(y_hi_set.sem, 1)

                def dilated_rms(t):
                    wait(act, dss_done, l, t + 1)
                    if t:
                        wait(act, dqk_set, l, t)
                    a.activation(rstd[:, :], ss[:, :], ACT.Ln, scale=1.0 / DH, bias=eps_col[:, :])\
                        .then_inc(dln_set.sem, 1)
                    wait(act, dln_set, l, t + 1)
                    a.activation(rstd[:, :], rstd[:, :], ACT.Exp, scale=-0.5).then_inc(dr_set.sem, 1)

                for g in range(STEPS):
                    if g % 2 == 0:
                        r = raw_of_step(g)
                        p = PN_DQK + 1 + g // 2
                        split_hi(l, p % 2, r // 2, r % 2, panel_done(p - 2))
                    softmax_exp(g, 0)
                    softmax_exp(g, 1)
                    if g and g % 2 == 0:
                        y_high(g // 2 - 1)
                    if 1 <= g <= HEADS:
                        dilated_rms(g - 1)
                    probT_copy(g, 0)
                    softmax_exp(g, 2)
                    probT_copy(g, 1)
                    softmax_exp(g, 3)
                    if HEADS <= g < STEPS - 2:
                        load_toeplitz(g - HEADS + 2)
                    wait(act, proj_done, l, g + 1)
                    if g < HEADS:
                        if g:
                            wait(act, dss_done, l, g)
                        a.activation(sumsq[:, :], bank[g % 2][:, :], ACT.Square).then_inc(dsq_set.sem, 1)
                    else:
                        a.activation(gate_a[:, g - HEADS, :], bank[g % 2][:, :], ACT.Copy).then_inc(ga_set.sem, 1)
                    probT_copy(g, 2)
                    probT_copy(g, 3)
                y_high(STEPS // 2 - 1)
                split_hi(l, 1, (PN_GB + 1 + RAW_LATE) // 2, 1, panel_done(PN_GB - 1), extra=1)
                a.preload_act_table_set("sigmoid_and_others")

                def branch(i, following):
                    for j in range(2):
                        wait(act, gb_done, l, 2 * i + j + 1)
                        a.activation(sig_b[:, j, :], bank[j][:, :], ACT.Sigmoid).then_inc(sigb_set.sem, 1)
                        a.activation(sig_a[:, j, :], gate_a[:, bass.ds(2 * i + j, 1), :], ACT.Sigmoid)\
                            .then_inc(siga_set.sem, 1)
                    following(0)
                    for j in range(2):
                        wait(act, mix_set, l, 2 * i + j + 1)
                        a.activation(m_hi[:, bass.ds(2 * i + j, 1), :], mix[:, j, :], ACT.Copy).then_inc(m_hi_set.sem, 1)
                    following(1)

                def next_branch(i):
                    def following(j):
                        m = (PN_GB + 2 + RAW_LATE) // 2 + i
                        if j == 0:
                            split_hi(l, 0, m, 0, (gb_done, 2 * i + 2))
                        else:
                            split_hi(l, 1, m, 1, (br_done, 4 * i + 4), extra=i + 2)
                    return following

                def late_hi(p, kind="full"):
                    split_hi(l, p % 2, (p + RAW_LATE) // 2, p % 2, panel_done(p - 2), kind, AB_EXTRA * (p % 2))

                def pair_at(p):
                    return lambda j: late_hi(p + j)

                with act.Fori(0, 3) as i:
                    branch(i, next_branch(i))
                branch(3, pair_at(PN_OUT))
                a.preload_act_table_set("natural_log_exp_and_others")

                for i in range(2):
                    for j in range(4):
                        square_x(l, 4 * i + j, j % 2, xT[:, 4 * i + j, :])
                        if j % 2:
                            late_hi(PN_OUT + 2 + 2 * i + j // 2)

                norm(l, 1, M_SH2)
                a.preload_act_table_set("sigmoid_and_others")

                def hidden(t, following):
                    for j in range(2):
                        wait(act, gate_done, l, 2 * t + j + 1)
                        wait(act, h_lo_set, l, 2 * KD)
                        a.activation(tn[:, j, :], bank[j][:, :], ACT.Sigmoid).then_inc(fsig_set.sem, 1)
                    following(0)
                    for j in range(2):
                        wait(act, act_set, l, 2 * t + j + 1)
                        a.activation(a_hi[:, bass.ds(2 * t + j, 1), :], sq[:, j, :], ACT.Copy).then_inc(a_hi_set.sem, 1)
                    following(1)

                def next_hidden(t):
                    m = (PN_FFN + 2 + RAW_LATE) // 2 + t
                    return lambda j: split_hi(l, j, m, j, ((gate_done, up_done)[j], 2 * t + 2), extra=AB_EXTRA * j)

                with act.Fori(0, KF // 2 - 1) as t:
                    hidden(t, next_hidden(t))
                hidden(KF // 2 - 1, pair_at(PN_DOWN))
                a.preload_act_table_set("natural_log_exp_and_others")

                for gr in range(4):
                    for q in range(3):
                        p = PN_DOWN + 2 + 3 * gr + q
                        if p < PANELS:
                            late_hi(p, "six" if (p - PN_DOWN) % 3 == 2 else "full")
                    for j in range(2):
                        square_x(l, KD + 2 * gr + j, j, xT[:, 2 * gr + j, :])

            for n in range(1, 2 * NT, 2):
                act.wait_ge(y_transposed, n + 1)
                a.activation(xout[:, n // 2, S:D], tr[:, 1, :], ACT.Copy).then_inc(xout_right, 1)

        @block.vector
        def _(dve):
            def split_lo(l, p, slot, raw_slot, kind="full"):
                wait(dve, hi_set, l, p + 1)
                his = split_pieces(kind, raw_slot, w_hi[slot])
                los = split_pieces(kind, raw_slot, w_lo[slot])
                for (hi, frm), (lo, _) in zip(his[:-1], los[:-1]):
                    v.tensor_tensor(lo, frm, hi.bitcast(F32), ALU.subtract)
                (hi, frm), (lo, _) = his[-1], los[-1]
                v.tensor_tensor(lo, frm, hi.bitcast(F32), ALU.subtract).then_inc(lo_set.sem, 1)

            def norm(l, n, shift, gain_row):
                if n:
                    wait(dve, mods_set, l, ADA_UNITS)
                v.scalar_tensor_tensor(g_norm[:, :], mods[:, shift + KD:shift + 2 * KD], 1.0,
                                       prl[:, gain_row:gain_row + KD], ALU.add, ALU.mult).then_inc(g_norm_set.sem, 1)
                wait(dve, g_norm_set, l, n + 1)
                wait(dve, rstd_set, l, n + 1)

                def low(k):
                    wait(dve, h_hi_set, l, KD * n + k + 1)
                    v.scalar_tensor_tensor(h_lo[:, k, :], tn[:, k % 2, :], mods[:, shift + k:shift + k + 1],
                                           h_hi[:, k, :].bitcast(F32), ALU.add, ALU.subtract).then_inc(h_lo_set.sem, 1)

                for k in range(KD):
                    if k >= 2:
                        wait(dve, h_lo_set, l, KD * n + k - 1)
                    v.scalar_tensor_tensor(tn[:, k % 2, :], xT[:, k, :], g_norm[:, k:k + 1], rstd[:, :],
                                           ALU.mult, ALU.mult).then_inc(norm_t.sem, 1)
                    if k:
                        low(k - 1)
                low(KD - 1)

            v.memset(ones[:, :], 1.0).then_inc(ones_set, 1)
            v.memset(spare[:, :], 0.0).then_inc(ones_set, 1)
            v.memset(eps_col[:, :], EPS).then_inc(ones_set, 1)
            dve.wait_ge(ones_set, 3)
            v.memset(spare[:, 0:1], 0.0).then_inc(lo_set.sem, lo_set.credit)
            v.memset(spare[:, 1:2], 0.0).then_inc(down_part.sem, down_part.credit)
            v.memset(spare[:, 2:3], 0.0).then_inc(down_done.sem, down_done.credit)
            for l in range(DEPTH):
                dve.wait_ge(prm_done, l + 1)
                v.tensor_copy(prm[:, l, :], tr[:, l, 0:ROWS]).then_inc(prm_set, 1)
            dve.wait_ge(sig_c_set, 1)
            v.tensor_tensor(silu_c[:, :], rstd[:, 0:KD], prm[:, 0, R_C:R_C + KD], ALU.mult).then_inc(c_set, 1)
            dve.wait_ge(pos_in, 16)
            dve.wait_ge(consts_in, 16)
            step = 0

            def angle_done(ins):
                ins.then_inc(angle_step, 1)
                dve.wait_ge(angle_step, step)

            two_pi = 2 * math.pi
            c1 = 6.28125
            c2 = float(np.float32(math.floor((two_pi - c1) * 2 ** 22) / 2 ** 22))
            c3 = float(np.float32(two_pi - c1 - c2))
            whole = float(1.5 * 2 ** 23)
            step = 1
            angle_done(v.tensor_copy(angle[:, :], pos_i[:, :]))
            step = 2
            angle_done(v.tensor_scalar(angle[:, :], angle[:, :], rope_inv, None, ALU.mult))
            step = 3
            angle_done(v.tensor_scalar(turns[:, :], angle[:, :], 1.0 / two_pi, rope_phase, ALU.mult, ALU.add))
            step = 4
            angle_done(v.tensor_scalar(turns[:, :], turns[:, :], whole, whole, ALU.add, ALU.subtract))
            for part in (c1, c2, c3):
                step += 1
                angle_done(v.scalar_tensor_tensor(angle[:, :], turns[:, :], -part, angle[:, :], ALU.mult, ALU.add))
            step = 8
            angle_done(v.tensor_scalar(angle[:, :], angle[:, :], rope_arg, None, ALU.add))
            step = 9
            pi_below = float(np.nextafter(np.float32(math.pi), np.float32(0)))
            angle_done(v.tensor_scalar(angle[:, :], angle[:, :], pi_below, -pi_below, ALU.min, ALU.max))
            dve.wait_ge(sin_set, 1)
            v.tensor_scalar(trig[:, :], trig[:, :], rope_sign, None, ALU.mult).then_inc(trig_set, 1)
            dve.wait_ge(trig_set, 1)
            v.memset(trig[0:NOPE, :], 1.0).then_inc(trig_set, 1)
            for k in range(KD):
                dve.wait_ge(x_transposed, k + 1)
                v.tensor_copy(xT[:, k, :], bank[2 + k % 2][:, :]).then_inc(x_set, 1)
            dve.wait_ge(c_set, 1)
            for u in range(4):
                dve.wait_ge(ada0_in[u], 16)
                for k in range(KD):
                    if k == 0:
                        ins = v.tensor_scalar(ada0[:, u, 0, :], ada0[:, u, 0, :], silu_c[:, 0:1], None, ALU.mult)
                    else:
                        ins = v.scalar_tensor_tensor(ada0[:, u, 0, :], ada0[:, u, k, :], silu_c[:, k:k + 1],
                                                     ada0[:, u, 0, :], ALU.mult, ALU.add)
                    ins.then_inc(ada0_step, 1)
                    dve.wait_ge(ada0_step, KD * u + k + 1)
                for n in range(4 * u, 4 * u + 4):
                    dve.wait_ge(bias_done, n + 1)
                    if n >= 2:
                        dve.wait_ge(bias_out[n % 2], 16 * (n // 2))
                    v.tensor_copy(btab[:, n % 2, :], bank[n % 2][:, :]).then_inc(btab_set, 1)
            dve.wait_ge(ada0_reduced, 1)
            v.tensor_tensor(mods[:, 0:M_G1], pv[:, 0:M_G1], prm[:, 0, R_ADAB:R_ADAB + M_G1], ALU.add)\
                .then_inc(mods0_set, 1)
            dve.wait_ge(mods0_set, 1)

            with dve.Fori(0, DEPTH) as l:
                v.tensor_copy(prl[:, :], prm[:, bass.ds(l, 1), :]).then_inc(prl_set.sem, 1)
                wait(dve, prl_set, l, 1)
                v.tensor_scalar(prl[:, R_QNB:R_QNB + 1], prl[:, R_QNB:R_QNB + 1], DH ** -0.5, None, ALU.mult)\
                    .then_inc(qnb_scaled.sem, 1)
                v.tensor_scalar(q_gain[:, :], trig[:, :], prl[:, R_QNA:R_QNA + 1], QK ** -0.5, ALU.mult, ALU.mult)\
                    .then_inc(q_gain_set.sem, 1)
                split_lo(l, 0, 0, 0)
                split_lo(l, 1, 1, 1, "kv")
                norm(l, 0, M_SH1, R_N1)

                wait(dve, lat_done, l, 2)
                wait(dve, lat_sq, l, 5)
                v.scalar_tensor_tensor(k_rot[64:128, :], s1[64:128, :], prl[64:128, R_KNA:R_KNA + 1], trig[64:128, :],
                                       ALU.mult, ALU.mult).then_inc(rot_parts.sem, 1)
                split_lo(l, 2, 0, 0)
                split_lo(l, 3, 1, 1)
                wait(dve, rot_sum, l, 1)
                v.tensor_copy(k_rot[64:128, :], s1[64:128, :]).then_inc(rot_set.sem, 1)
                latents = ((b0, 0, R_QA, qc_hi[:, 0, :], qc_lo[:, 0, :]), (b1, 0, R_QA + 1, qc_hi[:, 1, :], qc_lo[:, 1, :]),
                           (s0, 1, R_KVA, kvc_hi[:, :], kvc_lo[:, :]))
                for n, (acc, r, gain, hi, lo) in enumerate(latents):
                    wait(dve, lat_r, l, r + 1)
                    v.scalar_tensor_tensor(prob[:, n % 2, :], acc[:, :], prl[:, gain:gain + 1], r_qk[:, 0, r, :],
                                           ALU.mult, ALU.mult).then_inc(lat_t.sem, 1)
                    wait(dve, lat_hi, l, n + 1)
                    v.tensor_tensor(lo, prob[:, n % 2, :], hi.bitcast(F32), ALU.subtract).then_inc(lat_lo.sem, 1)
                    wait(dve, lat_lo, l, n + 1)
                split_lo(l, 4, 0, 0, "q_b")
                split_lo(l, 5, 1, 1, "kv_b")

                def head_scale(h):
                    i = h % 2
                    wait(dve, head_sq, l, 2 * h + 1)
                    v.tensor_tensor(qk[:, h, 0, :], bank[2 + i][:, :], q_gain[:, :], ALU.mult).then_inc(q_scaled.sem, 1)

                wait(dve, q_gain_set, l, 1)
                head_scale(0)
                for h in range(HEADS):
                    i = h % 2
                    if h + 1 < HEADS:
                        head_scale(h + 1)
                    wait(dve, head_r, l, h + 1)
                    v.scalar_tensor_tensor(qk[0:NOPE, h, 1, :], bank[i][0:NOPE, :], prl[0:NOPE, R_KNA:R_KNA + 1],
                                           r_qk[0:NOPE, i, 1, :], ALU.mult, ALU.mult).then_inc(k_set.sem, 1)
                    wait(dve, q_scaled, l, h + 1)
                    v.tensor_tensor(qk[:, h, 0, :], qk[:, h, 0, :], r_qk[:, i, 0, :], ALU.mult).then_inc(q_set.sem, 1)
                split_lo(l, 6, 0, 0)

                def ada_ops(g, first, last):
                    u = ada_unit(g)
                    if u is None:
                        return
                    r = raw_of_step(g) + (g % 2 == 0)
                    for k in range(first, last):
                        slot = (r + k // 4) % 2
                        if k % 4 == 0:
                            rr = r + k // 4
                            wait_raw(dve, l, rr // 2, rr % 2)
                        if k == 0:
                            if u:
                                wait(dve, ada_reduced, l, u)
                            ins = v.tensor_scalar(ada_acc[:, :], raw[slot][:, 0:S], silu_c[:, 0:1], None, ALU.mult)
                        else:
                            wait(dve, ada_step, l, KD * u + k)
                            ins = v.scalar_tensor_tensor(ada_acc[:, :], raw[slot][:, k % 4 * S:(k % 4 + 1) * S],
                                                         silu_c[:, k:k + 1], ada_acc[:, :], ALU.mult, ALU.add)
                        ins.then_inc(ada_step.sem, 1)

                def ada_mods(u):
                    wait(dve, ada_reduced, l, u + 1)
                    col = M_G1 + 4 * u if u < HEADS else 4 * (u - HEADS)
                    bias = prl[:, R_ADAB + col:R_ADAB + col + 4] if u < HEADS else \
                        prm[:, DEPTH - 1, R_ADAB + col:R_ADAB + col + 4]
                    v.tensor_tensor(mods[:, col:col + 4], ss[:, 0:4], bias, ALU.add).then_inc(mods_set.sem, 1)

                def softmax_max(g, i):
                    n = NT * g + i
                    wait(dve, scored, l, n + 1)
                    if g < HEADS:
                        v.tensor_reduce(nmax[:, i:i + 1], bank[2 + n % 2][:, :], AX.X, ALU.max, negate=True)\
                            .then_inc(max_set.sem, 1)
                        return
                    head = g - HEADS
                    if i == 0:
                        wait(dve, toep_in[head % 2], l, 16 * (head // 2 + 1))
                    wait(dve, transposed, l, n - 1)
                    v.tensor_tensor(prob[:, n % 2, :], bank[2 + n % 2][:, :],
                                    toep[:, head % 2, S - P - i * P:2 * S - P - i * P], ALU.add).then_inc(biased.sem, 1)
                    wait(dve, biased, l, NT * head + i + 1)
                    v.tensor_reduce(nmax[:, i:i + 1], prob[:, n % 2, :], AX.X, ALU.max, negate=True)\
                        .then_inc(max_set.sem, 1)

                def softmax_norm(g, i):
                    n = NT * g + i
                    wait(dve, exp_set, l, n + 1)
                    v.reciprocal(rden[:, i:i + 1], den[:, i:i + 1]).then_inc(rden_set.sem, 1)
                    wait(dve, rden_set, l, n + 1)
                    v.tensor_scalar(prob[:, n % 2, :], prob[:, n % 2, :], rden[:, i:i + 1], None, ALU.mult)\
                        .then_inc(prob_set.sem, 1)

                def y_low(pair):
                    wait(dve, y_hi_set, l, pair + 1)
                    hi, lo = (ya_hi[:, pair, :], ya_lo[:, pair, :]) if pair < 4 else \
                        (yb_hi[:, pair - 4, :], yb_lo[:, pair - 4, :])
                    v.tensor_tensor(lo, pv[:, :], hi.bitcast(F32), ALU.subtract).then_inc(y_lo_set.sem, 1)

                def dilated_scale(t):
                    gain = R_QNB if t < 4 else R_KNB
                    wait(dve, dr_set, l, t + 1)
                    v.scalar_tensor_tensor(dqk[:, t, :], bank[t % 2][:, :], prl[:, gain:gain + 1], rstd[:, :],
                                           ALU.mult, ALU.mult).then_inc(dqk_set.sem, 1)

                for g in range(STEPS):
                    if g % 2 == 0:
                        split_lo(l, PN_DQK + 1 + g // 2, (1 + g // 2) % 2, raw_of_step(g) % 2)
                    softmax_max(g, 0)
                    softmax_max(g, 1)
                    if g and ada_unit(g - 1) is not None:
                        ada_mods(ada_unit(g - 1))
                    softmax_norm(g, 0)
                    if g and g % 2 == 0:
                        y_low(g // 2 - 1)
                    if 1 <= g <= HEADS:
                        dilated_scale(g - 1)
                    ada_ops(g, 0, 2)
                    softmax_max(g, 2)
                    softmax_norm(g, 1)
                    ada_ops(g, 2, 4)
                    softmax_max(g, 3)
                    softmax_norm(g, 2)
                    ada_ops(g, 4, 6)
                    softmax_norm(g, 3)
                    ada_ops(g, 6, 8)
                y_low(STEPS // 2 - 1)
                split_lo(l, PN_GB + 1, 1, 1)

                def branch(i, following):
                    following(0)
                    for j in range(2):
                        n = 2 * i + j
                        wait(dve, siga_set, l, n + 1)
                        wait(dve, br_done, l, 2 * n + 1)
                        v.tensor_tensor(sig_a[:, j, :], sig_a[:, j, :], bank[2][:, :] if j == 0 else tr[:, 0, :],
                                        ALU.mult).then_inc(mix_a.sem, 1)
                        wait(dve, br_done, l, 2 * n + 2)
                        v.tensor_tensor(sig_b[:, j, :], sig_b[:, j, :], bank[3][:, :] if j == 0 else tr[:, 1, :],
                                        ALU.mult).then_inc(mix_b.sem, 1)
                        wait(dve, mix_a, l, n + 1)
                        wait(dve, mix_b, l, n + 1)
                        v.tensor_tensor(mix[:, j, :], sig_a[:, j, :], sig_b[:, j, :], ALU.add).then_inc(mix_set.sem, 1)
                    for j in range(2):
                        n = 2 * i + j
                        wait(dve, m_hi_set, l, n + 1)
                        v.tensor_tensor(m_lo[:, bass.ds(n, 1), :], mix[:, j, :], m_hi[:, bass.ds(n, 1), :].bitcast(F32),
                                        ALU.subtract).then_inc(m_lo_set.sem, 1)
                    following(1)

                def pair_at(p):
                    return lambda j: split_lo(l, p + j, j, j)

                with dve.Fori(0, 3) as i:
                    branch(i, pair_at(PN_GB + 2 + 2 * i))
                branch(3, pair_at(PN_OUT))

                def update_x(l, n, k, gate, acc):
                    v.scalar_tensor_tensor(xT[:, k, :], acc[:, :], mods[:, gate + k:gate + k + 1], xT[:, k, :],
                                           ALU.mult, ALU.add).then_inc(x_updated.sem, 1)

                wait(dve, mods_set, l, ADA_UNITS)
                for k in range(KD):
                    wait(dve, out_done, l, k + 1)
                    update_x(l, k, k, M_G1, bank[k % 4])
                    if k % 2:
                        p = PN_OUT + 2 + k // 2
                        split_lo(l, p, p % 2, p % 2)
                norm(l, 1, M_SH2, R_N2)

                def hidden(t, following):
                    for j in range(2):
                        n = 2 * t + j
                        wait(dve, fsig_set, l, n + 1)
                        v.tensor_tensor(tn[:, j, :], tn[:, j, :], bank[j][:, :], ALU.mult).then_inc(silu_set.sem, 1)
                    following(0)
                    for j in range(2):
                        n = 2 * t + j
                        wait(dve, up_done, l, n + 1)
                        wait(dve, silu_set, l, n + 1)
                        v.tensor_tensor(sq[:, j, :], tn[:, j, :], bank[2 + j][:, :], ALU.mult).then_inc(act_set.sem, 1)
                    for j in range(2):
                        n = 2 * t + j
                        wait(dve, a_hi_set, l, n + 1)
                        v.tensor_tensor(a_lo[:, bass.ds(n, 1), :], sq[:, j, :], a_hi[:, bass.ds(n, 1), :].bitcast(F32),
                                        ALU.subtract).then_inc(a_lo_set.sem, 1)
                    following(1)

                with dve.Fori(0, KF // 2 - 1) as t:
                    hidden(t, pair_at(PN_FFN + 2 + 2 * t))
                hidden(KF // 2 - 1, pair_at(PN_DOWN))

                for gr in range(4):
                    for q in range(3):
                        p = PN_DOWN + 2 + 3 * gr + q
                        if p < PANELS:
                            split_lo(l, p, p % 2, p % 2, "six" if (p - PN_DOWN) % 3 == 2 else "full")
                    for j in range(2):
                        k = 2 * gr + j
                        wait(dve, down_done, l, k + 1)
                        update_x(l, KD + k, k, M_G2, bank[k % 4])

            for n in range(0, 2 * NT, 2):
                dve.wait_ge(y_transposed, n + 1)
                v.tensor_copy(xout[:, n // 2, 0:S], tr[:, 0, :]).then_inc(xout_left, 1)

        @block.gpsimd
        def _(pool):
            pool.dma_start(bucket_sb[:, :], buckets).then_inc(buckets_in, 16)
            pool.dma_start(rel_sb[0:REL_BUCKETS, :], rel_bias).then_inc(buckets_in, 16)
            pool.dma_start(pos_i[:, :], positions.partition_broadcast(P)).then_inc(pos_in, 16)
            for i in range(NT):
                pool.dma_start(xnat[:, i, :], x[0, i * P:(i + 1) * P, :]).then_inc(x_in, 16)
            pool.memset(rel_sb[REL_BUCKETS:REL_BUCKETS + 1, :], 1.0).then_inc(rel_ones, 1)

            def add_square(k):
                first = sq[:, 0, :] if k == 1 else sumsq[:, :]
                nc.gpsimd.tensor_tensor(sumsq[:, :], first, sq[:, k % 2, :], ALU.add).then_inc(sum_done.sem, 1)

            for k in range(1, KD):
                pool.wait_ge(sq_set.sem, k + 1)
                if k >= 2:
                    pool.wait_ge(sum_done.sem, k - 1)
                add_square(k)
            for n in range(2 * HEADS):
                pool.wait_ge(btab_set, n + 1)
                if n >= 2:
                    pool.wait_ge(bias_out[n % 2], 16 * (n // 2))
                pool.dma_start(bias_scratch[n // 2, :, n % 2 * S:(n % 2 + 1) * S], btab[:, n % 2, :])\
                    .then_inc(bias_out[n % 2], 16)
            for i in range(2):
                pool.wait_ge(bias_out[i], 16 * HEADS)

            with pool.Fori(0, DEPTH) as l:
                wait(pool, rot_set, l, 1)
                for h in range(HEADS):
                    i = h % 2
                    wait(pool, head_r, l, h + 1)
                    nc.gpsimd.tensor_tensor(qk[64:128, h, 1, :], k_rot[64:128, :], r_qk[64:128, i, 1, :], ALU.mult)\
                        .then_inc(kr_set.sem, 1)
                for n in range(2):
                    wait(pool, norm_ss, l, n + 1)
                    if n == 0:
                        wait(pool, dss_done, l, HEADS)
                    for k in range(1, KD):
                        wait(pool, sq_set, l, KD * n + k + 1)
                        if k >= 2:
                            wait(pool, sum_done, l, ADDS * n + k - 1)
                        add_square(k)

        @block.tensor
        def _(pe):
            def product(out_, w, w_cols, rhs_hi, rhs_lo, start, stop):
                whi, wlo = w_hi[w][:, w_cols], w_lo[w][:, w_cols]
                pe_.matmul(out_, whi, rhs_hi, start=start, stop=False)
                pe_.matmul(out_, wlo, rhs_hi, start=False, stop=False)
                return pe_.matmul(out_, whi, rhs_lo, start=False, stop=stop)

            def cols(k, at, wid=PC, n=P):
                return slice(k * wid + at, k * wid + at + n)

            def tile_product(out_, w, at, hi, lo, k0=0, k1=KD, kn=KD, wid=PC, base=0, w_k0=0):
                for k in range(k0, k1):
                    last = product(out_, w, slice(base + (k - w_k0) * wid + at, base + (k - w_k0) * wid + at + P),
                                   hi[:, k, :], lo[:, k, :], k == 0, k == kn - 1)
                return last

            def split_ready(l, p):
                wait(pe, lo_set, l, p + 1)

            def norm_sum(l, n):
                wait(pe, sum_done, l, ADDS * n)
                pe_.matmul(ss[:, :], ones[:, :], sumsq[:, :], start=True, stop=True).then_inc(norm_ss.sem, 1)

            pe.wait_ge(consts_in, 16)
            pe.wait_ge(buckets_in, 32)
            pe.wait_ge(ones_set, 3)
            pe.wait_ge(rel_ones, 1)
            pe.wait_ge(rows_in, 16 * 17)
            for l in range(DEPTH):
                pe_.transpose(tr[:, l, 0:ROWS], rows[:, l, :], ident[0:ROWS, 0:ROWS]).then_inc(prm_done, 1)
            pe.wait_ge(x_in, 16 * NT)
            for k in range(KD):
                if k >= 2:
                    pe.wait_ge(x_set, k - 1)
                for i in range(NT):
                    last = pe_.transpose(bank[2 + k % 2][:, i * P:(i + 1) * P], xnat[:, i, k * P:(k + 1) * P], ident)
                last.then_inc(x_transposed, 1)
            for n in range(2 * HEADS):
                if n >= 2:
                    pe.wait_ge(btab_set, n - 1)
                pe_.matmul(bank[n % 2][:, :], rel_sb[:, n // 2:n // 2 + 1].broadcast_to([REL_BUCKETS + 1, P]),
                           bucket_sb[:, n % 2 * S:(n % 2 + 1) * S], start=True, stop=True).then_inc(bias_done, 1)
            for u in range(4):
                pe.wait_ge(ada0_step, KD * (u + 1))
                for j in range(4):
                    last = pe_.matmul(pv[:, 4 * u + j:4 * u + j + 1], ada0[:, u, 0, j * P:(j + 1) * P], ones[:, 0:1],
                                      start=True, stop=True)
            last.then_inc(ada0_reduced, 1)
            pe.wait_ge(mods0_set, 1)

            with pe.Fori(0, DEPTH) as l:
                norm_sum(l, 0)

                split_ready(l, 0)
                split_ready(l, 1)
                for k in range(KD):
                    wait(pe, h_lo_set, l, k + 1)
                    for j, (w, at) in enumerate(((0, 0), (0, P), (1, 0), (1, P))):
                        last = product(bank[j][:, :], w, cols(k, at), h_hi[:, k, :], h_lo[:, k, :], k == 0, k == KD - 1)
                        if k == KD - 1 and at:
                            last.then_inc(lat_done.sem, 1)

                def dilated_v(half):
                    split_ready(l, PN_DV + half)
                    for i in range(NT):
                        n = NT * half + i
                        if n >= 2:
                            wait(pe, v_set, l, n - 1)
                        tok = slice(i * P, (i + 1) * P)
                        for k in range(KD):
                            o, hh, hl = tr[:, i % 2, 0:PC], h_hi[:, k, tok], h_lo[:, k, tok]
                            whi, wlo = w_hi[half][:, k * PC:(k + 1) * PC], w_lo[half][:, k * PC:(k + 1) * PC]
                            pe_.matmul(o, hh, whi, start=k == 0, stop=False)
                            pe_.matmul(o, hh, wlo, start=False, stop=False)
                            last = pe_.matmul(o, hl, whi, start=False, stop=k == KD - 1)
                        last.then_inc(vd_done.sem, 1)

                dilated_v(0)
                wait(pe, lat_sq, l, 5)
                pe_.matmul(ss[:, :], ones[:, :], probT[:, 0, :], start=True, stop=False)
                pe_.matmul(ss[:, :], ones[:, :], probT[:, 1, :], start=False, stop=True).then_inc(lat_ss.sem, 1)
                pe_.matmul(pv[:, :], ones[:, :], probT[:, 2, :], start=True, stop=True).then_inc(lat_ss.sem, 1)
                wait(pe, rot_parts, l, 1)
                pe_.matmul(s1[:, :], pair_sum, k_rot[64:128, :], start=True, stop=True).then_inc(rot_sum.sem, 1)
                dilated_v(1)

                split_ready(l, PN_WKVB)
                wait(pe, lat_lo, l, 3)

                def heads_of(w):
                    return w[:, 0:HEADS * P].rearrange("p (h n) -> p h n", h=HEADS)[:, :, NOPE:P]

                for i, bank_ in enumerate((ss, pv, ss, pv)):
                    if i >= 2:
                        wait(pe, v_set, l, 2 * NT + i - 1)
                    tok = slice(i * P, (i + 1) * P)
                    acc = bank_[:, :].rearrange("p (h n) -> p h n", h=HEADS)
                    pe_.matmul(acc, kvc_hi[:, tok], heads_of(w_hi[1]), start=True, stop=False)
                    pe_.matmul(acc, kvc_hi[:, tok], heads_of(w_lo[1]), start=False, stop=False)
                    pe_.matmul(acc, kvc_lo[:, tok], heads_of(w_hi[1]), start=False, stop=True)\
                        .then_inc(vm_done.sem, 1)

                split_ready(l, PN_WQB)

                def head_sums(h):
                    i = h % 2
                    wait(pe, head_sq, l, 2 * h + 2)
                    if h:
                        wait(pe, head_r, l, h)
                    pe_.matmul(tr[:, 0, :], ones[0:QK, :], sq_qk[0:QK, i, 0, :], start=True, stop=True)
                    pe_.matmul(tr[:, 1, :], ones[0:QK, :], sq_qk[0:QK, i, 1, :], start=True, stop=True)\
                        .then_inc(head_ss.sem, 1)

                for h in range(HEADS):
                    i = h % 2
                    if h >= 2:
                        wait(pe, q_scaled, l, h - 1)
                        wait(pe, k_set, l, h - 1)
                    tile_product(bank[2 + i][:, :], 0, h * P, qc_hi, qc_lo, 0, 2, 2, HEADS * P).then_inc(q_done.sem, 1)
                    if h == 0:
                        wait(pe, rot_set, l, 1)
                    product(bank[i][:, :], 1, slice(h * P, (h + 1) * P), kvc_hi[:, :], kvc_lo[:, :], True, True)\
                        .then_inc(k_done.sem, 1)
                    if h:
                        head_sums(h - 1)
                head_sums(HEADS - 1)

                def scores(g, i):
                    n = NT * g + i
                    if g < HEADS:
                        if n == 0:
                            wait(pe, q_set, l, HEADS)
                            wait(pe, k_set, l, HEADS)
                            wait(pe, kr_set, l, HEADS)
                        q, k = qk[:, g, 0, i * P:(i + 1) * P], qk[:, g, 1, :]
                    else:
                        head = g - HEADS
                        half = slice(DH * (head % 2), DH * (head % 2) + DH)
                        if i == 0:
                            wait(pe, dqk_set, l, 5 + head // 2)
                        q, k = dqk[half, head // 2, i * P:(i + 1) * P], dqk[half, 4 + head // 2, :]
                    if n >= 2:
                        if n - 2 < NT * HEADS:
                            wait(pe, exp_set, l, n - 1)
                        else:
                            wait(pe, biased, l, n - 1 - NT * HEADS)
                    pe_.matmul(bank[2 + n % 2][:, :], q, k, start=True, stop=True).then_inc(scored.sem, 1)

                def transposes(g, i):
                    n = NT * g + i
                    wait(pe, prob_set, l, n + 1)
                    if n >= 2:
                        wait(pe, probT_set, l, n - 1)
                    for j in range(NT):
                        last = pe_.transpose(tr[:, n % 2, j * P:(j + 1) * P], prob[:, n % 2, j * P:(j + 1) * P], ident)
                    last.then_inc(transposed.sem, 1)

                def attend(g):
                    wait(pe, probT_set, l, NT * g + NT)
                    head = g % HEADS
                    vals = v_mla if g < HEADS else v_dil
                    if g >= 2 and g % 2 == 0:
                        wait(pe, y_lo_set, l, g // 2)
                    half = slice(DH * (head % 2), DH * (head % 2) + DH)
                    for j in range(NT):
                        last = pe_.matmul(pv[half, :], vals[:, j, head * DH:(head + 1) * DH], probT[:, j, :],
                                          start=j == 0, stop=j == NT - 1)
                    last.then_inc(pv_done.sem, 1)

                def projection(g, k0, k1):
                    p = PN_DQK + g // 2
                    if k0 == 0:
                        split_ready(l, p)
                        if g >= 2:
                            if g - 2 < HEADS:
                                wait(pe, dqk_set, l, g - 1)
                            else:
                                wait(pe, ga_set, l, g - 1 - HEADS)
                    last = tile_product(bank[g % 2][:, :], p % 2, g % 2 * P, h_hi, h_lo, k0, k1)
                    if k1 == KD:
                        last.then_inc(proj_done.sem, 1)

                def dilated_sums(t):
                    wait(pe, dsq_set, l, t + 1)
                    wait(pe, mods_set, l, t + 1)
                    pe_.matmul(ss[:, :], block_ones, sumsq[:, :], start=True, stop=True).then_inc(dss_done.sem, 1)

                def ada_reduce(g):
                    u = ada_unit(g)
                    if u is None:
                        return
                    wait(pe, ada_step, l, KD * (u + 1))
                    if g and g <= HEADS:
                        wait(pe, dln_set, l, g)
                    if u:
                        wait(pe, mods_set, l, u)
                    for j in range(4):
                        last = pe_.matmul(ss[:, j:j + 1], ada_acc[:, j * P:(j + 1) * P], ones[:, 0:1],
                                          start=True, stop=True)
                    last.then_inc(ada_reduced.sem, 1)

                for g in range(STEPS):
                    scores(g, 0)
                    scores(g, 1)
                    if g:
                        attend(g - 1)
                    if 1 <= g <= HEADS:
                        dilated_sums(g - 1)
                    projection(g, 0, 4)
                    transposes(g, 0)
                    scores(g, 2)
                    transposes(g, 1)
                    scores(g, 3)
                    projection(g, 4, KD)
                    transposes(g, 2)
                    transposes(g, 3)
                    ada_reduce(g)
                attend(STEPS - 1)

                def branch(i):
                    split_ready(l, PN_GB + 2 * i)
                    if isinstance(i, int):
                        wait(pe, ga_set, l, HEADS)
                    else:
                        wait(pe, sigb_set, l, 2 * i)
                    for j in range(2):
                        last = tile_product(bank[j][:, :], 0, j * P, h_hi, h_lo)
                        last.then_inc(gb_done.sem, 1)
                    split_ready(l, PN_GB + 1 + 2 * i)
                    if isinstance(i, int):
                        wait(pe, y_lo_set, l, STEPS // 2)
                    else:
                        wait(pe, mix_b, l, 2 * i)
                    for j in range(2):
                        acc_a, acc_b = (bank[2][:, :], bank[3][:, :]) if j == 0 else (tr[:, 0, :], tr[:, 1, :])
                        tile_product(acc_a, 1, j * P, ya_hi, ya_lo, 0, 4, 4).then_inc(br_done.sem, 1)
                        last = tile_product(acc_b, 1, j * P, yb_hi, yb_lo, 0, 4, 4, base=PANEL // 2)
                        last.then_inc(br_done.sem, 1)

                branch(0)
                with pe.Fori(1, 4) as i:
                    branch(i)

                wait(pe, m_lo_set, l, KD)
                for n in range(KD):
                    p = PN_OUT + n // 2
                    split_ready(l, p)
                    if n >= 4:
                        wait(pe, x_updated, l, n - 3)
                    last = tile_product(bank[n % 4][:, :], p % 2, n % 2 * P, m_hi, m_lo)
                    last.then_inc(out_done.sem, 1)
                norm_sum(l, 1)

                def hidden(t):
                    split_ready(l, PN_FFN + 2 * t)
                    wait(pe, h_lo_set, l, 2 * KD)
                    if not isinstance(t, int):
                        wait(pe, silu_set, l, 2 * t)
                    for j in range(2):
                        last = tile_product(bank[j][:, :], 0, j * P, h_hi, h_lo)
                        last.then_inc(gate_done.sem, 1)
                    split_ready(l, PN_FFN + 1 + 2 * t)
                    if not isinstance(t, int):
                        wait(pe, act_set, l, 2 * t)
                    for j in range(2):
                        last = tile_product(bank[2 + j][:, :], 1, j * P, h_hi, h_lo)
                        last.then_inc(up_done.sem, 1)

                hidden(0)
                with pe.Fori(1, KF // 2) as t:
                    hidden(t)

                for gr in range(4):
                    for q in range(3):
                        p = PN_DOWN + 3 * gr + q
                        split_ready(l, p)
                        if q == 0:
                            wait(pe, a_lo_set, l, KF)
                            if gr >= 2:
                                wait(pe, x_updated, l, KD + 2 * gr - 2)
                        k0, k1 = 8 * q, min(8 * q + 8, KF)
                        for j in range(2):
                            last = tile_product(bank[(2 * gr + j) % 4][:, :], p % 2, j * P, a_hi, a_lo, k0, k1, KF, w_k0=k0)
                            if q == 2:
                                last.then_inc(down_done.sem, 1)
                        if q < 2:
                            last.then_inc(down_part.sem, 1)

            pe.wait_ge(x_updated.sem, 2 * KD * DEPTH)
            for n in range(2 * NT):
                i, half = n // 2, n % 2
                if n >= 2:
                    pe.wait_ge(xout_right if half else xout_left, i)
                for k in range(4):
                    last = pe_.transpose(tr[:, half, k * P:(k + 1) * P], xT[:, 4 * half + k, i * P:(i + 1) * P], ident)
                last.then_inc(y_transposed, 1)


_INS = ["x", "c", "positions", "rel_bias", "norm1_g", "norm2_g", "ada_w", "ada_b", "w_in", "q_a_norm", "w_q_b",
        "kv_a_norm", "w_kv_b", "q_norm_a", "k_norm_a", "q_norm_b", "k_norm_b", "w_branch_a", "w_branch_b",
        "w_out", "w_ffn_gate", "w_ffn_up", "w_ffn_down"]


def shape_constants():
    cst = np.zeros((P, 3 * P + 4), np.float32)
    cst[:, 0:P] = np.eye(P)
    cst[:, P:2 * P] = np.kron(np.eye(2), np.ones((DH, DH)))
    cst[64:128, 2 * P:3 * P] = np.kron(np.ones((2, 4)), np.eye(ROPE))
    inv = (ROPE_THETA ** (-np.arange(HALF) / HALF)).astype(np.float32)
    rope = cst[:, 3 * P:]
    rope[:, 3] = 1.0
    rope[64:96, 0] = rope[96:128, 0] = np.tile(inv, 2)
    rope[64:96, 1] = 0.25
    rope[64:96, 2] = math.pi / 2
    rope[96:96 + HALF, 3] = -1.0

    rel = np.arange(-(S - 1), S + 1)
    n = np.abs(rel)
    half = REL_BUCKETS // 2
    exact = half // 2
    large = exact + (np.log(np.maximum(n, 1).astype(np.float32) / np.float32(exact))
                     / np.float32(math.log(REL_MAX_DIST / exact)) * (half - exact)).astype(np.int32)
    bucket = np.where(rel > 0, half, 0) + np.where(n < exact, n, np.minimum(large, half - 1))
    count = sum(((n % dil == 0) & (n <= window // 2)).astype(np.int64) for window, dil in PATTERNS)
    table = np.zeros((REL_BUCKETS + 1, 2 * S), np.float32)
    table[bucket, np.arange(2 * S)] = 1.0
    table[REL_BUCKETS] = np.where(count > 0, np.log(np.maximum(count, 1)), NEG_INF)
    return cst, table


def kernel(**inputs):
    import concourse.bacc as bacc
    from concourse.bass_utils import run_bass_kernel_spmd

    nc = bacc.Bacc("TRN2", target_bir_lowering=False, num_devices=1)
    arrays = {name: np.ascontiguousarray(inputs[name]) for name in _INS}
    arrays["consts"], arrays["buckets"] = shape_constants()
    args = [nc.dram_tensor(f"in_{n}", a.shape, mybir.dt.from_np(a.dtype), kind="ExternalInput").ap()
            for n, a in arrays.items()]
    out = nc.dram_tensor("out", (1, S, D), F32, kind="ExternalOutput").ap()
    encoder_trunk(nc, *args, out)
    result = run_bass_kernel_spmd(nc, [{f"in_{n}": a for n, a in arrays.items()}], core_ids=[0])
    return result.results[0]["out"]
```

```python
import math
from contextlib import ExitStack

import numpy as np

import concourse.bass as bass
from concourse import mybir

F32 = mybir.dt.float32
F32R = mybir.dt.float32r
I32 = mybir.dt.int32
ALU = mybir.AluOpType
ACT = mybir.ActivationFunctionType
AX = mybir.AxisListType

P = 128
D = 1024
S = 512
DEPTH = 2
KD = D // P
NT = S // P
HEADS = 8
Q_LORA, KV_LORA, ROPE, NOPE, VDIM = 256, 128, 32, 64, 64
QK = NOPE + ROPE
HALF = ROPE // 2
DH = 64
FFN = 2816
KF = FFN // P
EPS = 1e-6
NEG_INF = -1e30
PATTERNS = ((128, 1), (512, 4), (2048, 16))
REL_BUCKETS, REL_MAX_DIST = 32, 1024
ROPE_THETA = 10000.0
IN_COLS = Q_LORA + KV_LORA + ROPE + 3 * HEADS * DH + 2 * D
COL_KV = Q_LORA
COL_DIL = COL_KV + KV_LORA + ROPE
COL_DV = COL_DIL + 2 * HEADS * DH
COL_GA = COL_DIL + 3 * HEADS * DH
COL_GB = COL_GA + D
PANEL = 2048
PC = PANEL // KD
TW = 2 * S - P

R_ADAB, R_N1, R_N2, R_QA, R_KVA, R_QNA, R_KNA, R_QNB, R_KNB, R_C = 0, 48, 56, 64, 66, 67, 68, 69, 70, 71
ROWS = R_C + KD
M_SH1, M_SC1, M_G1, M_SH2, M_SC2, M_G2 = (KD * i for i in range(6))

PN_QC, PN_KV, PN_DV, PN_WQB, PN_WKVB, PN_DQK = 0, 1, 2, 4, 5, 6
PN_GA = PN_DQK + 4
PN_GB = PN_GA + 4
PN_OUT = PN_GB + 8
PN_FFN = PN_OUT + 4
PN_DOWN = PN_FFN + KF
PANELS = PN_DOWN + 12
ADA_UNITS = 12
STEPS = 2 * HEADS
CHUNK = PANEL // 2
RAW = 4


def ada_part(g):
    if g < HEADS:
        return g, 0, KD
    return HEADS + (g - HEADS) // 2, KD // 2 * (g % 2), KD // 2 * (g % 2 + 1)


def step_panel(g):
    return PN_DQK + 1 + g // 2 if g % 2 == 0 else None


def load_order():
    order = [("panel", p, c) for p in range(PN_DQK + 1) for c in range(2)]
    for g in range(STEPS):
        u, k0, k1 = ada_part(g)
        step = [("ada", u, j) for j in range(k0 // 2, k1 // 2)]
        if g % 2 == 0:
            step.insert(len(step) // 2 + 1, ("panel", step_panel(g), 1))
            step.insert(1, ("panel", step_panel(g), 0))
        order += step
    return order + [("panel", PN_GB + 1, c) for c in range(2)]


LOAD_ORDER = load_order()
LOADS = len(LOAD_ORDER) + 2 * (PANELS - PN_GB - 2)
LATE = (len(LOAD_ORDER) - 2 * (PN_GB + 2)) // RAW
assert len(LOAD_ORDER) % RAW == 0 and LOADS % RAW == 0 and PN_GB % 2 == 0


def load_of(kind, n, c):
    return LOAD_ORDER.index((kind, n, c))


class Event:

    def __init__(self, sem, per_layer, credit=0):
        self.sem, self.per_layer, self.credit = sem, per_layer, credit

    def at(self, layer, n):
        return layer * self.per_layer + (n + self.credit)


def encoder_trunk(nc, x, cond, positions, rel_bias, norm1_g, norm2_g, ada_w, ada_b, w_in, q_a_norm, w_q_b,
                  kv_a_norm, w_kv_b, q_norm_a, k_norm_a, q_norm_b, k_norm_b, w_branch_a, w_branch_b,
                  w_out, w_ffn_gate, w_ffn_up, w_ffn_down, consts, buckets, out):
    bias_row = nc.dram_tensor("bias_row", (HEADS, 2 * S), F32).ap()
    bias_scratch = nc.dram_tensor("bias_scratch", (HEADS, P, 2 * S), F32).ap()

    with ExitStack() as ctx:
        def sb(name, shape, dt=F32, within=ctx):
            return within.enter_context(nc.sbuf_tensor(name, shape, dt))

        def sem(name):
            return ctx.enter_context(nc.semaphore(name))

        def event(name, per_layer, credit=0):
            return Event(sem(name), per_layer, credit)

        xT = sb("xT", [P, KD, S])
        h_hi = sb("h_hi", [P, KD, S], F32R)
        h_lo = sb("h_lo", [P, KD, S], F32R)
        raw = [sb(f"raw{i}", [P, CHUNK]) for i in range(RAW)]
        w_hi = [sb(f"w_hi{i}", [P, PANEL], F32R) for i in range(2)]
        w_lo = [sb(f"w_lo{i}", [P, PANEL], F32R) for i in range(2)]
        sumsq = sb("sumsq", [P, S])
        rstd = sb("rstd", [P, S])
        trig = sb("trig", [P, S])
        cst = sb("cst", [P, 3 * P + 4])
        ones = sb("ones", [P, P])
        prm = sb("prm", [P, DEPTH, ROWS])
        prl = sb("prl", [P, ROWS])
        mods = sb("mods", [P, 6 * KD])
        g_norm = sb("g_norm", [P, KD])
        silu_c = sb("silu_c", [P, KD])
        eps_col = sb("eps_col", [P, 1])
        spare = sb("spare", [P, 4])
        nmax = sb("nmax", [P, NT])
        den = sb("den", [P, NT])
        rden = sb("rden", [P, NT])
        ident = cst[:, 0:P]
        block_ones = cst[:, P:2 * P]
        pair_sum = cst[64:128, 2 * P:3 * P]
        rope_inv, rope_phase, rope_arg, rope_sign = (cst[:, 3 * P + i:3 * P + i + 1] for i in range(4))

        def layout(*buffers):
            made = []
            with ExitStack() as scope:
                for name, shape, dt in buffers:
                    made.append(sb(name, shape, dt, scope))
            return made

        KB = 256
        (qk, dqk, v_mla, v_dil, ya_hi, ya_lo, prob, probT, toep, ada_acc) = layout(
            ("qk", [P, HEADS, 2, S], F32),
            ("dqk", [P, KD, S], F32),
            ("v_mla", [P, NT, HEADS * VDIM], F32), ("v_dil", [P, NT, HEADS * DH], F32),
            ("ya_hi", [P, 4, S], F32R), ("ya_lo", [P, 4, S], F32R),
            ("prob", [P, 2, S], F32), ("probT", [P, NT, S], F32),
            ("toep", [P, 2, TW], F32), ("ada_acc", [P, S], F32))
        (yb_hi, yb_lo, gate_a, m_hi, m_lo, _, sig_a, sig_b, mix) = layout(
            ("yb_hi", [P, 4, S], F32R), ("yb_lo", [P, 4, S], F32R), ("gate_a", [P, KD, S], F32),
            ("m_hi", [P, KD, S], F32R), ("m_lo", [P, KD, S], F32R), ("over_ya", [P, 16 * KB], F32),
            ("sig_a", [P, 2, S], F32), ("sig_b", [P, 2, S], F32), ("mix", [P, 2, S], F32))
        (_, sq_qk, r_qk, _, qc_hi, qc_lo, kvc_hi, kvc_lo, k_rot, q_gain) = layout(
            ("over_qk", [P, 32 * KB], F32), ("sq_qk", [P, 2, 2, S], F32), ("r_qk", [P, 2, 2, S], F32),
            ("over_v", [P, 16 * KB], F32),
            ("qc_hi", [P, 2, S], F32R), ("qc_lo", [P, 2, S], F32R),
            ("kvc_hi", [P, S], F32R), ("kvc_lo", [P, S], F32R), ("k_rot", [P, S], F32), ("q_gain", [P, S], F32))
        (a_hi, a_lo, tn, sq) = layout(
            ("a_hi", [P, KF, S], F32R), ("a_lo", [P, KF, S], F32R), ("tn", [P, 2, S], F32), ("sq", [P, 2, S], F32))
        (ada0, xnat, rows, pos_i, angle, turns, bucket_sb, rel_sb, _, btab) = layout(
            ("ada0", [P, 4, KD, S], F32), ("xnat", [P, NT, D], F32), ("rows", [ROWS, DEPTH, P], F32),
            ("pos_i", [P, S], I32), ("angle", [P, S], F32), ("turns", [P, S], F32),
            ("bucket_sb", [REL_BUCKETS + 1, 2 * S], F32), ("rel_sb", [REL_BUCKETS + 1, HEADS], F32),
            ("gap", [P, 5 * KB - 8], F32), ("btab", [HEADS, 2 * S], F32))
        (xout,) = layout(("xout", [P, NT, D], F32))
        sb("region", [P, 101 * KB])

        bank = [ctx.enter_context(nc.psum_tensor(f"bank{i}", [P, S], F32)) for i in range(4)]
        tr = ctx.enter_context(nc.psum_tensor("tr", [P, 2, S], F32))
        pv = ctx.enter_context(nc.psum_tensor("pv", [P, S], F32))
        ss = ctx.enter_context(nc.psum_tensor("ss", [P, S], F32))
        b0, b1, s0, s1 = bank

        consts_in, buckets_in, rows_in, pos_in, x_in, ones_set, rel_ones = (
            sem(n) for n in ("consts_in", "buckets_in", "rows_in", "pos_in", "x_in", "ones_set", "rel_ones"))
        bias_row_out, bias_out = sem("bias_row_out"), sem("bias_out")
        ada0_in = [sem(f"ada0_in{u}") for u in range(4)]
        prm_done, prm_set, sig_c_set, c_set, ada0_step, ada0_reduced, mods0_set = (
            sem(n) for n in ("prm_done", "prm_set", "sig_c_set", "c_set", "ada0_step", "ada0_reduced", "mods0_set"))
        x_transposed, x_set, bias_done, btab_set, angle_step, sin_set, trig_set = (
            sem(n) for n in ("x_transposed", "x_set", "bias_done", "btab_set", "angle_step", "sin_set", "trig_set"))
        raw_in = [event(f"raw_in{i}", 16 * LOADS // RAW) for i in range(RAW)]
        hi_set = event("hi_set", 2 * PANELS)
        POOLED = range(PN_DQK + 1, PN_GB + 1)
        lo_set = event("lo_set", 2 * (PANELS - len(POOLED)), credit=RAW)
        pool_lo_set = event("pool_lo_set", 2 * len(POOLED))

        def low_done(panel_, c):
            if isinstance(panel_, int) and panel_ in POOLED:
                return pool_lo_set, 2 * (panel_ - POOLED[0]) + c + 1
            early = isinstance(panel_, int) and panel_ < POOLED[0]
            return lo_set, 2 * (panel_ if early else panel_ - len(POOLED)) + c + 1

        x_updated = event("x_updated", 2 * KD)
        sq_set = event("sq_set", 2 * KD, credit=KD)
        ADDS = KD - 2
        sum_done = event("sum_done", 2 * ADDS, credit=ADDS)
        norm_ss = event("norm_ss", 2)
        norm_ln = event("norm_ln", 2)
        rstd_set = event("rstd_set", 2)
        norm_t = event("norm_t", 2 * KD)
        h_hi_set = event("h_hi_set", 2 * KD)
        h_lo_set = event("h_lo_set", 2 * KD)
        prl_set = event("prl_set", 1)
        qnb_scaled = event("qnb_scaled", 1)
        g_norm_set = event("g_norm_set", 2)
        lat_done = event("lat_done", 2)
        vd_done = event("vd_done", 2 * NT)
        vm_done = event("vm_done", NT)
        v_set = event("v_set", 3 * NT)
        lat_sq = event("lat_sq", 5)
        lat_ss = event("lat_ss", 2)
        lat_ln = event("lat_ln", 2)
        lat_r = event("lat_r", 2)
        lat_t = event("lat_t", 3)
        lat_hi = event("lat_hi", 3)
        lat_lo = event("lat_lo", 3)
        rot_parts = event("rot_parts", 1)
        rot_sum = event("rot_sum", 1)
        rot_set = event("rot_set", 1)
        q_gain_set = event("q_gain_set", 1)
        q_done = event("q_done", HEADS)
        k_done = event("k_done", HEADS)
        head_sq = event("head_sq", 2 * HEADS)
        head_ss = event("head_ss", HEADS)
        head_ln = event("head_ln", HEADS)
        head_r = event("head_r", HEADS)
        q_scaled = event("q_scaled", HEADS)
        q_set = event("q_set", HEADS)
        k_scaled = event("k_scaled", HEADS)
        k_set = event("k_set", HEADS)
        kr_set = event("kr_set", HEADS)
        scored = event("scored", NT * STEPS)
        biased = event("biased", NT * HEADS)
        max_set = event("max_set", NT * STEPS)
        exp_set = event("exp_set", NT * STEPS)
        rden_set = event("rden_set", NT * STEPS)
        prob_set = event("prob_set", NT * STEPS)
        transposed = event("transposed", NT * STEPS)
        probT_set = event("probT_set", NT * STEPS)
        pv_done = event("pv_done", STEPS)
        y_hi_set = event("y_hi_set", STEPS // 2)
        y_lo_set = event("y_lo_set", STEPS // 2)
        proj_done = event("proj_done", STEPS)
        dsq_set = event("dsq_set", HEADS)
        dss_done = event("dss_done", HEADS)
        dln_set = event("dln_set", HEADS)
        dr_set = event("dr_set", HEADS)
        dqk_set = event("dqk_set", HEADS)
        ga_set = event("ga_set", HEADS)
        toep_in = [event(f"toep_in{i}", 16 * HEADS // 2) for i in range(2)]
        ada_step = event("ada_step", KD * ADA_UNITS)
        ada_reduced = event("ada_reduced", ADA_UNITS)
        mods_set = event("mods_set", ADA_UNITS)
        gb_done = event("gb_done", KD)
        br_done = event("br_done", 2 * KD)
        siga_set = event("siga_set", KD)
        sigb_set = event("sigb_set", KD)
        mix_a = event("mix_a", KD)
        mix_b = event("mix_b", KD)
        mix_set = event("mix_set", KD)
        m_hi_set = event("m_hi_set", KD)
        m_lo_set = event("m_lo_set", KD)
        out_done = event("out_done", KD)
        gate_done = event("gate_done", KF)
        up_done = event("up_done", KF)
        fsig_set = event("fsig_set", KF)
        silu_set = event("silu_set", KF)
        act_set = event("act_set", KF)
        a_hi_set = event("a_hi_set", KF)
        a_lo_set = event("a_lo_set", KF)
        down_part = event("down_part", KD, credit=1)
        down_done = event("down_done", KD, credit=1)
        y_transposed, xout_left, xout_right, stored = (
            sem(n) for n in ("y_transposed", "xout_left", "xout_right", "stored"))

        block = ctx.enter_context(nc.Block())
        v = nc.vector
        a = nc.scalar
        pe_ = nc.tensor

        def wait(eng, ev, layer, n):
            eng.wait_ge(ev.sem, ev.at(layer, n))

        def panel(w, k=KD):
            return w[:, 0:PANEL].rearrange("p (k n) -> p k n", k=k)

        @block.sync
        def _(sp):
            sp.dma_start(cst[:, :], consts).then_inc(consts_in, 16)
            row_loads = [
                (R_ADAB, 6 * KD, ada_b.rearrange("l (r p) -> r l p", p=P)),
                (R_N1, KD, norm1_g.rearrange("l (r p) -> r l p", p=P)),
                (R_N2, KD, norm2_g.rearrange("l (r p) -> r l p", p=P)),
                (R_QA, 2, q_a_norm.rearrange("l (r p) -> r l p", p=P)),
                (R_KVA, 1, kv_a_norm.rearrange("l (r p) -> r l p", p=P))]
            for r, n, src in row_loads:
                sp.dma_start(rows[r:r + n, :, :], src).then_inc(rows_in, 16)
            for l in range(DEPTH):
                sp.dma_start(rows[R_C:R_C + KD, l, :], cond.rearrange("o (r p) -> (o r) p", p=P)).then_inc(rows_in, 16)
            for r, src in ((R_QNA, q_norm_a), (R_KNA, k_norm_a)):
                for at, frm, n in ((0, 0, QK), (QK, NOPE + HALF, HALF), (QK + HALF, NOPE, HALF)):
                    sp.dma_start(rows[r:r + 1, :, at:at + n], src[:, frm:frm + n].rearrange("(o l) n -> o l n", o=1))\
                        .then_inc(rows_in, 16)
            for r, src in ((R_QNB, q_norm_b), (R_KNB, k_norm_b)):
                for at in (0, DH):
                    sp.dma_start(rows[r:r + 1, :, at:at + DH], src.rearrange("(o l) n -> o l n", o=1))\
                        .then_inc(rows_in, 16)
            for u in range(4):
                sp.dma_start(ada0[:, u, :, :], ada_w[0, :, u * S:(u + 1) * S].rearrange("(k p) n -> p k n", p=P))\
                    .then_inc(ada0_in[u], 16)

            def columns(w, l, k0, k1, col, n=PC):
                return w[bass.ds(l, 1), k0 * P:k1 * P, bass.ds(col, n)].rearrange("o (k p) n -> p (o k) n", p=P)

            def load(l, slot, free, src, k):
                wait(sp, free[0], l, free[1])
                n = src.shape[-1]
                sp.dma_start(raw[slot][:, 0:k * n].rearrange("p (k n) -> p k n", k=k), src).then_inc(raw_in[slot].sem, 16)

            def half_k(w, l, c, col, n=PC):
                return columns(w, l, 4 * c, 4 * c + 4, col, n), 4

            def early_panel(l, p, c):
                if p == PN_QC:
                    return half_k(w_in, l, c, 0)
                if p == PN_KV:
                    return half_k(w_in, l, c, COL_KV, KV_LORA + ROPE)
                if p in (PN_DV, PN_DV + 1):
                    return half_k(w_in, l, c, COL_DV + (p - PN_DV) * PC)
                if p == PN_WQB:
                    return columns(w_q_b, l, c, c + 1, 0, HEADS * QK), 1
                if p == PN_WKVB:
                    return columns(w_kv_b, l, 0, 1, c * HEADS * P // 2, HEADS * P // 2), 1
                if p < PN_GA:
                    return half_k(w_in, l, c, COL_DIL + (p - PN_DQK) * PC)
                if p < PN_GB:
                    return half_k(w_in, l, c, COL_GA + (p - PN_GA) * PC)
                if p == PN_GB:
                    return half_k(w_in, l, c, COL_GB)
                return branch_weights(l, c, 0)

            def branch_weights(l, c, i):
                return columns((w_branch_a, w_branch_b)[c], l, 0, 4, i * PC), 4

            def ada_weights(l, u, j):
                layer = l if u < HEADS else DEPTH - 1
                return columns(ada_w, layer, 2 * j, 2 * j + 2, M_G1 * P + u * S if u < HEADS else (u - HEADS) * S, S), 2

            def late_slot(p, c):
                return 2 * (p % 2) + c

            with sp.Fori(0, DEPTH) as l:
                for r, (kind, n, c) in enumerate(LOAD_ORDER):
                    was, m, d = LOAD_ORDER[r - RAW] if r >= RAW else ("panel", -2 + r // 2, r % 2)
                    if was == "ada":
                        free = ada_step, KD * m + 2 * d + 2
                    else:
                        free = low_done(m, d) if m >= 0 else (lo_set, 2 * m + d + 1)
                    src, k = early_panel(l, n, c) if kind == "panel" else ada_weights(l, n, c)
                    load(l, r % RAW, free, src, k)
                with sp.Fori(1, 4) as i:
                    for j in range(2):
                        for c in range(2):
                            src, k = half_k(w_in, l, c, COL_GB + i * PC) if j == 0 else branch_weights(l, c, i)
                            if j == 0:
                                wait(sp, ada_step, l, KD * ADA_UNITS)
                            load(l, 2 * j + c, (lo_set, 2 * (PN_GB + j - len(POOLED)) + 4 * i - 4 + c + 1), src, k)
                for i in range(4):
                    for c in range(2):
                        src, k = half_k(w_out, l, c, i * PC)
                        load(l, late_slot(i, c), low_done(PN_OUT + i - 2, c), src, k)
                with sp.Fori(0, KF // 2) as t:
                    for j, w in enumerate((w_ffn_gate, w_ffn_up)):
                        for c in range(2):
                            src, k = half_k(w, l, c, t * PC)
                            load(l, 2 * j + c, low_done(PN_FFN + 2 * t + j - 2, c), src, k)
                for gr in range(4):
                    for q in range(3):
                        p = PN_DOWN + 3 * gr + q
                        for c in range(2):
                            k0 = 8 * q + 4 * c
                            k1 = min(k0 + 4, KF)
                            load(l, late_slot(p, c), low_done(p - 2, c), columns(w_ffn_down, l, k0, k1, gr * PC), k1 - k0)

            for i in range(NT):
                sp.wait_ge(xout_left, i + 1)
                sp.wait_ge(xout_right, i + 1)
                sp.dma_start(out[0, i * P:(i + 1) * P, :], xout[:, i, :]).then_inc(stored, 16)
            sp.wait_ge(stored, 16 * NT)

        def wait_raw(eng, layer, r):
            wait(eng, raw_in[r % RAW], layer, 16 * (r // RAW + 1))

        def pieces(kind, raw_slot, c, dst):
            src = raw[raw_slot]
            if kind in ("full", "six", "kv_b"):
                n = {"full": CHUNK, "six": CHUNK - c * 2 * PC, "kv_b": HEADS * P // 2}[kind]
                at = c * (n if kind == "kv_b" else CHUNK)
                return [(dst[:, at:at + n], src[:, 0:n])]
            if kind == "kv":
                k, wid, raw_wid = KD // 2, PC, KV_LORA + ROPE
                moves = [(0, 0, P), (P, 0, NOPE), (P + NOPE, KV_LORA, ROPE),
                         (P + QK, KV_LORA + HALF, HALF), (P + QK + HALF, KV_LORA, HALF)]
            else:
                k, wid, raw_wid = HEADS, P, QK
                moves = [(0, 0, QK), (QK, NOPE + HALF, HALF), (QK + HALF, NOPE, HALF)]
            frm = src[:, 0:k * raw_wid].rearrange("p (k n) -> p k n", k=k)
            to = dst[:, c * CHUNK:(c + 1) * CHUNK].rearrange("p (k n) -> p k n", k=k)
            return [(to[:, :, t:t + n], frm[:, :, f:f + n]) for t, f, n in moves]

        KINDS = {PN_KV: "kv", PN_WQB: "q_b", PN_WKVB: "kv_b"}
        KINDS.update({PN_DOWN + 3 * gr + 2: "six" for gr in range(4)})

        def panel_done(p):
            if p < 0:
                return (down_part if p == -2 else down_done), 0
            if p < PN_DV:
                return lat_done, p + 1
            if p < PN_WQB:
                return vd_done, NT * (p - PN_DV + 1)
            if p < PN_DQK:
                return (q_done if p == PN_WQB else k_done), HEADS
            if p < PN_GB:
                return proj_done, 2 * (p - PN_DQK + 1)
            if p < PN_OUT:
                i = (p - PN_GB) // 2
                return (br_done, 4 * i + 4) if (p - PN_GB) % 2 else (gb_done, 2 * i + 2)
            if p < PN_FFN:
                return out_done, 2 * (p - PN_OUT + 1)
            if p < PN_DOWN:
                return (up_done if (p - PN_FFN) % 2 else gate_done), 2 * ((p - PN_FFN) // 2) + 2
            gr, q = divmod(p - PN_DOWN, 3)
            return (down_done, 2 * gr + 2) if q == 2 else (down_part, 2 * gr + q + 1)

        @block.scalar
        def _(act):
            def hi_chunk(l, slot, c, raw_slot, landed, free=None, kind="full"):
                wait(act, raw_in[raw_slot], l, 16 * landed)
                if free:
                    wait(act, free[0], l, free[1])
                for to, frm in pieces(kind, raw_slot, c, w_hi[slot]):
                    last = a.activation(to, frm, ACT.Copy)
                last.then_inc(hi_set.sem, 1)

            def panel_hi(l, p, chunks=(0, 1)):
                for c in chunks:
                    r = load_of("panel", p, c) if p < PN_GB + 2 else 2 * p + c + RAW * LATE
                    hi_chunk(l, p % 2, c, r % RAW, r // RAW + 1, panel_done(p - 2) if c == 0 else None,
                             KINDS.get(p, "full"))

            def norm(l, n, shift, between=lambda k: None):
                wait(act, norm_ss, l, n + 1)
                a.activation(rstd[:, :], ss[:, :], ACT.Ln, scale=1.0 / D, bias=eps_col[:, :]).then_inc(norm_ln.sem, 1)
                wait(act, norm_ln, l, n + 1)
                a.activation(rstd[:, :], rstd[:, :], ACT.Exp, scale=-0.5).then_inc(rstd_set.sem, 1)
                for k in range(KD):
                    wait(act, norm_t, l, KD * n + k + 1)
                    a.activation(h_hi[:, k, :], tn[:, k % 2, :], ACT.Identity, bias=mods[:, shift + k:shift + k + 1])\
                        .then_inc(h_hi_set.sem, 1)
                    between(k)

            def square_x(l, n, slot, x_tile):
                wait(act, x_updated, l, n + 1)
                k = n % KD
                if k >= 2:
                    wait(act, sum_done, l, ADDS * (n // KD) + max(1, k - 2))
                a.activation(sq[:, slot, :], x_tile, ACT.Square).then_inc(sq_set.sem, 1)

            def load_toeplitz(head):
                src = bass.AP(tensor=bias_scratch.tensor, offset=head * P * 2 * S + P - 1,
                              ap=[[2 * S - 1, P], [1, TW]])
                act.dma_start(toep[:, head % 2, :], src).then_inc(toep_in[head % 2].sem, 16)

            a.preload_act_table_set("sigmoid_and_others")
            act.wait_ge(prm_set, DEPTH)
            a.activation(rstd[:, 0:KD], prm[:, 0, R_C:R_C + KD], ACT.Sigmoid).then_inc(sig_c_set, 1)
            act.wait_ge(angle_step, 9)
            a.activation(trig[:, :], angle[:, :], ACT.Sin).then_inc(sin_set, 1)
            a.preload_act_table_set("natural_log_exp_and_others")
            for k in range(KD):
                act.wait_ge(x_set, k + 1)
                if k >= 2:
                    act.wait_ge(sum_done.sem, max(1, k - 2))
                a.activation(sq[:, k % 2, :], xT[:, k, :], ACT.Square).then_inc(sq_set.sem, 1)

            act.wait_ge(bias_out, 16)
            with act.Fori(0, DEPTH) as l:
                panel_hi(l, 0)
                panel_hi(l, 1)
                norm(l, 0, M_SH1)
                load_toeplitz(0)
                load_toeplitz(1)

                wait(act, lat_done, l, 2)
                a.activation(probT[:, 0, :], b0[:, :], ACT.Square).then_inc(lat_sq.sem, 1)
                a.activation(probT[:, 1, :], b1[:, :], ACT.Square).then_inc(lat_sq.sem, 1)
                a.activation(probT[:, 2, :], s0[:, :], ACT.Square).then_inc(lat_sq.sem, 1)
                for i in range(2):
                    a.activation(sq_qk[64:128, i, 1, :], s1[64:128, :], ACT.Square).then_inc(lat_sq.sem, 1)
                panel_hi(l, 2)
                panel_hi(l, 3)

                def dilated_v(half):
                    for i in range(NT):
                        wait(act, vd_done, l, NT * half + i + 1)
                        a.activation(v_dil[:, i, half * PC:(half + 1) * PC], tr[:, i % 2, 0:PC], ACT.Copy)\
                            .then_inc(v_set.sem, 1)

                dilated_v(0)
                for n, (acc, size) in enumerate(((ss, Q_LORA), (pv, KV_LORA))):
                    wait(act, lat_ss, l, n + 1)
                    a.activation(r_qk[:, 0, n, :], acc[:, :], ACT.Ln, scale=1.0 / size, bias=eps_col[:, :])\
                        .then_inc(lat_ln.sem, 1)
                    wait(act, lat_ln, l, n + 1)
                    a.activation(r_qk[:, 0, n, :], r_qk[:, 0, n, :], ACT.Exp, scale=-0.5).then_inc(lat_r.sem, 1)
                panel_hi(l, 4)
                for n, to in enumerate((qc_hi[:, 0, :], qc_hi[:, 1, :], kvc_hi[:, :])):
                    wait(act, lat_t, l, n + 1)
                    a.activation(to, prob[:, n % 2, :], ACT.Copy).then_inc(lat_hi.sem, 1)
                dilated_v(1)
                panel_hi(l, 5)

                for i, acc in enumerate((ss, pv, ss, pv)):
                    wait(act, vm_done, l, i + 1)
                    a.activation(v_mla[:, i, :], acc[:, :], ACT.Copy).then_inc(v_set.sem, 1)

                def head_squares(h):
                    i = h % 2
                    wait(act, q_done, l, h + 1)
                    a.activation(sq_qk[0:QK, i, 0, :], bank[2 + i][0:QK, :], ACT.Square).then_inc(head_sq.sem, 1)
                    wait(act, k_done, l, h + 1)
                    a.activation(sq_qk[0:NOPE, i, 1, :], bank[i][0:NOPE, :], ACT.Square).then_inc(head_sq.sem, 1)

                def head_rms(h):
                    i = h % 2
                    wait(act, head_ss, l, h + 1)
                    if h >= 2:
                        wait(act, q_set, l, h - 1)
                        wait(act, kr_set, l, h - 1)
                    a.activation(r_qk[:, i, :, :], tr[:, :, :], ACT.Ln, scale=1.0 / QK, bias=eps_col[:, :])\
                        .then_inc(head_ln.sem, 1)
                    wait(act, head_ln, l, h + 1)
                    a.activation(r_qk[:, i, :, :], r_qk[:, i, :, :], ACT.Exp, scale=-0.5).then_inc(head_r.sem, 1)

                wait(act, lat_lo, l, 3)
                head_squares(0)
                for h in range(1, HEADS):
                    head_squares(h)
                    head_rms(h - 1)
                head_rms(HEADS - 1)
                panel_hi(l, 6)

                def probT_copy(g, i):
                    n = NT * g + i
                    wait(act, transposed, l, n + 1)
                    if i == 0 and g:
                        wait(act, pv_done, l, g)
                    a.activation(probT[:, :, i * P:(i + 1) * P],
                                 tr[:, n % 2, :].rearrange("p (j q) -> p j q", j=NT), ACT.Copy)\
                        .then_inc(probT_set.sem, 1)

                def softmax_exp(g, i):
                    n = NT * g + i
                    wait(act, max_set, l, n + 1)
                    if n >= 2:
                        wait(act, transposed, l, n - 1)
                    scores = bank[2 + n % 2][:, :] if g < HEADS else prob[:, n % 2, :]
                    a.activation(prob[:, n % 2, :], scores, ACT.Exp,
                                 bias=nmax[:, i:i + 1], accum_out=den[:, i:i + 1]).then_inc(exp_set.sem, 1)

                def y_high(pair):
                    wait(act, pv_done, l, 2 * pair + 2)
                    to = ya_hi[:, pair, :] if pair < 4 else yb_hi[:, pair - 4, :]
                    a.activation(to, pv[:, :], ACT.Copy).then_inc(y_hi_set.sem, 1)

                def dilated_rms(t):
                    wait(act, dss_done, l, t + 1)
                    if t:
                        wait(act, dqk_set, l, t)
                    a.activation(rstd[:, :], ss[:, :], ACT.Ln, scale=1.0 / DH, bias=eps_col[:, :])\
                        .then_inc(dln_set.sem, 1)
                    wait(act, dln_set, l, t + 1)
                    a.activation(rstd[:, :], rstd[:, :], ACT.Exp, scale=-0.5).then_inc(dr_set.sem, 1)

                for g in range(STEPS):
                    softmax_exp(g, 0)
                    softmax_exp(g, 1)
                    if g and g % 2 == 0:
                        y_high(g // 2 - 1)
                    if 1 <= g <= HEADS:
                        dilated_rms(g - 1)
                    probT_copy(g, 0)
                    if g % 2 == 0:
                        panel_hi(l, step_panel(g), (0,))
                    softmax_exp(g, 2)
                    probT_copy(g, 1)
                    softmax_exp(g, 3)
                    if HEADS <= g < STEPS - 2:
                        load_toeplitz(g - HEADS + 2)
                    if g % 2 == 0:
                        panel_hi(l, step_panel(g), (1,))
                    wait(act, proj_done, l, g + 1)
                    if g < HEADS:
                        if g:
                            wait(act, dss_done, l, g)
                        a.activation(sumsq[:, :], bank[g % 2][:, :], ACT.Square).then_inc(dsq_set.sem, 1)
                    else:
                        a.activation(gate_a[:, g - HEADS, :], bank[g % 2][:, :], ACT.Copy).then_inc(ga_set.sem, 1)
                    probT_copy(g, 2)
                    probT_copy(g, 3)
                y_high(STEPS // 2 - 1)
                panel_hi(l, PN_GB + 1)
                a.preload_act_table_set("sigmoid_and_others")

                def branch(i, following):
                    for j in range(2):
                        wait(act, gb_done, l, 2 * i + j + 1)
                        a.activation(sig_b[:, j, :], bank[j][:, :], ACT.Sigmoid).then_inc(sigb_set.sem, 1)
                        a.activation(sig_a[:, j, :], gate_a[:, bass.ds(2 * i + j, 1), :], ACT.Sigmoid)\
                            .then_inc(siga_set.sem, 1)
                    following(0)
                    for j in range(2):
                        wait(act, mix_set, l, 2 * i + j + 1)
                        a.activation(m_hi[:, bass.ds(2 * i + j, 1), :], mix[:, j, :], ACT.Copy).then_inc(m_hi_set.sem, 1)
                    following(1)

                def next_branch(i):
                    def following(j):
                        free = (gb_done, 2 * i + 2) if j == 0 else (br_done, 4 * i + 4)
                        for c in range(2):
                            hi_chunk(l, j, c, 2 * j + c, PN_GB // 2 + 2 + LATE + i, free if c == 0 else None)
                    return following

                def pair_at(p):
                    return lambda j: panel_hi(l, p + j)

                with act.Fori(0, 3) as i:
                    branch(i, next_branch(i))
                branch(3, pair_at(PN_OUT))
                a.preload_act_table_set("natural_log_exp_and_others")

                for i in range(2):
                    for j in range(4):
                        square_x(l, 4 * i + j, j % 2, xT[:, 4 * i + j, :])
                        if i == 0 and j % 2:
                            panel_hi(l, PN_OUT + 2 + j // 2)

                panel_hi(l, PN_FFN)
                norm(l, 1, M_SH2, lambda k: panel_hi(l, PN_FFN + 1, (k,)) if k < 2 else None)
                a.preload_act_table_set("sigmoid_and_others")

                def hidden(t, following):
                    for j in range(2):
                        wait(act, gate_done, l, 2 * t + j + 1)
                        wait(act, h_lo_set, l, 2 * KD)
                        a.activation(tn[:, j, :], bank[j][:, :], ACT.Sigmoid).then_inc(fsig_set.sem, 1)
                    following(0)
                    for j in range(2):
                        wait(act, act_set, l, 2 * t + j + 1)
                        a.activation(a_hi[:, bass.ds(2 * t + j, 1), :], sq[:, j, :], ACT.Copy).then_inc(a_hi_set.sem, 1)
                    following(1)

                def next_hidden(t):
                    def following(j):
                        for c in range(2):
                            hi_chunk(l, j, c, 2 * j + c, PN_FFN // 2 + 2 + LATE + t,
                                     ((gate_done, up_done)[j], 2 * t + 2) if c == 0 else None)
                    return following

                with act.Fori(0, KF // 2 - 1) as t:
                    hidden(t, next_hidden(t))
                hidden(KF // 2 - 1, pair_at(PN_DOWN))
                a.preload_act_table_set("natural_log_exp_and_others")

                for gr in range(4):
                    for q in range(3):
                        p = PN_DOWN + 2 + 3 * gr + q
                        if p < PANELS:
                            panel_hi(l, p)
                    for j in range(2):
                        square_x(l, KD + 2 * gr + j, j, xT[:, 2 * gr + j, :])

            for n in range(1, 2 * NT, 2):
                act.wait_ge(y_transposed, n + 1)
                a.activation(xout[:, n // 2, S:D], tr[:, 1, :], ACT.Copy).then_inc(xout_right, 1)

        @block.vector
        def _(dve):
            def lo_chunk(l, slot, c, raw_slot, made, kind="full"):
                wait(dve, hi_set, l, made)
                parts = list(zip(pieces(kind, raw_slot, c, w_hi[slot]), pieces(kind, raw_slot, c, w_lo[slot])))
                for (hi, frm), (lo, _) in parts:
                    last = v.tensor_tensor(lo, frm, hi.bitcast(F32), ALU.subtract)
                last.then_inc(lo_set.sem, 1)

            def panel_lo(l, p, chunks=(0, 1)):
                for c in chunks:
                    r = load_of("panel", p, c) if p < PN_GB + 2 else 2 * p + c + RAW * LATE
                    lo_chunk(l, p % 2, c, r % RAW, 2 * p + c + 1, KINDS.get(p, "full"))

            def norm(l, n, shift, gain_row):
                v.scalar_tensor_tensor(g_norm[:, :], mods[:, shift + KD:shift + 2 * KD], 1.0,
                                       prl[:, gain_row:gain_row + KD], ALU.add, ALU.mult).then_inc(g_norm_set.sem, 1)
                wait(dve, g_norm_set, l, n + 1)
                wait(dve, rstd_set, l, n + 1)

                def low(k):
                    wait(dve, h_hi_set, l, KD * n + k + 1)
                    v.scalar_tensor_tensor(h_lo[:, k, :], tn[:, k % 2, :], mods[:, shift + k:shift + k + 1],
                                           h_hi[:, k, :].bitcast(F32), ALU.add, ALU.subtract).then_inc(h_lo_set.sem, 1)

                for k in range(KD):
                    if k >= 2:
                        wait(dve, h_lo_set, l, KD * n + k - 1)
                    v.scalar_tensor_tensor(tn[:, k % 2, :], xT[:, k, :], g_norm[:, k:k + 1], rstd[:, :],
                                           ALU.mult, ALU.mult).then_inc(norm_t.sem, 1)
                    if k:
                        low(k - 1)
                low(KD - 1)

            v.memset(ones[:, :], 1.0).then_inc(ones_set, 1)
            v.memset(spare[:, :], 0.0).then_inc(ones_set, 1)
            v.memset(eps_col[:, :], EPS).then_inc(ones_set, 1)
            dve.wait_ge(ones_set, 3)
            v.memset(spare[:, 0:1], 0.0).then_inc(lo_set.sem, lo_set.credit)
            v.memset(spare[:, 1:2], 0.0).then_inc(down_part.sem, down_part.credit)
            v.memset(spare[:, 2:3], 0.0).then_inc(down_done.sem, down_done.credit)
            for l in range(DEPTH):
                dve.wait_ge(prm_done, l + 1)
                v.tensor_copy(prm[:, l, :], tr[:, l, 0:ROWS]).then_inc(prm_set, 1)
            dve.wait_ge(sig_c_set, 1)
            v.tensor_tensor(silu_c[:, :], rstd[:, 0:KD], prm[:, 0, R_C:R_C + KD], ALU.mult).then_inc(c_set, 1)
            dve.wait_ge(pos_in, 16)
            dve.wait_ge(consts_in, 16)
            step = 0

            def angle_done(ins):
                ins.then_inc(angle_step, 1)
                dve.wait_ge(angle_step, step)

            two_pi = 2 * math.pi
            c1 = 6.28125
            c2 = float(np.float32(math.floor((two_pi - c1) * 2 ** 22) / 2 ** 22))
            c3 = float(np.float32(two_pi - c1 - c2))
            whole = float(1.5 * 2 ** 23)
            step = 1
            angle_done(v.tensor_copy(angle[:, :], pos_i[:, :]))
            step = 2
            angle_done(v.tensor_scalar(angle[:, :], angle[:, :], rope_inv, None, ALU.mult))
            step = 3
            angle_done(v.tensor_scalar(turns[:, :], angle[:, :], 1.0 / two_pi, rope_phase, ALU.mult, ALU.add))
            step = 4
            angle_done(v.tensor_scalar(turns[:, :], turns[:, :], whole, whole, ALU.add, ALU.subtract))
            for part in (c1, c2, c3):
                step += 1
                angle_done(v.scalar_tensor_tensor(angle[:, :], turns[:, :], -part, angle[:, :], ALU.mult, ALU.add))
            step = 8
            angle_done(v.tensor_scalar(angle[:, :], angle[:, :], rope_arg, None, ALU.add))
            step = 9
            pi_below = float(np.nextafter(np.float32(math.pi), np.float32(0)))
            angle_done(v.tensor_scalar(angle[:, :], angle[:, :], pi_below, -pi_below, ALU.min, ALU.max))
            for i in range(2):
                dve.wait_ge(bias_done, i + 1)
                v.tensor_copy(btab[:, i * S:(i + 1) * S], bank[i][0:HEADS, :]).then_inc(btab_set, 1)
            dve.wait_ge(sin_set, 1)
            v.tensor_scalar(trig[:, :], trig[:, :], rope_sign, None, ALU.mult).then_inc(trig_set, 1)
            dve.wait_ge(trig_set, 1)
            v.memset(trig[0:NOPE, :], 1.0).then_inc(trig_set, 1)
            for k in range(KD):
                dve.wait_ge(x_transposed, k + 1)
                v.tensor_copy(xT[:, k, :], bank[2 + k % 2][:, :]).then_inc(x_set, 1)
            dve.wait_ge(c_set, 1)
            for u in range(4):
                dve.wait_ge(ada0_in[u], 16)
                for k in range(KD):
                    if k == 0:
                        ins = v.tensor_scalar(ada0[:, u, 0, :], ada0[:, u, 0, :], silu_c[:, 0:1], None, ALU.mult)
                    else:
                        ins = v.scalar_tensor_tensor(ada0[:, u, 0, :], ada0[:, u, k, :], silu_c[:, k:k + 1],
                                                     ada0[:, u, 0, :], ALU.mult, ALU.add)
                    ins.then_inc(ada0_step, 1)
                    dve.wait_ge(ada0_step, KD * u + k + 1)
            dve.wait_ge(ada0_reduced, 1)
            v.tensor_tensor(mods[:, 0:M_G1], pv[:, 0:M_G1], prm[:, 0, R_ADAB:R_ADAB + M_G1], ALU.add)\
                .then_inc(mods0_set, 1)
            dve.wait_ge(mods0_set, 1)

            with dve.Fori(0, DEPTH) as l:
                v.tensor_copy(prl[:, :], prm[:, bass.ds(l, 1), :]).then_inc(prl_set.sem, 1)
                wait(dve, prl_set, l, 1)
                v.tensor_scalar(prl[:, R_QNB:R_QNB + 1], prl[:, R_QNB:R_QNB + 1], DH ** -0.5, None, ALU.mult)\
                    .then_inc(qnb_scaled.sem, 1)
                v.tensor_scalar(q_gain[:, :], trig[:, :], prl[:, R_QNA:R_QNA + 1], QK ** -0.5, ALU.mult, ALU.mult)\
                    .then_inc(q_gain_set.sem, 1)
                panel_lo(l, 0)
                panel_lo(l, 1)
                norm(l, 0, M_SH1, R_N1)

                wait(dve, lat_done, l, 2)
                wait(dve, lat_sq, l, 5)
                v.scalar_tensor_tensor(k_rot[64:128, :], s1[64:128, :], prl[64:128, R_KNA:R_KNA + 1], trig[64:128, :],
                                       ALU.mult, ALU.mult).then_inc(rot_parts.sem, 1)
                panel_lo(l, 2)
                panel_lo(l, 3)
                wait(dve, rot_sum, l, 1)
                v.tensor_copy(k_rot[64:128, :], s1[64:128, :]).then_inc(rot_set.sem, 1)
                latents = ((b0, 0, R_QA, qc_hi[:, 0, :], qc_lo[:, 0, :]), (b1, 0, R_QA + 1, qc_hi[:, 1, :], qc_lo[:, 1, :]),
                           (s0, 1, R_KVA, kvc_hi[:, :], kvc_lo[:, :]))
                for n, (acc, r, gain, hi, lo) in enumerate(latents):
                    wait(dve, lat_r, l, r + 1)
                    v.scalar_tensor_tensor(prob[:, n % 2, :], acc[:, :], prl[:, gain:gain + 1], r_qk[:, 0, r, :],
                                           ALU.mult, ALU.mult).then_inc(lat_t.sem, 1)
                    wait(dve, lat_hi, l, n + 1)
                    v.tensor_tensor(lo, prob[:, n % 2, :], hi.bitcast(F32), ALU.subtract).then_inc(lat_lo.sem, 1)
                    wait(dve, lat_lo, l, n + 1)
                panel_lo(l, 4)
                panel_lo(l, 5)

                def head_scale(h):
                    i = h % 2
                    wait(dve, head_sq, l, 2 * h + 1)
                    v.tensor_tensor(qk[:, h, 0, :], bank[2 + i][:, :], q_gain[:, :], ALU.mult).then_inc(q_scaled.sem, 1)
                    wait(dve, head_sq, l, 2 * h + 2)
                    v.tensor_scalar(qk[0:NOPE, h, 1, :], bank[i][0:NOPE, :], prl[0:NOPE, R_KNA:R_KNA + 1], None,
                                    ALU.mult).then_inc(k_scaled.sem, 1)

                wait(dve, q_gain_set, l, 1)
                head_scale(0)
                for h in range(HEADS):
                    if h + 1 < HEADS:
                        head_scale(h + 1)
                    wait(dve, head_r, l, h + 1)
                    wait(dve, q_scaled, l, h + 1)
                    v.tensor_tensor(qk[:, h, 0, :], qk[:, h, 0, :], r_qk[:, h % 2, 0, :], ALU.mult).then_inc(q_set.sem, 1)
                panel_lo(l, 6)

                def ada_ops(g, part):
                    u, k0, k1 = ada_part(g)
                    n = (k1 - k0) // 4
                    for k in range(k0 + part * n, k0 + (part + 1) * n):
                        r = load_of("ada", u, k // 2)
                        src = raw[r % RAW][:, k % 2 * S:(k % 2 + 1) * S]
                        if k % 2 == 0:
                            wait_raw(dve, l, r)
                        if k == 0:
                            if u:
                                wait(dve, ada_reduced, l, u)
                            ins = v.tensor_scalar(ada_acc[:, :], src, silu_c[:, 0:1], None, ALU.mult)
                        else:
                            wait(dve, ada_step, l, KD * u + k)
                            ins = v.scalar_tensor_tensor(ada_acc[:, :], src, silu_c[:, k:k + 1], ada_acc[:, :],
                                                         ALU.mult, ALU.add)
                        ins.then_inc(ada_step.sem, 1)

                def ada_mods(u):
                    wait(dve, ada_reduced, l, u + 1)
                    col = M_G1 + 4 * u if u < HEADS else 4 * (u - HEADS)
                    bias = prl[:, R_ADAB + col:R_ADAB + col + 4] if u < HEADS else \
                        prm[:, DEPTH - 1, R_ADAB + col:R_ADAB + col + 4]
                    v.tensor_tensor(mods[:, col:col + 4], ss[:, 0:4], bias, ALU.add).then_inc(mods_set.sem, 1)

                def softmax_max(g, i):
                    n = NT * g + i
                    wait(dve, scored, l, n + 1)
                    if g < HEADS:
                        v.tensor_reduce(nmax[:, i:i + 1], bank[2 + n % 2][:, :], AX.X, ALU.max, negate=True)\
                            .then_inc(max_set.sem, 1)
                        return
                    head = g - HEADS
                    if i == 0:
                        wait(dve, toep_in[head % 2], l, 16 * (head // 2 + 1))
                    wait(dve, transposed, l, n - 1)
                    v.tensor_tensor(prob[:, n % 2, :], bank[2 + n % 2][:, :],
                                    toep[:, head % 2, S - P - i * P:2 * S - P - i * P], ALU.add).then_inc(biased.sem, 1)
                    wait(dve, biased, l, NT * head + i + 1)
                    v.tensor_reduce(nmax[:, i:i + 1], prob[:, n % 2, :], AX.X, ALU.max, negate=True)\
                        .then_inc(max_set.sem, 1)

                def softmax_norm(g, i):
                    n = NT * g + i
                    wait(dve, exp_set, l, n + 1)
                    v.reciprocal(rden[:, i:i + 1], den[:, i:i + 1]).then_inc(rden_set.sem, 1)
                    wait(dve, rden_set, l, n + 1)
                    v.tensor_scalar(prob[:, n % 2, :], prob[:, n % 2, :], rden[:, i:i + 1], None, ALU.mult)\
                        .then_inc(prob_set.sem, 1)

                def y_low(pair):
                    wait(dve, y_hi_set, l, pair + 1)
                    hi, lo = (ya_hi[:, pair, :], ya_lo[:, pair, :]) if pair < 4 else \
                        (yb_hi[:, pair - 4, :], yb_lo[:, pair - 4, :])
                    v.tensor_tensor(lo, pv[:, :], hi.bitcast(F32), ALU.subtract).then_inc(y_lo_set.sem, 1)

                def dilated_scale(t):
                    gain = R_QNB if t < 4 else R_KNB
                    wait(dve, dr_set, l, t + 1)
                    v.scalar_tensor_tensor(dqk[:, t, :], bank[t % 2][:, :], prl[:, gain:gain + 1], rstd[:, :],
                                           ALU.mult, ALU.mult).then_inc(dqk_set.sem, 1)

                for g in range(STEPS):
                    softmax_max(g, 0)
                    softmax_max(g, 1)
                    if g and ada_part(g - 1)[2] == KD:
                        ada_mods(ada_part(g - 1)[0])
                    softmax_norm(g, 0)
                    softmax_norm(g, 1)
                    if g and g % 2 == 0:
                        y_low(g // 2 - 1)
                    ada_ops(g, 0)
                    if 1 <= g <= HEADS:
                        dilated_scale(g - 1)
                    softmax_max(g, 2)
                    ada_ops(g, 1)
                    softmax_max(g, 3)
                    softmax_norm(g, 2)
                    softmax_norm(g, 3)
                    ada_ops(g, 2)
                    ada_ops(g, 3)
                ada_mods(ADA_UNITS - 1)
                y_low(STEPS // 2 - 1)
                panel_lo(l, PN_GB + 1)

                def branch(i, following):
                    following(0)
                    for j in range(2):
                        n = 2 * i + j
                        wait(dve, siga_set, l, n + 1)
                        wait(dve, br_done, l, 2 * n + 1)
                        v.tensor_tensor(sig_a[:, j, :], sig_a[:, j, :], bank[2][:, :] if j == 0 else tr[:, 0, :],
                                        ALU.mult).then_inc(mix_a.sem, 1)
                        wait(dve, br_done, l, 2 * n + 2)
                        v.tensor_tensor(sig_b[:, j, :], sig_b[:, j, :], bank[3][:, :] if j == 0 else tr[:, 1, :],
                                        ALU.mult).then_inc(mix_b.sem, 1)
                        wait(dve, mix_a, l, n + 1)
                        wait(dve, mix_b, l, n + 1)
                        v.tensor_tensor(mix[:, j, :], sig_a[:, j, :], sig_b[:, j, :], ALU.add).then_inc(mix_set.sem, 1)
                    for j in range(2):
                        n = 2 * i + j
                        wait(dve, m_hi_set, l, n + 1)
                        v.tensor_tensor(m_lo[:, bass.ds(n, 1), :], mix[:, j, :], m_hi[:, bass.ds(n, 1), :].bitcast(F32),
                                        ALU.subtract).then_inc(m_lo_set.sem, 1)
                    following(1)

                def pair_at(p):
                    def following(j):
                        for c in range(2):
                            lo_chunk(l, j, c, 2 * j + c, 2 * (p + j) + c + 1)
                    return following

                with dve.Fori(0, 3) as i:
                    branch(i, pair_at(PN_GB + 2 + 2 * i))
                branch(3, pair_at(PN_OUT))

                def update_x(l, n, k, gate, acc):
                    v.scalar_tensor_tensor(xT[:, k, :], acc[:, :], mods[:, gate + k:gate + k + 1], xT[:, k, :],
                                           ALU.mult, ALU.add).then_inc(x_updated.sem, 1)

                wait(dve, mods_set, l, ADA_UNITS)
                for k in range(KD):
                    wait(dve, out_done, l, k + 1)
                    update_x(l, k, k, M_G1, bank[k % 4])
                    if k in (1, 3):
                        panel_lo(l, PN_OUT + 2 + k // 2)
                panel_lo(l, PN_FFN)
                norm(l, 1, M_SH2, R_N2)
                panel_lo(l, PN_FFN + 1)

                def hidden(t, following):
                    for j in range(2):
                        n = 2 * t + j
                        wait(dve, fsig_set, l, n + 1)
                        v.tensor_tensor(tn[:, j, :], tn[:, j, :], bank[j][:, :], ALU.mult).then_inc(silu_set.sem, 1)
                    following(0)
                    for j in range(2):
                        n = 2 * t + j
                        wait(dve, up_done, l, n + 1)
                        wait(dve, silu_set, l, n + 1)
                        v.tensor_tensor(sq[:, j, :], tn[:, j, :], bank[2 + j][:, :], ALU.mult).then_inc(act_set.sem, 1)
                    for j in range(2):
                        n = 2 * t + j
                        wait(dve, a_hi_set, l, n + 1)
                        v.tensor_tensor(a_lo[:, bass.ds(n, 1), :], sq[:, j, :], a_hi[:, bass.ds(n, 1), :].bitcast(F32),
                                        ALU.subtract).then_inc(a_lo_set.sem, 1)
                    following(1)

                with dve.Fori(0, KF // 2 - 1) as t:
                    hidden(t, pair_at(PN_FFN + 2 + 2 * t))
                hidden(KF // 2 - 1, pair_at(PN_DOWN))

                for gr in range(4):
                    for q in range(3):
                        p = PN_DOWN + 2 + 3 * gr + q
                        if p < PANELS:
                            panel_lo(l, p)
                    for j in range(2):
                        k = 2 * gr + j
                        wait(dve, down_done, l, k + 1)
                        update_x(l, KD + k, k, M_G2, bank[k % 4])

            for n in range(0, 2 * NT, 2):
                dve.wait_ge(y_transposed, n + 1)
                v.tensor_copy(xout[:, n // 2, 0:S], tr[:, 0, :]).then_inc(xout_left, 1)

        @block.gpsimd
        def _(pool):
            pool.dma_start(bucket_sb[:, :], buckets).then_inc(buckets_in, 16)
            pool.dma_start(rel_sb[0:REL_BUCKETS, :], rel_bias).then_inc(buckets_in, 16)
            pool.dma_start(pos_i[:, :], positions.partition_broadcast(P)).then_inc(pos_in, 16)
            for i in range(NT):
                pool.dma_start(xnat[:, i, :], x[0, i * P:(i + 1) * P, :]).then_inc(x_in, 16)
            pool.memset(rel_sb[REL_BUCKETS:REL_BUCKETS + 1, :], 1.0).then_inc(rel_ones, 1)

            def add_square(k):
                first = sq[:, 0, :] if k == 1 else sumsq[:, :]
                nc.gpsimd.tensor_tensor(sumsq[:, :], first, sq[:, k % 2, :], ALU.add).then_inc(sum_done.sem, 1)

            for k in range(1, KD - 1):
                pool.wait_ge(sq_set.sem, k + 1)
                if k >= 2:
                    pool.wait_ge(sum_done.sem, k - 1)
                add_square(k)
            pool.wait_ge(btab_set, 2)
            pool.dma_start(bias_row, btab[:, :]).then_inc(bias_row_out, 16)
            pool.wait_ge(bias_row_out, 16)
            pool.wait_ge(ada0_in[3], 16)
            pool.dma_start(bias_scratch, bias_row.rearrange("h (o n) -> h o n", o=1).broadcast_to([HEADS, P, 2 * S]))\
                .then_inc(bias_out, 16)

            with pool.Fori(0, DEPTH) as l:
                wait(pool, rot_set, l, 1)
                for h in range(HEADS):
                    i = h % 2
                    wait(pool, head_r, l, h + 1)
                    nc.gpsimd.tensor_tensor(qk[64:128, h, 1, :], k_rot[64:128, :], r_qk[64:128, i, 1, :], ALU.mult)\
                        .then_inc(k_set.sem, 1)
                    wait(pool, k_scaled, l, h + 1)
                    nc.gpsimd.tensor_tensor(qk[0:NOPE, h, 1, :], qk[0:NOPE, h, 1, :], r_qk[0:NOPE, i, 1, :], ALU.mult)\
                        .then_inc(kr_set.sem, 1)
                for p in POOLED:
                    for c in range(2):
                        r = load_of("panel", p, c)
                        wait(pool, hi_set, l, 2 * p + c + 1)
                        nc.gpsimd.tensor_tensor(w_lo[p % 2][:, c * CHUNK:(c + 1) * CHUNK], raw[r % RAW][:, :],
                                                w_hi[p % 2][:, c * CHUNK:(c + 1) * CHUNK].bitcast(F32),
                                                ALU.subtract).then_inc(pool_lo_set.sem, 1)
                for n in range(2):
                    wait(pool, norm_ss, l, n + 1)
                    if n == 0:
                        wait(pool, dss_done, l, HEADS)
                    for k in range(1, KD - 1):
                        wait(pool, sq_set, l, KD * n + k + 1)
                        if k >= 2:
                            wait(pool, sum_done, l, ADDS * n + k - 1)
                        add_square(k)

        @block.tensor
        def _(pe):
            def product(out_, w, w_cols, rhs_hi, rhs_lo, start, stop):
                whi, wlo = w_hi[w][:, w_cols], w_lo[w][:, w_cols]
                pe_.matmul(out_, whi, rhs_hi, start=start, stop=False)
                pe_.matmul(out_, wlo, rhs_hi, start=False, stop=False)
                return pe_.matmul(out_, whi, rhs_lo, start=False, stop=stop)

            def cols(k, at, wid=PC, n=P):
                return slice(k * wid + at, k * wid + at + n)

            def tile_product(out_, w, at, hi, lo, k0=0, k1=KD, kn=KD, wid=PC, base=0, w_k0=0):
                for k in range(k0, k1):
                    last = product(out_, w, slice(base + (k - w_k0) * wid + at, base + (k - w_k0) * wid + at + P),
                                   hi[:, k, :], lo[:, k, :], k == 0, k == kn - 1)
                return last

            def split_ready(l, p):
                ev, n = low_done(p, 1)
                wait(pe, ev, l, n)

            def norm_sum(l, n):
                wait(pe, sum_done, l, ADDS * n)
                pe_.matmul(ss[:, :], ones[:, :], sumsq[:, :], start=True, stop=False)
                wait(pe, sq_set, l, KD * n)
                pe_.matmul(ss[:, :], ones[:, :], sq[:, 1, :], start=False, stop=True).then_inc(norm_ss.sem, 1)

            pe.wait_ge(consts_in, 16)
            pe.wait_ge(buckets_in, 32)
            pe.wait_ge(ones_set, 3)
            pe.wait_ge(rel_ones, 1)
            pe.wait_ge(rows_in, 16 * 17)
            for l in range(DEPTH):
                pe_.transpose(tr[:, l, 0:ROWS], rows[:, l, :], ident[0:ROWS, 0:ROWS]).then_inc(prm_done, 1)
            for i in range(2):
                pe_.matmul(bank[i][0:HEADS, :], rel_sb[:, :], bucket_sb[:, i * S:(i + 1) * S], start=True, stop=True)\
                    .then_inc(bias_done, 1)
            pe.wait_ge(x_in, 16 * NT)
            for k in range(KD):
                if k >= 2:
                    pe.wait_ge(x_set, k - 1)
                for i in range(NT):
                    last = pe_.transpose(bank[2 + k % 2][:, i * P:(i + 1) * P], xnat[:, i, k * P:(k + 1) * P], ident)
                last.then_inc(x_transposed, 1)
            for u in range(4):
                pe.wait_ge(ada0_step, KD * (u + 1))
                for j in range(4):
                    last = pe_.matmul(pv[:, 4 * u + j:4 * u + j + 1], ada0[:, u, 0, j * P:(j + 1) * P], ones[:, 0:1],
                                      start=True, stop=True)
            last.then_inc(ada0_reduced, 1)
            pe.wait_ge(mods0_set, 1)

            with pe.Fori(0, DEPTH) as l:
                norm_sum(l, 0)

                split_ready(l, 0)
                split_ready(l, 1)
                for k in range(KD):
                    wait(pe, h_lo_set, l, k + 1)
                    for j, (w, at) in enumerate(((0, 0), (0, P), (1, 0), (1, P))):
                        last = product(bank[j][:, :], w, cols(k, at), h_hi[:, k, :], h_lo[:, k, :], k == 0, k == KD - 1)
                        if k == KD - 1 and at:
                            last.then_inc(lat_done.sem, 1)

                def dilated_v(half):
                    split_ready(l, PN_DV + half)
                    for i in range(NT):
                        n = NT * half + i
                        if n >= 2:
                            wait(pe, v_set, l, n - 1)
                        tok = slice(i * P, (i + 1) * P)
                        for k in range(KD):
                            o, hh, hl = tr[:, i % 2, 0:PC], h_hi[:, k, tok], h_lo[:, k, tok]
                            whi, wlo = w_hi[half][:, k * PC:(k + 1) * PC], w_lo[half][:, k * PC:(k + 1) * PC]
                            pe_.matmul(o, hh, whi, start=k == 0, stop=False)
                            pe_.matmul(o, hh, wlo, start=False, stop=False)
                            last = pe_.matmul(o, hl, whi, start=False, stop=k == KD - 1)
                        last.then_inc(vd_done.sem, 1)

                dilated_v(0)
                wait(pe, lat_sq, l, 5)
                pe_.matmul(ss[:, :], ones[:, :], probT[:, 0, :], start=True, stop=False)
                pe_.matmul(ss[:, :], ones[:, :], probT[:, 1, :], start=False, stop=True).then_inc(lat_ss.sem, 1)
                pe_.matmul(pv[:, :], ones[:, :], probT[:, 2, :], start=True, stop=True).then_inc(lat_ss.sem, 1)
                wait(pe, rot_parts, l, 1)
                pe_.matmul(s1[:, :], pair_sum, k_rot[64:128, :], start=True, stop=True).then_inc(rot_sum.sem, 1)
                dilated_v(1)

                split_ready(l, PN_WKVB)
                wait(pe, lat_lo, l, 3)

                def heads_of(w):
                    return w[:, 0:HEADS * P].rearrange("p (h n) -> p h n", h=HEADS)[:, :, NOPE:P]

                for i, bank_ in enumerate((ss, pv, ss, pv)):
                    if i >= 2:
                        wait(pe, v_set, l, 2 * NT + i - 1)
                    tok = slice(i * P, (i + 1) * P)
                    acc = bank_[:, :].rearrange("p (h n) -> p h n", h=HEADS)
                    pe_.matmul(acc, kvc_hi[:, tok], heads_of(w_hi[1]), start=True, stop=False)
                    pe_.matmul(acc, kvc_hi[:, tok], heads_of(w_lo[1]), start=False, stop=False)
                    pe_.matmul(acc, kvc_lo[:, tok], heads_of(w_hi[1]), start=False, stop=True)\
                        .then_inc(vm_done.sem, 1)

                split_ready(l, PN_WQB)

                def head_sums(h):
                    i = h % 2
                    wait(pe, head_sq, l, 2 * h + 2)
                    if h:
                        wait(pe, head_ln, l, h)
                    pe_.matmul(tr[:, 0, :], ones[0:QK, :], sq_qk[0:QK, i, 0, :], start=True, stop=True)
                    pe_.matmul(tr[:, 1, :], ones[0:QK, :], sq_qk[0:QK, i, 1, :], start=True, stop=True)\
                        .then_inc(head_ss.sem, 1)

                for h in range(HEADS):
                    i = h % 2
                    if h >= 2:
                        wait(pe, q_scaled, l, h - 1)
                        wait(pe, k_scaled, l, h - 1)
                    tile_product(bank[2 + i][:, :], 0, h * P, qc_hi, qc_lo, 0, 2, 2, HEADS * P).then_inc(q_done.sem, 1)
                    if h == 0:
                        wait(pe, rot_set, l, 1)
                    product(bank[i][:, :], 1, slice(h * P, (h + 1) * P), kvc_hi[:, :], kvc_lo[:, :], True, True)\
                        .then_inc(k_done.sem, 1)
                    if h:
                        head_sums(h - 1)
                head_sums(HEADS - 1)

                def scores(g, i):
                    n = NT * g + i
                    if g < HEADS:
                        if n == 0:
                            wait(pe, q_set, l, HEADS)
                            wait(pe, k_set, l, HEADS)
                            wait(pe, kr_set, l, HEADS)
                        q, k = qk[:, g, 0, i * P:(i + 1) * P], qk[:, g, 1, :]
                    else:
                        head = g - HEADS
                        half = slice(DH * (head % 2), DH * (head % 2) + DH)
                        if i == 0:
                            wait(pe, dqk_set, l, 5 + head // 2)
                        q, k = dqk[half, head // 2, i * P:(i + 1) * P], dqk[half, 4 + head // 2, :]
                    if n >= 2:
                        if n - 2 < NT * HEADS:
                            wait(pe, exp_set, l, n - 1)
                        else:
                            wait(pe, biased, l, n - 1 - NT * HEADS)
                    pe_.matmul(bank[2 + n % 2][:, :], q, k, start=True, stop=True).then_inc(scored.sem, 1)

                def transposes(g, i):
                    n = NT * g + i
                    wait(pe, prob_set, l, n + 1)
                    if n >= 2:
                        wait(pe, probT_set, l, n - 1)
                    for j in range(NT):
                        last = pe_.transpose(tr[:, n % 2, j * P:(j + 1) * P], prob[:, n % 2, j * P:(j + 1) * P], ident)
                    last.then_inc(transposed.sem, 1)

                def attend(g):
                    wait(pe, probT_set, l, NT * g + NT)
                    head = g % HEADS
                    vals = v_mla if g < HEADS else v_dil
                    if g >= 2 and g % 2 == 0:
                        wait(pe, y_lo_set, l, g // 2)
                    half = slice(DH * (head % 2), DH * (head % 2) + DH)
                    for j in range(NT):
                        last = pe_.matmul(pv[half, :], vals[:, j, head * DH:(head + 1) * DH], probT[:, j, :],
                                          start=j == 0, stop=j == NT - 1)
                    last.then_inc(pv_done.sem, 1)

                def projection(g, k0, k1):
                    p = PN_DQK + g // 2
                    if k0 == 0:
                        split_ready(l, p)
                        if g >= 2:
                            if g - 2 < HEADS:
                                wait(pe, dqk_set, l, g - 1)
                            else:
                                wait(pe, ga_set, l, g - 1 - HEADS)
                    last = tile_product(bank[g % 2][:, :], p % 2, g % 2 * P, h_hi, h_lo, k0, k1)
                    if k1 == KD:
                        last.then_inc(proj_done.sem, 1)

                def dilated_sums(t):
                    wait(pe, dsq_set, l, t + 1)
                    wait(pe, mods_set, l, t + 1)
                    pe_.matmul(ss[:, :], block_ones, sumsq[:, :], start=True, stop=True).then_inc(dss_done.sem, 1)

                def ada_reduce(g):
                    u, _, k1 = ada_part(g)
                    if k1 != KD:
                        return
                    wait(pe, ada_step, l, KD * (u + 1))
                    if g and g <= HEADS:
                        wait(pe, dln_set, l, g)
                    if u:
                        wait(pe, mods_set, l, u)
                    for j in range(4):
                        last = pe_.matmul(ss[:, j:j + 1], ada_acc[:, j * P:(j + 1) * P], ones[:, 0:1],
                                          start=True, stop=True)
                    last.then_inc(ada_reduced.sem, 1)

                for g in range(STEPS):
                    scores(g, 0)
                    scores(g, 1)
                    if g:
                        attend(g - 1)
                    if 1 <= g <= HEADS:
                        dilated_sums(g - 1)
                    transposes(g, 0)
                    scores(g, 2)
                    transposes(g, 1)
                    scores(g, 3)
                    projection(g, 0, KD)
                    transposes(g, 2)
                    transposes(g, 3)
                    ada_reduce(g)
                attend(STEPS - 1)

                def branch(i):
                    split_ready(l, PN_GB + 2 * i)
                    if isinstance(i, int):
                        wait(pe, ga_set, l, HEADS)
                    else:
                        wait(pe, sigb_set, l, 2 * i)
                    for j in range(2):
                        last = tile_product(bank[j][:, :], 0, j * P, h_hi, h_lo)
                        last.then_inc(gb_done.sem, 1)
                    split_ready(l, PN_GB + 1 + 2 * i)
                    if isinstance(i, int):
                        wait(pe, y_lo_set, l, STEPS // 2)
                    else:
                        wait(pe, mix_b, l, 2 * i)
                    for j in range(2):
                        acc_a, acc_b = (bank[2][:, :], bank[3][:, :]) if j == 0 else (tr[:, 0, :], tr[:, 1, :])
                        tile_product(acc_a, 1, j * P, ya_hi, ya_lo, 0, 4, 4).then_inc(br_done.sem, 1)
                        last = tile_product(acc_b, 1, j * P, yb_hi, yb_lo, 0, 4, 4, base=PANEL // 2)
                        last.then_inc(br_done.sem, 1)

                branch(0)
                with pe.Fori(1, 4) as i:
                    branch(i)

                wait(pe, m_lo_set, l, KD)
                for n in range(KD):
                    p = PN_OUT + n // 2
                    split_ready(l, p)
                    if n >= 4:
                        wait(pe, x_updated, l, n - 3)
                    last = tile_product(bank[n % 4][:, :], p % 2, n % 2 * P, m_hi, m_lo)
                    last.then_inc(out_done.sem, 1)
                norm_sum(l, 1)

                def hidden(t):
                    split_ready(l, PN_FFN + 2 * t)
                    wait(pe, silu_set, l, 2 * t)
                    for j in range(2):
                        last = tile_product(bank[j][:, :], 0, j * P, h_hi, h_lo)
                        last.then_inc(gate_done.sem, 1)
                    split_ready(l, PN_FFN + 1 + 2 * t)
                    wait(pe, act_set, l, 2 * t)
                    for j in range(2):
                        last = tile_product(bank[2 + j][:, :], 1, j * P, h_hi, h_lo)
                        last.then_inc(up_done.sem, 1)

                split_ready(l, PN_FFN)
                for k in range(KD):
                    wait(pe, h_lo_set, l, KD + k + 1)
                    for j in range(2):
                        last = product(bank[j][:, :], 0, cols(k, j * P), h_hi[:, k, :], h_lo[:, k, :], k == 0, k == KD - 1)
                        if k == KD - 1:
                            last.then_inc(gate_done.sem, 1)
                split_ready(l, PN_FFN + 1)
                for j in range(2):
                    tile_product(bank[2 + j][:, :], 1, j * P, h_hi, h_lo).then_inc(up_done.sem, 1)
                with pe.Fori(1, KF // 2) as t:
                    hidden(t)

                for gr in range(4):
                    for q in range(3):
                        p = PN_DOWN + 3 * gr + q
                        split_ready(l, p)
                        if q == 0:
                            wait(pe, a_lo_set, l, KF)
                            if gr >= 2:
                                wait(pe, x_updated, l, KD + 2 * gr - 2)
                        k0, k1 = 8 * q, min(8 * q + 8, KF)
                        for j in range(2):
                            last = tile_product(bank[(2 * gr + j) % 4][:, :], p % 2, j * P, a_hi, a_lo, k0, k1, KF, w_k0=k0)
                            if q == 2:
                                last.then_inc(down_done.sem, 1)
                        if q < 2:
                            last.then_inc(down_part.sem, 1)

            pe.wait_ge(x_updated.sem, 2 * KD * DEPTH)
            for n in range(2 * NT):
                i, half = n // 2, n % 2
                if n >= 2:
                    pe.wait_ge(xout_right if half else xout_left, i)
                for k in range(4):
                    last = pe_.transpose(tr[:, half, k * P:(k + 1) * P], xT[:, 4 * half + k, i * P:(i + 1) * P], ident)
                last.then_inc(y_transposed, 1)


_INS = ["x", "c", "positions", "rel_bias", "norm1_g", "norm2_g", "ada_w", "ada_b", "w_in", "q_a_norm", "w_q_b",
        "kv_a_norm", "w_kv_b", "q_norm_a", "k_norm_a", "q_norm_b", "k_norm_b", "w_branch_a", "w_branch_b",
        "w_out", "w_ffn_gate", "w_ffn_up", "w_ffn_down"]


def shape_constants():
    cst = np.zeros((P, 3 * P + 4), np.float32)
    cst[:, 0:P] = np.eye(P)
    cst[:, P:2 * P] = np.kron(np.eye(2), np.ones((DH, DH)))
    cst[64:128, 2 * P:3 * P] = np.kron(np.ones((2, 4)), np.eye(ROPE))
    inv = (ROPE_THETA ** (-np.arange(HALF) / HALF)).astype(np.float32)
    rope = cst[:, 3 * P:]
    rope[:, 3] = 1.0
    rope[64:96, 0] = rope[96:128, 0] = np.tile(inv, 2)
    rope[64:96, 1] = 0.25
    rope[64:96, 2] = math.pi / 2
    rope[96:96 + HALF, 3] = -1.0

    rel = np.arange(-(S - 1), S + 1)
    n = np.abs(rel)
    half = REL_BUCKETS // 2
    exact = half // 2
    large = exact + (np.log(np.maximum(n, 1).astype(np.float32) / np.float32(exact))
                     / np.float32(math.log(REL_MAX_DIST / exact)) * (half - exact)).astype(np.int32)
    bucket = np.where(rel > 0, half, 0) + np.where(n < exact, n, np.minimum(large, half - 1))
    count = sum(((n % dil == 0) & (n <= window // 2)).astype(np.int64) for window, dil in PATTERNS)
    table = np.zeros((REL_BUCKETS + 1, 2 * S), np.float32)
    table[bucket, np.arange(2 * S)] = 1.0
    table[REL_BUCKETS] = np.where(count > 0, np.log(np.maximum(count, 1)), NEG_INF)
    return cst, table


def kernel(**inputs):
    import concourse.bacc as bacc
    from concourse.bass_utils import run_bass_kernel_spmd

    nc = bacc.Bacc("TRN2", target_bir_lowering=False, num_devices=1)
    arrays = {name: np.ascontiguousarray(inputs[name]) for name in _INS}
    arrays["consts"], arrays["buckets"] = shape_constants()
    args = [nc.dram_tensor(f"in_{n}", a.shape, mybir.dt.from_np(a.dtype), kind="ExternalInput").ap()
            for n, a in arrays.items()]
    out = nc.dram_tensor("out", (1, S, D), F32, kind="ExternalOutput").ap()
    encoder_trunk(nc, *args, out)
    result = run_bass_kernel_spmd(nc, [{f"in_{n}": a for n, a in arrays.items()}], core_ids=[0])
    return result.results[0]["out"]
```

```python
import math
from contextlib import ExitStack

import numpy as np

import concourse.bass as bass
from concourse import mybir

F32 = mybir.dt.float32
F32R = mybir.dt.float32r
I32 = mybir.dt.int32
ALU = mybir.AluOpType
ACT = mybir.ActivationFunctionType
AX = mybir.AxisListType

P = 128
D = 1024
S = 512
DEPTH = 2
KD = D // P
NT = S // P
HEADS = 8
Q_LORA, KV_LORA, ROPE, NOPE, VDIM = 256, 128, 32, 64, 64
QK = NOPE + ROPE
HALF = ROPE // 2
DH = 64
FFN = 2816
KF = FFN // P
EPS = 1e-6
NEG_INF = -1e30
PATTERNS = ((128, 1), (512, 4), (2048, 16))
REL_BUCKETS, REL_MAX_DIST = 32, 1024
ROPE_THETA = 10000.0
IN_COLS = Q_LORA + KV_LORA + ROPE + 3 * HEADS * DH + 2 * D
COL_KV = Q_LORA
COL_DIL = COL_KV + KV_LORA + ROPE
COL_DV = COL_DIL + 2 * HEADS * DH
COL_GA = COL_DIL + 3 * HEADS * DH
COL_GB = COL_GA + D
PANEL = 2048
PC = PANEL // KD
TW = 2 * S - P

R_ADAB, R_N1, R_N2, R_QA, R_KVA, R_QNA, R_KNA, R_QNB, R_KNB = 0, 48, 56, 64, 66, 67, 68, 69, 70
ROWS = R_KNB + 1
M_SH1, M_SC1, M_G1, M_SH2, M_SC2, M_G2 = (KD * i for i in range(6))

PN_QC, PN_KV, PN_DV, PN_WQB, PN_WKVB, PN_DQK = 0, 1, 2, 4, 5, 6
PN_GA = PN_DQK + 4
PN_GB = PN_GA + 4
PN_OUT = PN_GB + 8
PN_FFN = PN_OUT + 4
PN_DOWN = PN_FFN + KF
PANELS = PN_DOWN + 12
ADA_UNITS = 12
STEPS = 2 * HEADS
CHUNK = PANEL // 2
RAW = 4


def ada_part(g):
    if g < HEADS:
        return g, 0, KD
    return HEADS + (g - HEADS) // 2, KD // 2 * (g % 2), KD // 2 * (g % 2 + 1)


def step_panel(g):
    return PN_DQK + 1 + g // 2


def load_order():
    order = [("panel", p, c) for p in range(PN_DQK + 1) for c in range(2)]
    for g in range(STEPS):
        u, k0, k1 = ada_part(g)
        step = [("ada", u, j) for j in range(k0 // 2, k1 // 2)]
        step.insert(0 if g % 2 else len(step), ("panel", step_panel(g), g % 2))
        order += step
    return order + [("panel", PN_GB + 1, c) for c in range(2)]


LOAD_ORDER = load_order()
LOADS = len(LOAD_ORDER) + 2 * (PANELS - PN_GB - 2)
LATE = (len(LOAD_ORDER) - 2 * (PN_GB + 2)) // RAW
assert len(LOAD_ORDER) % RAW == 0 and LOADS % RAW == 0 and PN_GB % 2 == 0


def load_of(kind, n, c):
    return LOAD_ORDER.index((kind, n, c))


class Event:

    def __init__(self, sem, per_layer, credit=0):
        self.sem, self.per_layer, self.credit = sem, per_layer, credit

    def at(self, layer, n):
        return layer * self.per_layer + (n + self.credit)


def encoder_trunk(nc, x, cond, positions, rel_bias, norm1_g, norm2_g, ada_w, ada_b, w_in, q_a_norm, w_q_b,
                  kv_a_norm, w_kv_b, q_norm_a, k_norm_a, q_norm_b, k_norm_b, w_branch_a, w_branch_b,
                  w_out, w_ffn_gate, w_ffn_up, w_ffn_down, consts, buckets, out):
    bias_row = nc.dram_tensor("bias_row", (HEADS, 2 * S), F32).ap()
    bias_scratch = nc.dram_tensor("bias_scratch", (HEADS, P, 2 * S), F32).ap()

    with ExitStack() as ctx:
        def sb(name, shape, dt=F32, within=ctx):
            return within.enter_context(nc.sbuf_tensor(name, shape, dt))

        def sem(name):
            return ctx.enter_context(nc.semaphore(name))

        def event(name, per_layer, credit=0):
            return Event(sem(name), per_layer, credit)

        xT = sb("xT", [P, KD, S])
        h_hi = sb("h_hi", [P, KD, S], F32R)
        h_lo = sb("h_lo", [P, KD, S], F32R)
        raw = [sb(f"raw{i}", [P, CHUNK]) for i in range(RAW)]
        w_hi = [sb(f"w_hi{i}", [P, PANEL], F32R) for i in range(2)]
        w_lo = [sb(f"w_lo{i}", [P, PANEL], F32R) for i in range(2)]
        sumsq = sb("sumsq", [P, S])
        rstd = sb("rstd", [P, S])
        trig = sb("trig", [P, S])
        cst = sb("cst", [P, 3 * P + 4])
        ones = sb("ones", [P, P])
        prm = sb("prm", [P, DEPTH, ROWS])
        prl = sb("prl", [P, ROWS])
        mods = sb("mods", [P, 6 * KD])
        g_norm = sb("g_norm", [P, KD])
        silu_c = sb("silu_c", [P, KD])
        eps_col = sb("eps_col", [P, 1])
        spare = sb("spare", [P, 4])
        nmax = sb("nmax", [P, NT])
        den = sb("den", [P, NT])
        rden = sb("rden", [P, NT])
        ident = cst[:, 0:P]
        block_ones = cst[:, P:2 * P]
        pair_sum = cst[64:128, 2 * P:3 * P]
        rope_inv, rope_phase, rope_arg, rope_sign = (cst[:, 3 * P + i:3 * P + i + 1] for i in range(4))

        def layout(*buffers):
            made = []
            with ExitStack() as scope:
                for name, shape, dt in buffers:
                    made.append(sb(name, shape, dt, scope))
            return made

        KB = 256
        (qk, dqk, v_mla, v_dil, ya_hi, ya_lo, prob, probT, toep, _, ada_acc) = layout(
            ("qk", [P, HEADS, 2, S], F32),
            ("dqk", [P, KD, S], F32),
            ("v_mla", [P, NT, HEADS * VDIM], F32), ("v_dil", [P, NT, HEADS * DH], F32),
            ("ya_hi", [P, 4, S], F32R), ("ya_lo", [P, 4, S], F32R),
            ("prob", [P, 2, S], F32), ("probT", [P, NT, S], F32),
            ("toep", [P, 2, TW], F32), ("over_first_hi", [P, KB], F32), ("ada_acc", [P, S], F32))
        qk_r, dqk_r, _, first_hi = layout(
            ("qk_r", [P, HEADS, 2, S], F32R), ("dqk_r", [P, KD, S], F32R), ("over_v_ya_prob", [P, 44 * KB], F32),
            ("first_hi", [P, 2, 2, S], F32R))
        (yb_hi, yb_lo, gate_a, m_hi, m_lo, _, sig_a, sig_b, mix) = layout(
            ("yb_hi", [P, 4, S], F32R), ("yb_lo", [P, 4, S], F32R), ("gate_a", [P, KD, S], F32),
            ("m_hi", [P, KD, S], F32R), ("m_lo", [P, KD, S], F32R), ("over_ya", [P, 16 * KB], F32),
            ("sig_a", [P, 2, S], F32), ("sig_b", [P, 2, S], F32), ("mix", [P, 2, S], F32))
        (_, sq_qk, r_qk, _, qc_hi, qc_lo, kvc_hi, kvc_lo, k_rot, q_gain) = layout(
            ("over_qk", [P, 32 * KB], F32), ("sq_qk", [P, 2, 2, S], F32), ("r_qk", [P, 2, 2, S], F32),
            ("over_v", [P, 16 * KB], F32),
            ("qc_hi", [P, 2, S], F32R), ("qc_lo", [P, 2, S], F32R),
            ("kvc_hi", [P, S], F32R), ("kvc_lo", [P, S], F32R), ("k_rot", [P, S], F32), ("q_gain", [P, S], F32))
        (a_hi, a_lo, tn, sq) = layout(
            ("a_hi", [P, KF, S], F32R), ("a_lo", [P, KF, S], F32R), ("tn", [P, 2, S], F32), ("sq", [P, 2, S], F32))
        (ada0, xnat, rows, pos_i, angle, turns, bucket_sb, rel_sb, c_rows, _, btab) = layout(
            ("ada0", [P, 4, KD, S], F32), ("xnat", [P, NT, D], F32), ("rows", [ROWS, DEPTH, P], F32),
            ("pos_i", [P, S], I32), ("angle", [P, S], F32), ("turns", [P, S], F32),
            ("bucket_sb", [REL_BUCKETS + 1, 2 * S], F32), ("rel_sb", [REL_BUCKETS + 1, HEADS], F32),
            ("c_rows", [KD, P], F32), ("gap", [P, 5 * KB - HEADS - P], F32), ("btab", [HEADS, 2 * S], F32))
        (xout,) = layout(("xout", [P, NT, D], F32))
        sb("region", [P, 102 * KB])

        bank = [ctx.enter_context(nc.psum_tensor(f"bank{i}", [P, S], F32)) for i in range(4)]
        tr = ctx.enter_context(nc.psum_tensor("tr", [P, 2, S], F32))
        acc = ctx.enter_context(nc.psum_tensor("acc", [P, 2, S], F32))
        pv, ss = acc[:, 0, :], acc[:, 1, :]
        b0, b1, s0, s1 = bank

        consts_in, buckets_in, rows_in, c_in, c_transposed, pos_in, x_in, ones_set, rel_ones = (
            sem(n) for n in ("consts_in", "buckets_in", "rows_in", "c_in", "c_transposed", "pos_in", "x_in",
                             "ones_set", "rel_ones"))
        bias_row_out, bias_out = sem("bias_row_out"), sem("bias_out")
        ada0_in = [sem(f"ada0_in{n}") for n in range(8)]
        prm_done, prm_set, sig_c_set, c_set, ada0_step, ada0_reduced, mods0_set = (
            sem(n) for n in ("prm_done", "prm_set", "sig_c_set", "c_set", "ada0_step", "ada0_reduced", "mods0_set"))
        x_transposed, x_set, bias_done, btab_set, angle_step, sin_set, trig_set = (
            sem(n) for n in ("x_transposed", "x_set", "bias_done", "btab_set", "angle_step", "sin_set", "trig_set"))
        raw_in = [event(f"raw_in{i}", 16 * LOADS // RAW) for i in range(RAW)]
        hi_set = event("hi_set", 2 * PANELS)
        POOLED = [(PN_QC, 1), (PN_KV, 0), (PN_KV, 1)] + \
            [(p, c) for p in range(PN_DQK + 1, PN_GB + 1) for c in range(2)]
        lo_set = event("lo_set", 2 * PANELS - len(POOLED), credit=RAW)
        pool_lo_set = event("pool_lo_set", len(POOLED))

        def low_done(p, c):
            if isinstance(p, int) and (p, c) in POOLED:
                return pool_lo_set, POOLED.index((p, c)) + 1
            before = sum(chunk < (p, c) for chunk in POOLED) if isinstance(p, int) else len(POOLED)
            return lo_set, 2 * p + c + 1 - before

        x_updated = event("x_updated", 2 * KD)
        sq_set = event("sq_set", 2 * KD, credit=KD)
        ADDS = KD - 2
        sum_done = event("sum_done", 2 * ADDS, credit=ADDS)
        norm_ss = event("norm_ss", 2)
        norm_ln = event("norm_ln", 2)
        rstd_set = event("rstd_set", 2)
        norm_t = event("norm_t", 2 * KD)
        h_hi_set = event("h_hi_set", 2 * KD)
        h_lo_set = event("h_lo_set", 2 * KD)
        prl_set = event("prl_set", 1)
        qnb_scaled = event("qnb_scaled", 1)
        g_norm_set = event("g_norm_set", 2)
        lat_done = event("lat_done", 2)
        vd_done = event("vd_done", 2 * NT)
        vm_done = event("vm_done", NT)
        v_set = event("v_set", 3 * NT)
        lat_sq = event("lat_sq", 5)
        lat_ss = event("lat_ss", 2)
        lat_ln = event("lat_ln", 2)
        lat_r = event("lat_r", 2)
        lat_t = event("lat_t", 3)
        lat_hi = event("lat_hi", 3)
        lat_lo = event("lat_lo", 3)
        rot_parts = event("rot_parts", 1)
        rot_sum = event("rot_sum", 1)
        rot_set = event("rot_set", 1)
        q_gain_set = event("q_gain_set", 1)
        q_done = event("q_done", HEADS)
        k_done = event("k_done", HEADS)
        head_sq = event("head_sq", 2 * HEADS)
        head_ss = event("head_ss", HEADS)
        head_ln = event("head_ln", HEADS)
        head_r = event("head_r", HEADS)
        q_scaled = event("q_scaled", HEADS)
        q_set = event("q_set", HEADS)
        k_scaled = event("k_scaled", HEADS)
        k_set = event("k_set", HEADS)
        kr_set = event("kr_set", HEADS)
        split_hi = event("split_hi", 2 * HEADS + KD)
        split_lo = event("split_lo", 2 * HEADS + KD)
        scored = event("scored", NT * STEPS)
        biased = event("biased", NT * HEADS)
        max_set = event("max_set", NT * STEPS)
        exp_set = event("exp_set", NT * STEPS)
        rden_set = event("rden_set", NT * STEPS)
        prob_set = event("prob_set", NT * STEPS)
        transposed = event("transposed", NT * STEPS)
        probT_set = event("probT_set", NT * STEPS)
        pv_done = event("pv_done", STEPS)
        y_hi_set = event("y_hi_set", STEPS // 2)
        y_lo_set = event("y_lo_set", STEPS // 2)
        proj_done = event("proj_done", STEPS)
        dsq_set = event("dsq_set", HEADS)
        dss_done = event("dss_done", HEADS)
        dln_set = event("dln_set", HEADS)
        dr_set = event("dr_set", HEADS)
        dqk_set = event("dqk_set", HEADS)
        ga_set = event("ga_set", HEADS)
        toep_in = [event(f"toep_in{i}", 16 * HEADS // 2) for i in range(2)]
        ada_step = event("ada_step", KD * ADA_UNITS)
        ada_reduced = event("ada_reduced", ADA_UNITS)
        mods_set = event("mods_set", ADA_UNITS)
        gb_done = event("gb_done", KD)
        br_done = event("br_done", 2 * KD)
        siga_set = event("siga_set", KD)
        sigb_set = event("sigb_set", KD)
        mix_a = event("mix_a", KD)
        mix_b = event("mix_b", KD)
        mix_set = event("mix_set", KD)
        m_hi_set = event("m_hi_set", KD)
        m_lo_set = event("m_lo_set", KD)
        out_done = event("out_done", KD)
        gate_done = event("gate_done", KF)
        up_done = event("up_done", KF)
        fsig_set = event("fsig_set", KF)
        silu_set = event("silu_set", KF)
        act_set = event("act_set", KF)
        a_hi_set = event("a_hi_set", KF)
        a_lo_set = event("a_lo_set", KF)
        down_part = event("down_part", KD, credit=1)
        down_done = event("down_done", KD, credit=1)
        y_transposed, xout_left, xout_right, stored = (
            sem(n) for n in ("y_transposed", "xout_left", "xout_right", "stored"))

        block = ctx.enter_context(nc.Block())
        v = nc.vector
        a = nc.scalar
        pe_ = nc.tensor

        def wait(eng, ev, layer, n):
            eng.wait_ge(ev.sem, ev.at(layer, n))

        def score_parts(m, j):
            if m < HEADS:
                high = first_hi[:, m, j, :] if m < 2 else qk_r[:, m - 2, j, :]
                return qk[:, m, j, :], high, qk_r[:, m, j, :]
            t = m - HEADS
            high = qk_r[:, HEADS - 2 + t, j, :] if t < 2 else dqk_r[:, t - 2 + 4 * j, :]
            return dqk[:, t + 4 * j, :], high, dqk_r[:, t + 4 * j, :]

        def next_split(g):
            if g < HEADS - 1:
                return g + 1
            return HEADS + (g + 1 - HEADS) // 2 if g % 2 and g < STEPS - 1 else None

        @block.sync
        def _(sp):
            def first_modulation(u):
                for half in range(2):
                    rows_of = ada_w[0, half * D // 2:(half + 1) * D // 2, u * S:(u + 1) * S]
                    sp.dma_start(ada0[:, u, half * 4:half * 4 + 4, :], rows_of.rearrange("(k p) n -> p k n", p=P))\
                        .then_inc(ada0_in[2 * u + half], 16)

            sp.dma_start(c_rows[:, :], cond.rearrange("o (k p) -> (o k) p", p=P)).then_inc(c_in, 16)
            sp.dma_start(cst[:, :], consts).then_inc(consts_in, 16)
            first_modulation(0)
            for i in range(NT):
                sp.dma_start(xnat[:, i, :], x[0, i * P:(i + 1) * P, :]).then_inc(x_in, 16)
            first_modulation(1)
            row_loads = [
                (R_ADAB, 6 * KD, ada_b.rearrange("l (r p) -> r l p", p=P)),
                (R_N1, KD, norm1_g.rearrange("l (r p) -> r l p", p=P)),
                (R_N2, KD, norm2_g.rearrange("l (r p) -> r l p", p=P)),
                (R_QA, 2, q_a_norm.rearrange("l (r p) -> r l p", p=P)),
                (R_KVA, 1, kv_a_norm.rearrange("l (r p) -> r l p", p=P))]
            for r, n, src in row_loads:
                sp.dma_start(rows[r:r + n, :, :], src).then_inc(rows_in, 16)
            for r, src in ((R_QNA, q_norm_a), (R_KNA, k_norm_a)):
                for at, frm, n in ((0, 0, QK), (QK, NOPE + HALF, HALF), (QK + HALF, NOPE, HALF)):
                    sp.dma_start(rows[r:r + 1, :, at:at + n], src[:, frm:frm + n].rearrange("(o l) n -> o l n", o=1))\
                        .then_inc(rows_in, 16)
            for r, src in ((R_QNB, q_norm_b), (R_KNB, k_norm_b)):
                for at in (0, DH):
                    sp.dma_start(rows[r:r + 1, :, at:at + DH], src.rearrange("(o l) n -> o l n", o=1))\
                        .then_inc(rows_in, 16)
            first_modulation(2)
            first_modulation(3)

            def columns(w, l, k0, k1, col, n=PC):
                return w[bass.ds(l, 1), k0 * P:k1 * P, bass.ds(col, n)].rearrange("o (k p) n -> p (o k) n", p=P)

            def load(l, slot, free, src, k):
                wait(sp, free[0], l, free[1])
                n = src.shape[-1]
                sp.dma_start(raw[slot][:, 0:k * n].rearrange("p (k n) -> p k n", k=k), src)\
                    .then_inc(raw_in[slot].sem, 16)

            def half_k(w, l, c, col, n=PC):
                return columns(w, l, 4 * c, 4 * c + 4, col, n), 4

            def early_panel(l, p, c):
                if p == PN_QC:
                    return half_k(w_in, l, c, 0)
                if p == PN_KV:
                    return half_k(w_in, l, c, COL_KV, KV_LORA + ROPE)
                if p in (PN_DV, PN_DV + 1):
                    return half_k(w_in, l, c, COL_DV + (p - PN_DV) * PC)
                if p == PN_WQB:
                    return columns(w_q_b, l, c, c + 1, 0, HEADS * QK), 1
                if p == PN_WKVB:
                    return columns(w_kv_b, l, 0, 1, c * HEADS * P // 2, HEADS * P // 2), 1
                if p < PN_GA:
                    return half_k(w_in, l, c, COL_DIL + (p - PN_DQK) * PC)
                if p < PN_GB:
                    return half_k(w_in, l, c, COL_GA + (p - PN_GA) * PC)
                if p == PN_GB:
                    return half_k(w_in, l, c, COL_GB)
                return branch_weights(l, c, 0)

            def branch_weights(l, c, i):
                return columns((w_branch_a, w_branch_b)[c], l, 0, 4, i * PC), 4

            def ada_weights(l, u, j):
                layer = l if u < HEADS else DEPTH - 1
                return columns(ada_w, layer, 2 * j, 2 * j + 2, M_G1 * P + u * S if u < HEADS else (u - HEADS) * S, S), 2

            def late_slot(p, c):
                return 2 * (p % 2) + c

            with sp.Fori(0, DEPTH) as l:
                for r, (kind, n, c) in enumerate(LOAD_ORDER):
                    was, m, d = LOAD_ORDER[r - RAW] if r >= RAW else ("panel", -2 + r // 2, r % 2)
                    if was == "ada":
                        free = ada_step, KD * m + 2 * d + 2
                    else:
                        free = low_done(m, d) if m >= 0 else (lo_set, 2 * m + d + 1)
                    src, k = early_panel(l, n, c) if kind == "panel" else ada_weights(l, n, c)
                    load(l, r % RAW, free, src, k)
                with sp.Fori(1, 4) as i:
                    for j in range(2):
                        for c in range(2):
                            src, k = half_k(w_in, l, c, COL_GB + i * PC) if j == 0 else branch_weights(l, c, i)
                            if j == 0:
                                wait(sp, ada_step, l, KD * ADA_UNITS)
                            load(l, 2 * j + c, (lo_set, 2 * (PN_GB + j) + 4 * i - 4 + c + 1 - len(POOLED)), src, k)
                for i in range(4):
                    for c in range(2):
                        src, k = half_k(w_out, l, c, i * PC)
                        load(l, late_slot(i, c), low_done(PN_OUT + i - 2, c), src, k)
                with sp.Fori(0, KF // 2) as t:
                    for j, w in enumerate((w_ffn_gate, w_ffn_up)):
                        for c in range(2):
                            src, k = half_k(w, l, c, t * PC)
                            load(l, 2 * j + c, low_done(PN_FFN + 2 * t + j - 2, c), src, k)
                for gr in range(4):
                    for q in range(3):
                        p = PN_DOWN + 3 * gr + q
                        for c in range(2):
                            k0 = 8 * q + 4 * c
                            k1 = min(k0 + 4, KF)
                            src = columns(w_ffn_down, l, k0, k1, gr * PC)
                            load(l, late_slot(p, c), low_done(p - 2, c), src, k1 - k0)

            for i in range(NT):
                sp.wait_ge(xout_left, i + 1)
                sp.wait_ge(xout_right, i + 1)
                sp.dma_start(out[0, i * P:(i + 1) * P, :], xout[:, i, :]).then_inc(stored, 16)
            sp.wait_ge(stored, 16 * NT)

        def wait_raw(eng, layer, r):
            wait(eng, raw_in[r % RAW], layer, 16 * (r // RAW + 1))

        def pieces(kind, raw_slot, c, dst):
            src = raw[raw_slot]
            if kind in ("full", "six", "kv_b"):
                n = {"full": CHUNK, "six": CHUNK - c * 2 * PC, "kv_b": HEADS * P // 2}[kind]
                at = c * (n if kind == "kv_b" else CHUNK)
                return [(dst[:, at:at + n], src[:, 0:n])]
            if kind == "kv":
                k, wid, raw_wid = KD // 2, PC, KV_LORA + ROPE
                moves = [(0, 0, P), (P, 0, NOPE), (P + NOPE, KV_LORA, ROPE),
                         (P + QK, KV_LORA + HALF, HALF), (P + QK + HALF, KV_LORA, HALF)]
            else:
                k, wid, raw_wid = HEADS, P, QK
                moves = [(0, 0, QK), (QK, NOPE + HALF, HALF), (QK + HALF, NOPE, HALF)]
            frm = src[:, 0:k * raw_wid].rearrange("p (k n) -> p k n", k=k)
            to = dst[:, c * CHUNK:(c + 1) * CHUNK].rearrange("p (k n) -> p k n", k=k)
            return [(to[:, :, t:t + n], frm[:, :, f:f + n]) for t, f, n in moves]

        KINDS = {PN_KV: "kv", PN_WQB: "q_b", PN_WKVB: "kv_b"}
        KINDS.update({PN_DOWN + 3 * gr + 2: "six" for gr in range(4)})

        def panel_done(p):
            if p < 0:
                return (down_part if p == -2 else down_done), 0
            if p < PN_DV:
                return lat_done, p + 1
            if p < PN_WQB:
                return vd_done, NT * (p - PN_DV + 1)
            if p < PN_DQK:
                return (q_done if p == PN_WQB else k_done), HEADS
            if p < PN_GB:
                return proj_done, 2 * (p - PN_DQK + 1)
            if p < PN_OUT:
                i = (p - PN_GB) // 2
                return (br_done, 4 * i + 4) if (p - PN_GB) % 2 else (gb_done, 2 * i + 2)
            if p < PN_FFN:
                return out_done, 2 * (p - PN_OUT + 1)
            if p < PN_DOWN:
                return (up_done if (p - PN_FFN) % 2 else gate_done), 2 * ((p - PN_FFN) // 2) + 2
            gr, q = divmod(p - PN_DOWN, 3)
            return (down_done, 2 * gr + 2) if q == 2 else (down_part, 2 * gr + q + 1)

        @block.scalar
        def _(act):
            def hi_chunk(l, slot, c, raw_slot, landed, free=None, kind="full"):
                wait(act, raw_in[raw_slot], l, 16 * landed)
                if free:
                    wait(act, free[0], l, free[1])
                for to, frm in pieces(kind, raw_slot, c, w_hi[slot]):
                    last = a.activation(to, frm, ACT.Copy)
                last.then_inc(hi_set.sem, 1)

            def panel_hi(l, p, chunks=(0, 1)):
                for c in chunks:
                    r = load_of("panel", p, c) if p < PN_GB + 2 else 2 * p + c + RAW * LATE
                    hi_chunk(l, p % 2, c, r % RAW, r // RAW + 1, panel_done(p - 2) if c == 0 else None,
                             KINDS.get(p, "full"))

            def norm(l, n, shift, between):
                wait(act, norm_ss, l, n + 1)
                a.activation(rstd[:, :], ss[:, :], ACT.Ln, scale=1.0 / D, bias=eps_col[:, :]).then_inc(norm_ln.sem, 1)
                wait(act, norm_ln, l, n + 1)
                a.activation(rstd[:, :], rstd[:, :], ACT.Exp, scale=-0.5).then_inc(rstd_set.sem, 1)
                for k in range(KD):
                    wait(act, norm_t, l, KD * n + k + 1)
                    a.activation(h_hi[:, k, :], tn[:, k % 2, :], ACT.Identity, bias=mods[:, shift + k:shift + k + 1])\
                        .then_inc(h_hi_set.sem, 1)
                    between(k)

            def square_x(l, n, slot, x_tile):
                wait(act, x_updated, l, n + 1)
                k = n % KD
                if k >= 2:
                    wait(act, sum_done, l, ADDS * (n // KD) + max(1, k - 2))
                a.activation(sq[:, slot, :], x_tile, ACT.Square).then_inc(sq_set.sem, 1)

            def load_toeplitz(head):
                src = bass.AP(tensor=bias_scratch.tensor, offset=head * P * 2 * S + P - 1,
                              ap=[[2 * S - 1, P], [1, TW]])
                act.dma_start(toep[:, head % 2, :], src).then_inc(toep_in[head % 2].sem, 16)

            a.preload_act_table_set("sigmoid_and_others")
            act.wait_ge(c_transposed, 1)
            a.activation(rstd[:, 0:KD], pv[:, 0:KD], ACT.Sigmoid).then_inc(sig_c_set, 1)
            for k in range(KD):
                act.wait_ge(x_transposed, k + 1)
                a.activation(xT[:, k, :], bank[2 + k % 2][:, :], ACT.Copy).then_inc(x_set, 1)
                act.wait_ge(x_set, k + 1)
                if k >= 2:
                    act.wait_ge(sum_done.sem, max(1, k - 2))
                a.activation(sq[:, k % 2, :], xT[:, k, :], ACT.Square).then_inc(sq_set.sem, 1)
            for i in range(2):
                act.wait_ge(bias_done, i + 1)
                a.activation(btab[:, i * S:(i + 1) * S], bank[i][0:HEADS, :], ACT.Copy).then_inc(btab_set, 1)
            act.wait_ge(angle_step, 9)
            a.activation(trig[64:128, :], angle[64:128, :], ACT.Sin).then_inc(sin_set, 1)
            a.preload_act_table_set("natural_log_exp_and_others")
            act.wait_ge(sin_set, 1)
            a.activation(trig[64:128, :], trig[64:128, :], ACT.Copy, scale=rope_sign[64:128, :]).then_inc(sin_set, 1)

            with act.Fori(0, DEPTH) as l:
                panel_hi(l, PN_QC, (0,))
                following_norm = {0: (PN_QC, 1), 1: (PN_KV, 0), 3: (PN_KV, 1)}
                norm(l, 0, M_SH1, lambda k: panel_hi(l, following_norm[k][0], following_norm[k][1:])
                     if k in following_norm else None)

                wait(act, lat_done, l, 1)
                a.activation(probT[:, 0, :], b0[:, :], ACT.Square).then_inc(lat_sq.sem, 1)
                a.activation(probT[:, 1, :], b1[:, :], ACT.Square).then_inc(lat_sq.sem, 1)
                panel_hi(l, PN_DV)
                wait(act, lat_done, l, 2)
                a.activation(probT[:, 2, :], s0[:, :], ACT.Square).then_inc(lat_sq.sem, 1)
                for i in range(2):
                    a.activation(sq_qk[64:128, i, 1, :], s1[64:128, :], ACT.Square).then_inc(lat_sq.sem, 1)
                panel_hi(l, PN_DV + 1)

                def dilated_v(n):
                    half, i = divmod(n, NT)
                    wait(act, vd_done, l, n + 1)
                    a.activation(v_dil[:, i, half * PC:(half + 1) * PC], tr[:, i % 2, 0:PC], ACT.Copy)\
                        .then_inc(v_set.sem, 1)

                def latent_high(n):
                    wait(act, lat_t, l, n + 1)
                    to = qc_hi[:, n, :] if n < 2 else kvc_hi[:, :]
                    a.activation(to, prob[:, n % 2, :], ACT.Copy).then_inc(lat_hi.sem, 1)

                dilated_v(0)
                dilated_v(1)
                for n, (sums, size) in enumerate(((ss, Q_LORA), (pv, KV_LORA))):
                    wait(act, lat_ss, l, n + 1)
                    a.activation(r_qk[:, 0, n, :], sums[:, :], ACT.Ln, scale=1.0 / size, bias=eps_col[:, :])\
                        .then_inc(lat_ln.sem, 1)
                    wait(act, lat_ln, l, n + 1)
                    a.activation(r_qk[:, 0, n, :], r_qk[:, 0, n, :], ACT.Exp, scale=-0.5).then_inc(lat_r.sem, 1)
                latent_high(0)
                dilated_v(2)
                latent_high(1)
                latent_high(2)
                dilated_v(3)
                panel_hi(l, PN_WQB)
                for n in range(NT, 2 * NT):
                    dilated_v(n)
                panel_hi(l, PN_WKVB)
                act.wait_ge(bias_out, 16)

                for i, bank_ in enumerate((ss, pv, ss, pv)):
                    wait(act, vm_done, l, i + 1)
                    a.activation(v_mla[:, i, :], bank_[:, :], ACT.Copy).then_inc(v_set.sem, 1)

                def head_squares(h):
                    i = h % 2
                    wait(act, q_done, l, h + 1)
                    a.activation(sq_qk[0:QK, i, 0, :], bank[2 + i][0:QK, :], ACT.Square).then_inc(head_sq.sem, 1)
                    wait(act, k_done, l, h + 1)
                    a.activation(sq_qk[0:NOPE, i, 1, :], bank[i][0:NOPE, :], ACT.Square).then_inc(head_sq.sem, 1)

                def head_rms(h):
                    i = h % 2
                    wait(act, head_ss, l, h + 1)
                    if h >= 2:
                        wait(act, q_set, l, h - 1)
                        wait(act, kr_set, l, h - 1)
                    a.activation(r_qk[:, i, :, :], (tr, acc)[i][:, :, :], ACT.Ln, scale=1.0 / QK, bias=eps_col[:, :])\
                        .then_inc(head_ln.sem, 1)
                    wait(act, head_ln, l, h + 1)
                    a.activation(r_qk[:, i, :, :], r_qk[:, i, :, :], ACT.Exp, scale=-0.5).then_inc(head_r.sem, 1)

                def split_high(m, j):
                    if m >= HEADS:
                        wait(act, dqk_set, l, 5 + m - HEADS)
                    elif j == 0:
                        wait(act, q_set, l, m + 1)
                    else:
                        wait(act, k_set, l, m + 1)
                        wait(act, kr_set, l, m + 1)
                    whole, high, _ = score_parts(m, j)
                    a.activation(high, whole, ACT.Copy).then_inc(split_hi.sem, 1)

                wait(act, lat_lo, l, 3)
                head_squares(0)
                for h in range(1, HEADS):
                    head_squares(h)
                    if h == HEADS - 1:
                        panel_hi(l, PN_DQK)
                    head_rms(h - 1)
                    if h == 3:
                        split_high(0, 0)
                        split_high(0, 1)

                def probT_copy(n):
                    wait(act, transposed, l, n + 1)
                    g, i = divmod(n, NT)
                    if i == 0 and g:
                        wait(act, pv_done, l, g)
                    a.activation(probT[:, :, i * P:(i + 1) * P],
                                 tr[:, n % 2, :].rearrange("p (j q) -> p j q", j=NT), ACT.Copy)\
                        .then_inc(probT_set.sem, 1)

                def softmax_exp(n):
                    i = n % NT
                    wait(act, max_set, l, n + 1)
                    if n >= 2:
                        wait(act, transposed, l, n - 1)
                    scores = bank[2 + n % 2][:, :] if n < NT * HEADS else prob[:, n % 2, :]
                    a.activation(prob[:, n % 2, :], scores, ACT.Exp,
                                 bias=nmax[:, i:i + 1], accum_out=den[:, i:i + 1]).then_inc(exp_set.sem, 1)

                def y_high(pair):
                    wait(act, pv_done, l, 2 * pair + 2)
                    to = ya_hi[:, pair, :] if pair < 4 else yb_hi[:, pair - 4, :]
                    a.activation(to, pv[:, :], ACT.Copy).then_inc(y_hi_set.sem, 1)

                def read_projection(g):
                    wait(act, proj_done, l, g + 1)
                    if g < HEADS:
                        if g:
                            wait(act, dss_done, l, g)
                        a.activation(sumsq[:, :], bank[g % 2][:, :], ACT.Square).then_inc(dsq_set.sem, 1)
                    else:
                        a.activation(gate_a[:, g - HEADS, :], bank[g % 2][:, :], ACT.Copy).then_inc(ga_set.sem, 1)

                def dilated_rms(t):
                    wait(act, dss_done, l, t + 1)
                    if t:
                        wait(act, dqk_set, l, t)
                    a.activation(rstd[:, :], ss[:, :], ACT.Ln, scale=1.0 / DH, bias=eps_col[:, :])\
                        .then_inc(dln_set.sem, 1)
                    wait(act, dln_set, l, t + 1)
                    a.activation(rstd[:, :], rstd[:, :], ACT.Exp, scale=-0.5).then_inc(dr_set.sem, 1)

                for n in range(NT * STEPS + 2):
                    g, i = divmod(n, NT)
                    if n >= 2 and i != 2:
                        probT_copy(n - 2)
                    if g < STEPS:
                        softmax_exp(n)
                    if n == 0:
                        head_rms(HEADS - 1)
                    elif i == 0:
                        read_projection(g - 1)
                    if n == NT * STEPS:
                        panel_hi(l, PN_GB + 1)
                    if g < STEPS and i < 2 and next_split(g) is not None:
                        split_high(next_split(g), i)
                    if i == 1 and g % 2:
                        panel_hi(l, step_panel(g), (1,))
                    if i == 2:
                        if 1 <= g <= HEADS:
                            dilated_rms(g - 1)
                        probT_copy(n - 2)
                    if i == 3:
                        if g % 2 == 0:
                            panel_hi(l, step_panel(g), (0,))
                            if g:
                                y_high(g // 2 - 1)
                        if HEADS - 2 <= g < STEPS - 2:
                            load_toeplitz(g - HEADS + 2)
                y_high(STEPS // 2 - 1)
                a.preload_act_table_set("sigmoid_and_others")

                def branch(i, following):
                    for j in range(2):
                        wait(act, gb_done, l, 2 * i + j + 1)
                        a.activation(sig_b[:, j, :], bank[j][:, :], ACT.Sigmoid).then_inc(sigb_set.sem, 1)
                        a.activation(sig_a[:, j, :], gate_a[:, bass.ds(2 * i + j, 1), :], ACT.Sigmoid)\
                            .then_inc(siga_set.sem, 1)
                    following(0)
                    for j in range(2):
                        wait(act, mix_set, l, 2 * i + j + 1)
                        a.activation(m_hi[:, bass.ds(2 * i + j, 1), :], mix[:, j, :], ACT.Copy)\
                            .then_inc(m_hi_set.sem, 1)
                    following(1)

                def next_branch(i):
                    def following(j):
                        free = (gb_done, 2 * i + 2) if j == 0 else (br_done, 4 * i + 4)
                        for c in range(2):
                            hi_chunk(l, j, c, 2 * j + c, PN_GB // 2 + 2 + LATE + i, free if c == 0 else None)
                    return following

                def pair_at(p):
                    return lambda j: panel_hi(l, p + j)

                with act.Fori(0, 3) as i:
                    branch(i, next_branch(i))
                branch(3, pair_at(PN_OUT))
                a.preload_act_table_set("natural_log_exp_and_others")

                for n in range(KD):
                    square_x(l, n, n % 2, xT[:, n, :])
                    if n in (1, 3, 5):
                        panel_hi(l, PN_OUT + 2 + n // 2)

                norm(l, 1, M_SH2, lambda k: panel_hi(l, PN_FFN + 1, (k,)) if k < 2 else None)
                a.preload_act_table_set("sigmoid_and_others")

                def hidden(t, following):
                    for j in range(2):
                        wait(act, gate_done, l, 2 * t + j + 1)
                        wait(act, h_lo_set, l, 2 * KD)
                        a.activation(tn[:, j, :], bank[j][:, :], ACT.Sigmoid).then_inc(fsig_set.sem, 1)
                    following(0)
                    for j in range(2):
                        wait(act, act_set, l, 2 * t + j + 1)
                        a.activation(a_hi[:, bass.ds(2 * t + j, 1), :], sq[:, j, :], ACT.Copy).then_inc(a_hi_set.sem, 1)
                    following(1)

                def next_hidden(t):
                    def following(j):
                        for c in range(2):
                            hi_chunk(l, j, c, 2 * j + c, PN_FFN // 2 + 2 + LATE + t,
                                     ((gate_done, up_done)[j], 2 * t + 2) if c == 0 else None)
                    return following

                with act.Fori(0, KF // 2 - 1) as t:
                    hidden(t, next_hidden(t))
                hidden(KF // 2 - 1, pair_at(PN_DOWN))
                a.preload_act_table_set("natural_log_exp_and_others")

                for gr in range(4):
                    for q in range(3):
                        p = PN_DOWN + 2 + 3 * gr + q
                        if p < PANELS:
                            panel_hi(l, p)
                    for j in range(2):
                        square_x(l, KD + 2 * gr + j, j, xT[:, 2 * gr + j, :])

            for n in range(1, 2 * NT, 2):
                act.wait_ge(y_transposed, n + 1)
                a.activation(xout[:, n // 2, S:D], tr[:, 1, :], ACT.Copy).then_inc(xout_right, 1)

        @block.vector
        def _(dve):
            def lo_chunk(l, slot, c, raw_slot, made, kind="full"):
                wait(dve, hi_set, l, made)
                parts = list(zip(pieces(kind, raw_slot, c, w_hi[slot]), pieces(kind, raw_slot, c, w_lo[slot])))
                for (hi, frm), (lo, _) in parts:
                    last = v.tensor_tensor(lo, frm, hi.bitcast(F32), ALU.subtract)
                last.then_inc(lo_set.sem, 1)

            def panel_lo(l, p, chunks=(0, 1)):
                for c in chunks:
                    r = load_of("panel", p, c) if p < PN_GB + 2 else 2 * p + c + RAW * LATE
                    if (p, c) not in POOLED:
                        lo_chunk(l, p % 2, c, r % RAW, 2 * p + c + 1, KINDS.get(p, "full"))

            def norm(l, n, shift, gain_row):
                v.scalar_tensor_tensor(g_norm[:, :], mods[:, shift + KD:shift + 2 * KD], 1.0,
                                       prl[:, gain_row:gain_row + KD], ALU.add, ALU.mult).then_inc(g_norm_set.sem, 1)
                wait(dve, g_norm_set, l, n + 1)
                wait(dve, rstd_set, l, n + 1)

                def low(k):
                    wait(dve, h_hi_set, l, KD * n + k + 1)
                    v.scalar_tensor_tensor(h_lo[:, k, :], tn[:, k % 2, :], mods[:, shift + k:shift + k + 1],
                                           h_hi[:, k, :].bitcast(F32), ALU.add, ALU.subtract).then_inc(h_lo_set.sem, 1)

                for k in range(KD):
                    if k >= 2:
                        wait(dve, h_lo_set, l, KD * n + k - 1)
                    v.scalar_tensor_tensor(tn[:, k % 2, :], xT[:, k, :], g_norm[:, k:k + 1], rstd[:, :],
                                           ALU.mult, ALU.mult).then_inc(norm_t.sem, 1)
                    if k:
                        low(k - 1)
                low(KD - 1)

            v.memset(ones[:, :], 1.0).then_inc(ones_set, 1)
            v.memset(spare[:, :], 0.0).then_inc(ones_set, 1)
            v.memset(eps_col[:, :], EPS).then_inc(ones_set, 1)
            v.memset(trig[0:NOPE, :], 1.0).then_inc(trig_set, 1)
            dve.wait_ge(ones_set, 3)
            v.memset(spare[:, 0:1], 0.0).then_inc(lo_set.sem, lo_set.credit)
            v.memset(spare[:, 1:2], 0.0).then_inc(down_part.sem, down_part.credit)
            v.memset(spare[:, 2:3], 0.0).then_inc(down_done.sem, down_done.credit)
            dve.wait_ge(sig_c_set, 1)
            v.tensor_tensor(silu_c[:, :], rstd[:, 0:KD], pv[:, 0:KD], ALU.mult).then_inc(c_set, 1)
            def first_modulation(u):
                for k in range(KD):
                    if k % 4 == 0:
                        dve.wait_ge(ada0_in[2 * u + k // 4], 16)
                    if k == 0:
                        ins = v.tensor_scalar(ada0[:, u, 0, :], ada0[:, u, 0, :], silu_c[:, 0:1], None, ALU.mult)
                    else:
                        ins = v.scalar_tensor_tensor(ada0[:, u, 0, :], ada0[:, u, k, :], silu_c[:, k:k + 1],
                                                     ada0[:, u, 0, :], ALU.mult, ALU.add)
                    ins.then_inc(ada0_step, 1)
                    dve.wait_ge(ada0_step, KD * u + k + 1)

            dve.wait_ge(c_set, 1)
            first_modulation(0)
            dve.wait_ge(pos_in, 16)
            dve.wait_ge(consts_in, 16)
            step = 0

            def angle_done(ins):
                ins.then_inc(angle_step, 1)
                dve.wait_ge(angle_step, step)

            two_pi = 2 * math.pi
            c1 = 6.28125
            c2 = float(np.float32(math.floor((two_pi - c1) * 2 ** 22) / 2 ** 22))
            c3 = float(np.float32(two_pi - c1 - c2))
            whole = float(1.5 * 2 ** 23)
            step = 1
            angle_done(v.tensor_copy(angle[:, :], pos_i[:, :]))
            step = 2
            angle_done(v.tensor_scalar(angle[:, :], angle[:, :], rope_inv, None, ALU.mult))
            step = 3
            angle_done(v.tensor_scalar(turns[:, :], angle[:, :], 1.0 / two_pi, rope_phase, ALU.mult, ALU.add))
            step = 4
            angle_done(v.tensor_scalar(turns[:, :], turns[:, :], whole, whole, ALU.add, ALU.subtract))
            for part in (c1, c2, c3):
                step += 1
                angle_done(v.scalar_tensor_tensor(angle[:, :], turns[:, :], -part, angle[:, :], ALU.mult, ALU.add))
            step = 8
            angle_done(v.tensor_scalar(angle[:, :], angle[:, :], rope_arg, None, ALU.add))
            step = 9
            pi_below = float(np.nextafter(np.float32(math.pi), np.float32(0)))
            angle_done(v.tensor_scalar(angle[:, :], angle[:, :], pi_below, -pi_below, ALU.min, ALU.max))
            first_modulation(1)
            first_modulation(2)
            for l in range(DEPTH):
                dve.wait_ge(prm_done, l + 1)
                v.tensor_copy(prm[:, l, :], tr[:, l, 0:ROWS]).then_inc(prm_set, 1)
            first_modulation(3)
            dve.wait_ge(prm_set, DEPTH)
            dve.wait_ge(ada0_reduced, 1)
            v.tensor_tensor(mods[:, 0:M_G1], pv[:, 0:M_G1], prm[:, 0, R_ADAB:R_ADAB + M_G1], ALU.add)\
                .then_inc(mods0_set, 1)
            dve.wait_ge(mods0_set, 1)

            with dve.Fori(0, DEPTH) as l:
                v.tensor_copy(prl[:, :], prm[:, bass.ds(l, 1), :]).then_inc(prl_set.sem, 1)
                wait(dve, prl_set, l, 1)
                v.tensor_scalar(prl[:, R_QNB:R_QNB + 1], prl[:, R_QNB:R_QNB + 1], DH ** -0.5, None, ALU.mult)\
                    .then_inc(qnb_scaled.sem, 1)
                panel_lo(l, PN_QC)
                norm(l, 0, M_SH1, R_N1)
                dve.wait_ge(trig_set, 1)
                dve.wait_ge(sin_set, 2)
                v.tensor_scalar(q_gain[:, :], trig[:, :], prl[:, R_QNA:R_QNA + 1], QK ** -0.5, ALU.mult, ALU.mult)\
                    .then_inc(q_gain_set.sem, 1)
                panel_lo(l, PN_DV)

                wait(dve, lat_done, l, 2)
                wait(dve, lat_sq, l, 5)
                v.scalar_tensor_tensor(k_rot[64:128, :], s1[64:128, :], prl[64:128, R_KNA:R_KNA + 1], trig[64:128, :],
                                       ALU.mult, ALU.mult).then_inc(rot_parts.sem, 1)
                panel_lo(l, PN_DV + 1)
                wait(dve, rot_sum, l, 1)
                v.tensor_copy(k_rot[64:128, :], s1[64:128, :]).then_inc(rot_set.sem, 1)
                latents = ((b0, 0, R_QA, qc_hi[:, 0, :], qc_lo[:, 0, :]),
                           (b1, 0, R_QA + 1, qc_hi[:, 1, :], qc_lo[:, 1, :]),
                           (s0, 1, R_KVA, kvc_hi[:, :], kvc_lo[:, :]))
                for n, (src, r, gain, hi, lo) in enumerate(latents):
                    wait(dve, lat_r, l, r + 1)
                    v.scalar_tensor_tensor(prob[:, n % 2, :], src[:, :], prl[:, gain:gain + 1], r_qk[:, 0, r, :],
                                           ALU.mult, ALU.mult).then_inc(lat_t.sem, 1)
                    wait(dve, lat_hi, l, n + 1)
                    v.tensor_tensor(lo, prob[:, n % 2, :], hi.bitcast(F32), ALU.subtract).then_inc(lat_lo.sem, 1)
                    wait(dve, lat_lo, l, n + 1)
                panel_lo(l, PN_WQB)
                panel_lo(l, PN_WKVB)

                def head_scale(h):
                    i = h % 2
                    wait(dve, head_sq, l, 2 * h + 1)
                    v.tensor_tensor(qk[:, h, 0, :], bank[2 + i][:, :], q_gain[:, :], ALU.mult).then_inc(q_scaled.sem, 1)
                    wait(dve, head_sq, l, 2 * h + 2)
                    v.tensor_scalar(qk[0:NOPE, h, 1, :], bank[i][0:NOPE, :], prl[0:NOPE, R_KNA:R_KNA + 1], None,
                                    ALU.mult).then_inc(k_scaled.sem, 1)

                def head_q(h):
                    wait(dve, head_r, l, h + 1)
                    wait(dve, q_scaled, l, h + 1)
                    v.tensor_tensor(qk[:, h, 0, :], qk[:, h, 0, :], r_qk[:, h % 2, 0, :], ALU.mult)\
                        .then_inc(q_set.sem, 1)

                wait(dve, q_gain_set, l, 1)
                head_scale(0)
                for h in range(1, HEADS):
                    head_scale(h)
                    if h < HEADS - 1:
                        head_q(h - 1)
                panel_lo(l, PN_DQK)

                def ada_ops(g, part):
                    u, k0, k1 = ada_part(g)
                    bounds = [min(k1, k0 - (-3 * i * (k1 - k0) // KD)) for i in range(4)]
                    for k in range(bounds[part], bounds[part + 1]):
                        r = load_of("ada", u, k // 2)
                        src = raw[r % RAW][:, k % 2 * S:(k % 2 + 1) * S]
                        if k % 2 == 0:
                            wait_raw(dve, l, r)
                        if k == 0:
                            if u:
                                wait(dve, ada_reduced, l, u)
                            ins = v.tensor_scalar(ada_acc[:, :], src, silu_c[:, 0:1], None, ALU.mult)
                        else:
                            wait(dve, ada_step, l, KD * u + k)
                            ins = v.scalar_tensor_tensor(ada_acc[:, :], src, silu_c[:, k:k + 1], ada_acc[:, :],
                                                         ALU.mult, ALU.add)
                        ins.then_inc(ada_step.sem, 1)

                def ada_mods(u):
                    wait(dve, ada_reduced, l, u + 1)
                    col = M_G1 + 4 * u if u < HEADS else 4 * (u - HEADS)
                    bias = prl[:, R_ADAB + col:R_ADAB + col + 4] if u < HEADS else \
                        prm[:, DEPTH - 1, R_ADAB + col:R_ADAB + col + 4]
                    v.tensor_tensor(mods[:, col:col + 4], ss[:, 0:4], bias, ALU.add).then_inc(mods_set.sem, 1)

                def softmax_max(n):
                    g, i = divmod(n, NT)
                    wait(dve, scored, l, n + 1)
                    if g < HEADS:
                        v.tensor_reduce(nmax[:, i:i + 1], bank[2 + n % 2][:, :], AX.X, ALU.max, negate=True)\
                            .then_inc(max_set.sem, 1)
                        return
                    head = g - HEADS
                    if i == 0:
                        wait(dve, toep_in[head % 2], l, 16 * (head // 2 + 1))
                    wait(dve, transposed, l, n - 1)
                    v.tensor_tensor(prob[:, n % 2, :], bank[2 + n % 2][:, :],
                                    toep[:, head % 2, S - P - i * P:2 * S - P - i * P], ALU.add).then_inc(biased.sem, 1)
                    wait(dve, biased, l, NT * head + i + 1)
                    v.tensor_reduce(nmax[:, i:i + 1], prob[:, n % 2, :], AX.X, ALU.max, negate=True)\
                        .then_inc(max_set.sem, 1)

                def softmax_norm(n):
                    i = n % NT
                    wait(dve, exp_set, l, n + 1)
                    v.reciprocal(rden[:, i:i + 1], den[:, i:i + 1]).then_inc(rden_set.sem, 1)
                    wait(dve, rden_set, l, n + 1)
                    v.tensor_scalar(prob[:, n % 2, :], prob[:, n % 2, :], rden[:, i:i + 1], None, ALU.mult)\
                        .then_inc(prob_set.sem, 1)

                def y_low(pair):
                    wait(dve, y_hi_set, l, pair + 1)
                    hi, lo = (ya_hi[:, pair, :], ya_lo[:, pair, :]) if pair < 4 else \
                        (yb_hi[:, pair - 4, :], yb_lo[:, pair - 4, :])
                    v.tensor_tensor(lo, pv[:, :], hi.bitcast(F32), ALU.subtract).then_inc(y_lo_set.sem, 1)

                def dilated_scale(t):
                    gain = R_QNB if t < 4 else R_KNB
                    wait(dve, dr_set, l, t + 1)
                    if t == 0:
                        wait(dve, kr_set, l, HEADS)
                    v.scalar_tensor_tensor(dqk[:, t, :], bank[t % 2][:, :], prl[:, gain:gain + 1], rstd[:, :],
                                           ALU.mult, ALU.mult).then_inc(dqk_set.sem, 1)

                for n in range(NT * STEPS + 1):
                    g, i = divmod(n, NT)
                    if n:
                        softmax_norm(n - 1)
                    if g < STEPS:
                        softmax_max(n)
                    if n < 2:
                        head_q(HEADS - 2 + n)
                    if i == 0 and g >= 3 and g % 2:
                        y_low((g - 3) // 2)
                    if i == 1 and g and ada_part(g - 1)[2] == KD:
                        ada_mods(ada_part(g - 1)[0])
                    if i == 3 and 1 <= g <= HEADS:
                        dilated_scale(g - 1)
                    if i:
                        ada_ops(g, i - 1)
                panel_lo(l, PN_GB + 1)
                ada_mods(ADA_UNITS - 1)
                y_low(STEPS // 2 - 1)

                def branch(i, following):
                    following(0)
                    for j in range(2):
                        n = 2 * i + j
                        wait(dve, siga_set, l, n + 1)
                        wait(dve, br_done, l, 2 * n + 1)
                        v.tensor_tensor(sig_a[:, j, :], sig_a[:, j, :], bank[2][:, :] if j == 0 else tr[:, 0, :],
                                        ALU.mult).then_inc(mix_a.sem, 1)
                        wait(dve, br_done, l, 2 * n + 2)
                        v.tensor_tensor(sig_b[:, j, :], sig_b[:, j, :], bank[3][:, :] if j == 0 else tr[:, 1, :],
                                        ALU.mult).then_inc(mix_b.sem, 1)
                        wait(dve, mix_a, l, n + 1)
                        wait(dve, mix_b, l, n + 1)
                        v.tensor_tensor(mix[:, j, :], sig_a[:, j, :], sig_b[:, j, :], ALU.add).then_inc(mix_set.sem, 1)
                    for j in range(2):
                        n = 2 * i + j
                        wait(dve, m_hi_set, l, n + 1)
                        v.tensor_tensor(m_lo[:, bass.ds(n, 1), :], mix[:, j, :], m_hi[:, bass.ds(n, 1), :].bitcast(F32),
                                        ALU.subtract).then_inc(m_lo_set.sem, 1)
                    following(1)

                def pair_at(p):
                    def following(j):
                        for c in range(2):
                            lo_chunk(l, j, c, 2 * j + c, 2 * (p + j) + c + 1)
                    return following

                with dve.Fori(0, 3) as i:
                    branch(i, pair_at(PN_GB + 2 + 2 * i))
                branch(3, pair_at(PN_OUT))

                def update_x(l, n, k, gate, product):
                    v.scalar_tensor_tensor(xT[:, k, :], product[:, :], mods[:, gate + k:gate + k + 1], xT[:, k, :],
                                           ALU.mult, ALU.add).then_inc(x_updated.sem, 1)

                wait(dve, mods_set, l, ADA_UNITS)
                for k in range(KD):
                    wait(dve, out_done, l, k + 1)
                    update_x(l, k, k, M_G1, bank[k % 4])
                    if k in (1, 3, 5):
                        panel_lo(l, PN_OUT + 2 + k // 2)
                norm(l, 1, M_SH2, R_N2)
                panel_lo(l, PN_FFN + 1)

                def hidden(t, following):
                    for j in range(2):
                        n = 2 * t + j
                        wait(dve, fsig_set, l, n + 1)
                        v.tensor_tensor(tn[:, j, :], tn[:, j, :], bank[j][:, :], ALU.mult).then_inc(silu_set.sem, 1)
                    following(0)
                    for j in range(2):
                        n = 2 * t + j
                        wait(dve, up_done, l, n + 1)
                        wait(dve, silu_set, l, n + 1)
                        v.tensor_tensor(sq[:, j, :], tn[:, j, :], bank[2 + j][:, :], ALU.mult).then_inc(act_set.sem, 1)
                    for j in range(2):
                        n = 2 * t + j
                        wait(dve, a_hi_set, l, n + 1)
                        v.tensor_tensor(a_lo[:, bass.ds(n, 1), :], sq[:, j, :], a_hi[:, bass.ds(n, 1), :].bitcast(F32),
                                        ALU.subtract).then_inc(a_lo_set.sem, 1)
                    following(1)

                with dve.Fori(0, KF // 2 - 1) as t:
                    hidden(t, pair_at(PN_FFN + 2 + 2 * t))
                hidden(KF // 2 - 1, pair_at(PN_DOWN))

                for gr in range(4):
                    for q in range(3):
                        p = PN_DOWN + 2 + 3 * gr + q
                        if p < PANELS:
                            panel_lo(l, p)
                    for j in range(2):
                        k = 2 * gr + j
                        wait(dve, down_done, l, k + 1)
                        update_x(l, KD + k, k, M_G2, bank[k % 4])

            for n in range(0, 2 * NT, 2):
                dve.wait_ge(y_transposed, n + 1)
                v.tensor_copy(xout[:, n // 2, 0:S], tr[:, 0, :]).then_inc(xout_left, 1)

        @block.gpsimd
        def _(pool):
            pool.dma_start(bucket_sb[:, :], buckets).then_inc(buckets_in, 16)
            pool.dma_start(rel_sb[0:REL_BUCKETS, :], rel_bias).then_inc(buckets_in, 16)
            pool.dma_start(pos_i[:, :], positions.partition_broadcast(P)).then_inc(pos_in, 16)
            pool.memset(rel_sb[REL_BUCKETS:REL_BUCKETS + 1, :], 1.0).then_inc(rel_ones, 1)

            def add_square(k):
                first = sq[:, 0, :] if k == 1 else sumsq[:, :]
                nc.gpsimd.tensor_tensor(sumsq[:, :], first, sq[:, k % 2, :], ALU.add).then_inc(sum_done.sem, 1)

            def pool_lo(l, p, c):
                raw_slot, kind = load_of("panel", p, c) % RAW, KINDS.get(p, "full")
                wait(pool, hi_set, l, 2 * p + c + 1)
                parts = zip(pieces(kind, raw_slot, c, w_hi[p % 2]), pieces(kind, raw_slot, c, w_lo[p % 2]))
                for (hi, frm), (lo, _) in parts:
                    last = nc.gpsimd.tensor_tensor(lo, frm, hi.bitcast(F32), ALU.subtract)
                last.then_inc(pool_lo_set.sem, 1)

            pool.wait_ge(rel_ones, 1)
            for k in range(1, KD - 1):
                pool.wait_ge(sq_set.sem, k + 1)
                if k >= 2:
                    pool.wait_ge(sum_done.sem, k - 1)
                add_square(k)
            pool.wait_ge(btab_set, 2)
            pool.dma_start(bias_row, btab[:, :]).then_inc(bias_row_out, 16)
            pool.wait_ge(bias_row_out, 16)
            pool.wait_ge(raw_in[3].sem, 16)
            pool.dma_start(bias_scratch, bias_row.rearrange("h (o n) -> h o n", o=1).broadcast_to([HEADS, P, 2 * S]))\
                .then_inc(bias_out, 16)

            with pool.Fori(0, DEPTH) as l:
                for p, c in POOLED[:3]:
                    pool_lo(l, p, c)

                def split_low(m):
                    for j in range(2):
                        wait(pool, split_hi, l, 2 * m + j + 1)
                        whole, high, low = score_parts(m, j)
                        nc.gpsimd.tensor_tensor(low, whole, high.bitcast(F32), ALU.subtract).then_inc(split_lo.sem, 1)

                wait(pool, rot_set, l, 1)
                for h in range(HEADS):
                    i = h % 2
                    wait(pool, head_r, l, h + 1)
                    nc.gpsimd.tensor_tensor(qk[64:128, h, 1, :], k_rot[64:128, :], r_qk[64:128, i, 1, :], ALU.mult)\
                        .then_inc(k_set.sem, 1)
                    wait(pool, k_scaled, l, h + 1)
                    nc.gpsimd.tensor_tensor(qk[0:NOPE, h, 1, :], qk[0:NOPE, h, 1, :], r_qk[0:NOPE, i, 1, :], ALU.mult)\
                        .then_inc(kr_set.sem, 1)
                    if h in (3, HEADS - 1):
                        wait(pool, k_set, l, h + 1)
                        wait(pool, kr_set, l, h + 1)
                    if h == 3:
                        split_low(0)
                        wait(pool, split_lo, l, 2)
                for g in range(STEPS):
                    if next_split(g) is not None:
                        split_low(next_split(g))
                    pool_lo(l, step_panel(g), g % 2)
                for n in range(2):
                    wait(pool, norm_ss, l, n + 1)
                    if n == 0:
                        wait(pool, dss_done, l, HEADS)
                    for k in range(1, KD - 1):
                        wait(pool, sq_set, l, KD * n + k + 1)
                        if k >= 2:
                            wait(pool, sum_done, l, ADDS * n + k - 1)
                        add_square(k)

        @block.tensor
        def _(pe):
            def product(out_, w, w_cols, rhs_hi, rhs_lo, start, stop):
                whi, wlo = w_hi[w][:, w_cols], w_lo[w][:, w_cols]
                pe_.matmul(out_, whi, rhs_hi, start=start, stop=False)
                pe_.matmul(out_, wlo, rhs_hi, start=False, stop=False)
                return pe_.matmul(out_, whi, rhs_lo, start=False, stop=stop)

            def cols(k, at, wid=PC, n=P):
                return slice(k * wid + at, k * wid + at + n)

            def tile_product(out_, w, at, hi, lo, k0=0, k1=KD, kn=KD, wid=PC, base=0, w_k0=0):
                for k in range(k0, k1):
                    last = product(out_, w, slice(base + (k - w_k0) * wid + at, base + (k - w_k0) * wid + at + P),
                                   hi[:, k, :], lo[:, k, :], k == 0, k == kn - 1)
                return last

            def split_ready(l, p, c=1):
                ev, n = low_done(p, c)
                wait(pe, ev, l, n)

            def norm_sum(l, n):
                wait(pe, sum_done, l, ADDS * n)
                pe_.matmul(ss[:, :], ones[:, :], sumsq[:, :], start=True, stop=False)
                wait(pe, sq_set, l, KD * n)
                pe_.matmul(ss[:, :], ones[:, :], sq[:, 1, :], start=False, stop=True).then_inc(norm_ss.sem, 1)

            pe.wait_ge(consts_in, 16)
            pe.wait_ge(c_in, 16)
            pe_.transpose(pv[:, 0:KD], c_rows[:, :], ident[0:KD, 0:KD]).then_inc(c_transposed, 1)
            pe.wait_ge(x_in, 16 * NT)
            for k in range(KD):
                if k >= 2:
                    pe.wait_ge(x_set, k - 1)
                for i in range(NT):
                    last = pe_.transpose(bank[2 + k % 2][:, i * P:(i + 1) * P], xnat[:, i, k * P:(k + 1) * P], ident)
                last.then_inc(x_transposed, 1)
            pe.wait_ge(buckets_in, 32)
            pe.wait_ge(ones_set, 3)
            pe.wait_ge(rel_ones, 1)
            for i in range(2):
                pe_.matmul(bank[i][0:HEADS, :], rel_sb[:, :], bucket_sb[:, i * S:(i + 1) * S], start=True, stop=True)\
                    .then_inc(bias_done, 1)
            pe.wait_ge(rows_in, 16 * 15)
            for l in range(DEPTH):
                pe_.transpose(tr[:, l, 0:ROWS], rows[:, l, :], ident[0:ROWS, 0:ROWS]).then_inc(prm_done, 1)
            norm_sum(0, 0)
            for u in range(4):
                pe.wait_ge(ada0_step, KD * (u + 1))
                for j in range(4):
                    last = pe_.matmul(pv[:, 4 * u + j:4 * u + j + 1], ada0[:, u, 0, j * P:(j + 1) * P], ones[:, 0:1],
                                      start=True, stop=True)
            last.then_inc(ada0_reduced, 1)

            with pe.Fori(0, DEPTH) as l:
                for k in range(KD):
                    if k % 4 == 0:
                        split_ready(l, PN_QC, k // 4)
                    wait(pe, h_lo_set, l, k + 1)
                    for j in range(2):
                        last = product(bank[j][:, :], 0, cols(k, j * P), h_hi[:, k, :], h_lo[:, k, :],
                                       k == 0, k == KD - 1)
                last.then_inc(lat_done.sem, 1)
                split_ready(l, PN_KV)
                for j in range(2):
                    last = tile_product(bank[2 + j][:, :], 1, j * P, h_hi, h_lo)
                last.then_inc(lat_done.sem, 1)

                def dilated_v(n):
                    half, i = divmod(n, NT)
                    if i == 0:
                        split_ready(l, PN_DV + half)
                    if n >= 2:
                        wait(pe, v_set, l, n - 1)
                    tok = slice(i * P, (i + 1) * P)
                    for k in range(KD):
                        o, hh, hl = tr[:, i % 2, 0:PC], h_hi[:, k, tok], h_lo[:, k, tok]
                        whi, wlo = w_hi[half][:, k * PC:(k + 1) * PC], w_lo[half][:, k * PC:(k + 1) * PC]
                        pe_.matmul(o, hh, whi, start=k == 0, stop=False)
                        pe_.matmul(o, hh, wlo, start=False, stop=False)
                        last = pe_.matmul(o, hl, whi, start=False, stop=k == KD - 1)
                    last.then_inc(vd_done.sem, 1)

                dilated_v(0)
                dilated_v(1)
                wait(pe, lat_sq, l, 5)
                pe.wait_ge(mods0_set, 1)
                pe_.matmul(ss[:, :], ones[:, :], probT[:, 0, :], start=True, stop=False)
                pe_.matmul(ss[:, :], ones[:, :], probT[:, 1, :], start=False, stop=True).then_inc(lat_ss.sem, 1)
                pe_.matmul(pv[:, :], ones[:, :], probT[:, 2, :], start=True, stop=True).then_inc(lat_ss.sem, 1)
                wait(pe, rot_parts, l, 1)
                pe_.matmul(s1[:, :], pair_sum, k_rot[64:128, :], start=True, stop=True).then_inc(rot_sum.sem, 1)
                for n in range(2, 2 * NT):
                    dilated_v(n)

                def head_q(h):
                    if h >= 2:
                        wait(pe, q_scaled, l, h - 1)
                    tile_product(bank[2 + h % 2][:, :], 0, h * P, qc_hi, qc_lo, 0, 2, 2, HEADS * P)\
                        .then_inc(q_done.sem, 1)

                def head_k(h):
                    if h >= 2:
                        wait(pe, k_scaled, l, h - 1)
                    product(bank[h % 2][:, :], 1, slice(h * P, (h + 1) * P), kvc_hi[:, :], kvc_lo[:, :], True, True)\
                        .then_inc(k_done.sem, 1)

                def head_sums(h):
                    i = h % 2
                    wait(pe, head_sq, l, 2 * h + 2)
                    if h >= 2:
                        wait(pe, head_ln, l, h - 1)
                    sums = (tr, acc)[i]
                    pe_.matmul(sums[:, 0, :], ones[0:QK, :], sq_qk[0:QK, i, 0, :], start=True, stop=True)
                    pe_.matmul(sums[:, 1, :], ones[0:QK, :], sq_qk[0:QK, i, 1, :], start=True, stop=True)\
                        .then_inc(head_ss.sem, 1)

                def heads_of(w):
                    return w[:, 0:HEADS * P].rearrange("p (h n) -> p h n", h=HEADS)[:, :, NOPE:P]

                split_ready(l, PN_WQB)
                wait(pe, lat_lo, l, 3)
                wait(pe, rot_set, l, 1)
                head_q(0)
                head_q(1)
                split_ready(l, PN_WKVB)
                for i, bank_ in enumerate((ss, pv, ss, pv)):
                    if i >= 2:
                        wait(pe, v_set, l, 2 * NT + i - 1)
                    tok = slice(i * P, (i + 1) * P)
                    v_out = bank_[:, :].rearrange("p (h n) -> p h n", h=HEADS)
                    pe_.matmul(v_out, kvc_hi[:, tok], heads_of(w_hi[1]), start=True, stop=False)
                    pe_.matmul(v_out, kvc_hi[:, tok], heads_of(w_lo[1]), start=False, stop=False)
                    pe_.matmul(v_out, kvc_lo[:, tok], heads_of(w_hi[1]), start=False, stop=True)\
                        .then_inc(vm_done.sem, 1)
                head_k(0)
                head_k(1)
                head_sums(0)
                for h in range(2, HEADS):
                    head_q(h)
                    head_k(h)
                    head_sums(h - 1)
                head_sums(HEADS - 1)

                def gate_b(i, j):
                    if j == 0:
                        split_ready(l, PN_GB + 2 * i)
                    if isinstance(i, int):
                        wait(pe, ga_set, l, HEADS - 1 + j)
                    elif j == 0:
                        wait(pe, sigb_set, l, 2 * i)
                    tile_product(bank[j][:, :], 0, j * P, h_hi, h_lo).then_inc(gb_done.sem, 1)

                def scores(n):
                    g, i = divmod(n, NT)
                    if n < 2:
                        wait(pe, q_scaled, l, HEADS - 1 + n)
                    m = g if g < HEADS else HEADS + (g - HEADS) // 2
                    half = slice(0, P) if g < HEADS else slice(DH * (g % 2), DH * (g % 2) + DH)
                    if i == 0:
                        wait(pe, split_lo, l, 2 * m + 2)
                    (_, q_hi, q_lo), (_, k_hi, k_lo) = score_parts(m, 0), score_parts(m, 1)
                    queries = slice(i * P, (i + 1) * P)
                    if n >= 2:
                        if n - 2 < NT * HEADS:
                            wait(pe, exp_set, l, n - 1)
                        else:
                            wait(pe, biased, l, n - 1 - NT * HEADS)
                    out_ = bank[2 + n % 2][:, :]
                    pe_.matmul(out_, q_hi[half, queries], k_hi[half, :], start=True, stop=False)
                    pe_.matmul(out_, q_lo[half, queries], k_hi[half, :], start=False, stop=False)
                    pe_.matmul(out_, q_hi[half, queries], k_lo[half, :], start=False, stop=True).then_inc(scored.sem, 1)

                def transposes(n):
                    wait(pe, prob_set, l, n + 1)
                    if n >= 2:
                        wait(pe, probT_set, l, n - 1)
                    for j in range(NT):
                        last = pe_.transpose(tr[:, n % 2, j * P:(j + 1) * P], prob[:, n % 2, j * P:(j + 1) * P], ident)
                    last.then_inc(transposed.sem, 1)

                def attend(g):
                    wait(pe, probT_set, l, NT * g + NT)
                    head = g % HEADS
                    vals = v_mla if g < HEADS else v_dil
                    if g >= 2 and g % 2 == 0:
                        wait(pe, y_lo_set, l, g // 2)
                    half = slice(DH * (head % 2), DH * (head % 2) + DH)
                    for j in range(NT):
                        last = pe_.matmul(pv[half, :], vals[:, j, head * DH:(head + 1) * DH], probT[:, j, :],
                                          start=j == 0, stop=j == NT - 1)
                    last.then_inc(pv_done.sem, 1)

                def projection(g, k0, k1):
                    p = PN_DQK + g // 2
                    if k0 == 0:
                        split_ready(l, p)
                        if g < 2:
                            wait(pe, k_scaled, l, HEADS - 1 + g)
                        else:
                            if g - 2 < HEADS:
                                wait(pe, dqk_set, l, g - 1)
                            else:
                                wait(pe, ga_set, l, g - 1 - HEADS)
                    last = tile_product(bank[g % 2][:, :], p % 2, g % 2 * P, h_hi, h_lo, k0, k1)
                    if k1 == KD:
                        last.then_inc(proj_done.sem, 1)

                def dilated_sums(t):
                    wait(pe, dsq_set, l, t + 1)
                    wait(pe, mods_set, l, t + 1)
                    pe_.matmul(ss[:, :], block_ones, sumsq[:, :], start=True, stop=True).then_inc(dss_done.sem, 1)

                def ada_reduce(g):
                    u, _, k1 = ada_part(g)
                    if k1 != KD:
                        return
                    wait(pe, ada_step, l, KD * (u + 1))
                    if g == 0:
                        wait(pe, head_ln, l, HEADS)
                    elif g <= HEADS:
                        wait(pe, dln_set, l, g)
                    if u:
                        wait(pe, mods_set, l, u)
                    for j in range(4):
                        last = pe_.matmul(ss[:, j:j + 1], ada_acc[:, j * P:(j + 1) * P], ones[:, 0:1],
                                          start=True, stop=True)
                    last.then_inc(ada_reduced.sem, 1)

                parts = {0: (0, 2), 1: (2, 4), 2: (4, 6), 3: (6, KD)}
                for n in range(NT * STEPS + 2):
                    g, i = divmod(n, NT)
                    if g < STEPS:
                        scores(n)
                    if n >= 2:
                        transposes(n - 2)
                    if g < STEPS:
                        projection(g, *parts[i])
                    if i == 0 and g:
                        ada_reduce(g - 1)
                    if i == 1 and 1 <= g <= HEADS:
                        dilated_sums(g - 1)
                    if i == 2 and g:
                        attend(g - 1)
                    if g == STEPS:
                        gate_b(0, i)
                attend(STEPS - 1)

                def branch(i):
                    split_ready(l, PN_GB + 1 + 2 * i)
                    if isinstance(i, int):
                        wait(pe, y_lo_set, l, STEPS // 2)
                    else:
                        wait(pe, mix_b, l, 2 * i)
                    for j in range(2):
                        acc_a, acc_b = (bank[2][:, :], bank[3][:, :]) if j == 0 else (tr[:, 0, :], tr[:, 1, :])
                        tile_product(acc_a, 1, j * P, ya_hi, ya_lo, 0, 4, 4).then_inc(br_done.sem, 1)
                        last = tile_product(acc_b, 1, j * P, yb_hi, yb_lo, 0, 4, 4, base=PANEL // 2)
                        last.then_inc(br_done.sem, 1)

                branch(0)
                with pe.Fori(1, 4) as i:
                    gate_b(i, 0)
                    gate_b(i, 1)
                    branch(i)

                for n in range(KD):
                    p = PN_OUT + n // 2
                    split_ready(l, p)
                    if n >= 4:
                        wait(pe, x_updated, l, n - 3)
                    if n == 0:
                        wait(pe, m_lo_set, l, KD - 2)
                        tile_product(bank[0][:, :], p % 2, 0, m_hi, m_lo, 0, KD - 2)
                        wait(pe, m_lo_set, l, KD)
                    last = tile_product(bank[n % 4][:, :], p % 2, n % 2 * P, m_hi, m_lo, 0 if n else KD - 2)
                    last.then_inc(out_done.sem, 1)
                norm_sum(l, 1)

                def hidden(t):
                    split_ready(l, PN_FFN + 2 * t)
                    wait(pe, silu_set, l, 2 * t)
                    for j in range(2):
                        last = tile_product(bank[j][:, :], 0, j * P, h_hi, h_lo)
                        last.then_inc(gate_done.sem, 1)
                    split_ready(l, PN_FFN + 1 + 2 * t)
                    wait(pe, act_set, l, 2 * t)
                    for j in range(2):
                        last = tile_product(bank[2 + j][:, :], 1, j * P, h_hi, h_lo)
                        last.then_inc(up_done.sem, 1)

                split_ready(l, PN_FFN)
                for k in range(KD):
                    wait(pe, h_lo_set, l, KD + k + 1)
                    for j in range(2):
                        last = product(bank[j][:, :], 0, cols(k, j * P), h_hi[:, k, :], h_lo[:, k, :],
                                       k == 0, k == KD - 1)
                        if k == KD - 1:
                            last.then_inc(gate_done.sem, 1)
                split_ready(l, PN_FFN + 1)
                for j in range(2):
                    tile_product(bank[2 + j][:, :], 1, j * P, h_hi, h_lo).then_inc(up_done.sem, 1)
                with pe.Fori(1, KF // 2) as t:
                    hidden(t)

                for gr in range(4):
                    for q in range(3):
                        p = PN_DOWN + 3 * gr + q
                        split_ready(l, p)
                        if q == 0:
                            wait(pe, a_lo_set, l, KF)
                            if gr >= 2:
                                wait(pe, x_updated, l, KD + 2 * gr - 2)
                        k0, k1 = 8 * q, min(8 * q + 8, KF)
                        for j in range(2):
                            last = tile_product(bank[(2 * gr + j) % 4][:, :], p % 2, j * P, a_hi, a_lo,
                                                k0, k1, KF, w_k0=k0)
                            if q == 2:
                                last.then_inc(down_done.sem, 1)
                        if q < 2:
                            last.then_inc(down_part.sem, 1)
                norm_sum(l, 2)

            for n in range(2 * NT):
                i, half = n // 2, n % 2
                if n < 2:
                    pe.wait_ge(x_updated.sem, 2 * KD * DEPTH - (4, 0)[n])
                if n >= 2:
                    pe.wait_ge(xout_right if half else xout_left, i)
                for k in range(4):
                    last = pe_.transpose(tr[:, half, k * P:(k + 1) * P], xT[:, 4 * half + k, i * P:(i + 1) * P], ident)
                last.then_inc(y_transposed, 1)


_INS = ["x", "c", "positions", "rel_bias", "norm1_g", "norm2_g", "ada_w", "ada_b", "w_in", "q_a_norm", "w_q_b",
        "kv_a_norm", "w_kv_b", "q_norm_a", "k_norm_a", "q_norm_b", "k_norm_b", "w_branch_a", "w_branch_b",
        "w_out", "w_ffn_gate", "w_ffn_up", "w_ffn_down"]


def shape_constants():
    cst = np.zeros((P, 3 * P + 4), np.float32)
    cst[:, 0:P] = np.eye(P)
    cst[:, P:2 * P] = np.kron(np.eye(2), np.ones((DH, DH)))
    cst[64:128, 2 * P:3 * P] = np.kron(np.ones((2, 4)), np.eye(ROPE))
    inv = (ROPE_THETA ** (-np.arange(HALF) / HALF)).astype(np.float32)
    rope = cst[:, 3 * P:]
    rope[:, 3] = 1.0
    rope[64:96, 0] = rope[96:128, 0] = np.tile(inv, 2)
    rope[64:96, 1] = 0.25
    rope[64:96, 2] = math.pi / 2
    rope[96:96 + HALF, 3] = -1.0

    rel = np.arange(-(S - 1), S + 1)
    n = np.abs(rel)
    half = REL_BUCKETS // 2
    exact = half // 2
    large = exact + (np.log(np.maximum(n, 1).astype(np.float32) / np.float32(exact))
                     / np.float32(math.log(REL_MAX_DIST / exact)) * (half - exact)).astype(np.int32)
    bucket = np.where(rel > 0, half, 0) + np.where(n < exact, n, np.minimum(large, half - 1))
    count = sum(((n % dil == 0) & (n <= window // 2)).astype(np.int64) for window, dil in PATTERNS)
    table = np.zeros((REL_BUCKETS + 1, 2 * S), np.float32)
    table[bucket, np.arange(2 * S)] = 1.0
    table[REL_BUCKETS] = np.where(count > 0, np.log(np.maximum(count, 1)), NEG_INF)
    return cst, table


def kernel(**inputs):
    import concourse.bacc as bacc
    from concourse.bass_utils import run_bass_kernel_spmd

    nc = bacc.Bacc("TRN2", target_bir_lowering=False, num_devices=1)
    arrays = {name: np.ascontiguousarray(inputs[name]) for name in _INS}
    arrays["consts"], arrays["buckets"] = shape_constants()
    args = [nc.dram_tensor(f"in_{n}", a.shape, mybir.dt.from_np(a.dtype), kind="ExternalInput").ap()
            for n, a in arrays.items()]
    out = nc.dram_tensor("out", (1, S, D), F32, kind="ExternalOutput").ap()
    encoder_trunk(nc, *args, out)
    result = run_bass_kernel_spmd(nc, [{f"in_{n}": a for n, a in arrays.items()}], core_ids=[0])
    return result.results[0]["out"]
```
